# Optimizing a Trainium2 kernel written in Bass

```python
import functools
import jax, jax.numpy as jnp
from jax import lax
import numpy as np

D_MODEL = 1024
BATCH = 1
SEQ = 256
DEPTH = 1
DEC_BATCH = 8
DEC_SEQ = 8
PAST_LEN = 1024
PAGE_SIZE = 128

HEAD_DIM = 64
CONV_WIDTH = D_MODEL // 4
CONV_GROUPS = CONV_WIDTH // HEAD_DIM
FOX_HEADS = (3 * D_MODEL // 8) // HEAD_DIM
MOBA_HEADS = (3 * D_MODEL // 8) // HEAD_DIM
FOX_WIDTH = FOX_HEADS * HEAD_DIM
MOBA_WIDTH = MOBA_HEADS * HEAD_DIM
MIX_WIDTH = CONV_WIDTH + FOX_WIDTH + MOBA_WIDTH
SHORT_CONV_W = 3
FFN_CONV_W = 3
D_FF = 2816
MOBA_BLOCK = 256
MOBA_TOPK = 3
Q_BLOCK = 128
LN_EPS = 1e-5
DN_ALPHA = (2 * DEPTH) ** 0.25
DN_BETA = (8 * DEPTH) ** -0.25
ATTN_SCALE = HEAD_DIM ** -0.5
IN_SIZES = (CONV_WIDTH, CONV_WIDTH, CONV_WIDTH,
            FOX_WIDTH, FOX_WIDTH, FOX_WIDTH, FOX_HEADS,
            MOBA_WIDTH, MOBA_WIDTH, MOBA_WIDTH)
N_IN = sum(IN_SIZES)

kernel_name = "hymba_conv_fox_moba_decoder_step"

def layer_norm(x, g, b):
    xf = x.astype(jnp.float32)
    mu = jnp.mean(xf, axis=-1, keepdims=True)
    var = jnp.mean(jnp.square(xf - mu), axis=-1, keepdims=True)
    y = (xf - mu) * lax.rsqrt(var + LN_EPS) * g.astype(jnp.float32) + b.astype(jnp.float32)
    return y.astype(x.dtype)

def causal_dwconv(u, prev, w):
    width = w.shape[0]
    t = u.shape[1]
    ext = jnp.concatenate([prev.astype(u.dtype), u], axis=1)
    out = ext[:, 0:t] * w[0]
    for j in range(1, width):
        out = out + ext[:, j:j + t] * w[j]
    return out, ext[:, t:]

def split_cols(p):
    parts, off = [], 0
    for n in IN_SIZES:
        parts.append(p[..., off:off + n])
        off += n
    return parts

def gather_pages(pool, page_table):
    g = pool[page_table]
    return g.reshape((g.shape[0], g.shape[1] * g.shape[2]) + g.shape[3:])

def alibi_slopes(n_heads):
    return jnp.asarray(2.0 ** (-8.0 * np.arange(1, n_heads + 1) / n_heads), jnp.float32)

def fox_logits(q, k, fq, fk, tq, sk):
    s = jnp.einsum("bqhd,bshd->bhqs", q, k).astype(jnp.float32) * ATTN_SCALE
    s = s + jnp.transpose(fq, (0, 2, 1))[:, :, :, None] - jnp.transpose(fk, (0, 2, 1))[:, :, None, :]
    return jnp.where(sk[None, :] <= tq[:, None], s, -jnp.inf)

def fox_prompt(q, k, v, logf):
    g, t, h, d = q.shape
    cum = jnp.cumsum(logf.astype(jnp.float32), axis=1)
    pos = jnp.arange(t)

    def one_block(i):
        st = i * Q_BLOCK
        qb = lax.dynamic_slice_in_dim(q, st, Q_BLOCK, axis=1)
        fb = lax.dynamic_slice_in_dim(cum, st, Q_BLOCK, axis=1)
        s = fox_logits(qb, k, fb, cum, st + jnp.arange(Q_BLOCK), pos)
        p = jax.nn.softmax(s, axis=-1)
        return jnp.einsum("bhqs,bshd->bqhd", p.astype(v.dtype), v)

    out = lax.map(one_block, jnp.arange(t // Q_BLOCK))
    return jnp.transpose(out, (1, 0, 2, 3, 4)).reshape(g, t, h * d)

def fox_sample(q, k, v, logf, k_past, v_past, logf_past):
    g, t, h, d = q.shape
    p_len = k_past.shape[1]
    cum_p = jnp.cumsum(logf_past.astype(jnp.float32), axis=1)
    cum_n = cum_p[:, -1:] + jnp.cumsum(logf.astype(jnp.float32), axis=1)
    tq = p_len + jnp.arange(t)
    s_past = fox_logits(q, k_past.astype(q.dtype), cum_n, cum_p, tq, jnp.arange(p_len))
    s_new = fox_logits(q, k, cum_n, cum_n, tq, tq)
    p = jax.nn.softmax(jnp.concatenate([s_past, s_new], axis=-1), axis=-1).astype(v.dtype)
    out = (jnp.einsum("bhqs,bshd->bqhd", p[..., :p_len], v_past.astype(v.dtype))
           + jnp.einsum("bhqs,bshd->bqhd", p[..., p_len:], v))
    return out.reshape(g, t, h * d)

def moba_attend_seq(q, tq, k_seq, v_seq):
    l, h, d = k_seq.shape
    nb = l // MOBA_BLOCK
    kb = k_seq.reshape(nb, MOBA_BLOCK, h, d).transpose(2, 0, 1, 3)
    vb = v_seq.reshape(nb, MOBA_BLOCK, h, d).transpose(2, 0, 1, 3)
    means = jnp.mean(kb.astype(jnp.float32), axis=2)
    own = tq // MOBA_BLOCK
    gate = jnp.einsum("qhd,hnd->qhn", q.astype(jnp.float32), means)
    gate = jnp.where(jnp.arange(nb)[None, None, :] < own[:, None, None], gate, -jnp.inf)
    n_sel = min(MOBA_TOPK, nb)
    _, top = lax.top_k(gate, n_sel)
    tq_n = tq.shape[0]
    own_b = jnp.broadcast_to(own[:, None, None], (tq_n, h, 1)).astype(top.dtype)
    blocks = jnp.concatenate([top, own_b], axis=-1)
    sel_ok = jnp.arange(n_sel)[None, None, :] < own[:, None, None]
    ok = jnp.concatenate([jnp.broadcast_to(sel_ok, (tq_n, h, n_sel)),
                          jnp.ones((tq_n, h, 1), dtype=bool)], axis=-1)
    hidx = jnp.arange(h)[None, :, None]
    kg = kb[hidx, blocks]
    vg = vb[hidx, blocks]
    s = jnp.einsum("qhd,qhnkd->qhnk", q, kg).astype(jnp.float32) * ATTN_SCALE
    dist = tq[:, None, None, None] - (blocks[..., None] * MOBA_BLOCK + jnp.arange(MOBA_BLOCK))
    s = s - alibi_slopes(h)[None, :, None, None] * dist.astype(jnp.float32)
    s = jnp.where(ok[..., None] & (dist >= 0), s, -jnp.inf)
    p = jax.nn.softmax(s.reshape(tq_n, h, -1), axis=-1).reshape(s.shape)
    out = jnp.einsum("qhnk,qhnkd->qhd", p.astype(v_seq.dtype), vg)
    return out.reshape(tq_n, h * d)

def moba_prompt(q, k, v):
    g, t, h, d = q.shape
    lp = -(-t // MOBA_BLOCK) * MOBA_BLOCK
    pad = ((0, 0), (0, lp - t), (0, 0), (0, 0))
    kp, vp = jnp.pad(k, pad), jnp.pad(v, pad)
    nqb = t // Q_BLOCK
    qb = q.reshape(g * nqb, Q_BLOCK, h, d)
    seq_id = jnp.repeat(jnp.arange(g), nqb)
    start = jnp.tile(jnp.arange(nqb) * Q_BLOCK, g)

    def one_block(args):
        qi, si, st = args
        return moba_attend_seq(qi, st + jnp.arange(Q_BLOCK), kp[si], vp[si])

    out = lax.map(one_block, (qb, seq_id, start))
    return out.reshape(g, t, h * d)

def moba_sample(q, k, v, k_past, v_past):
    g, t, h, d = q.shape
    p_len = k_past.shape[1]
    total = p_len + t
    lp = -(-total // MOBA_BLOCK) * MOBA_BLOCK
    pad = ((0, 0), (0, lp - total), (0, 0), (0, 0))
    k_all = jnp.pad(jnp.concatenate([k_past.astype(k.dtype), k], axis=1), pad)
    v_all = jnp.pad(jnp.concatenate([v_past.astype(v.dtype), v], axis=1), pad)
    tq = p_len + jnp.arange(t)
    return jax.vmap(lambda qi, ki, vi: moba_attend_seq(qi, tq, ki, vi))(q, k_all, v_all)

def trunk_layer(x, c, conv_prev, ffn_prev, fox_fn, moba_fn,
                w_ada, b_ada, w_in, b_f, conv_w, w_o, ln1_g, ln1_b,
                w_up, ffn_conv_w, ffn_conv_b, w_down, ln2_g, ln2_b):
    g, t, _ = x.shape
    ada = jax.nn.silu(c) @ w_ada + b_ada
    sh_a, sc_a, gt_a, sh_f, sc_f, gt_f = [a[:, None, :] for a in jnp.split(ada, 6, axis=-1)]
    h = x * (1 + sc_a) + sh_a
    cb, cc, cx, fq, fk, fv, ff, mq, mk, mv = split_cols(h @ w_in)
    conv_out, conv_state = causal_dwconv(cc * cx, conv_prev, conv_w)
    y_conv = cb * conv_out

    def heads(a):
        return a.reshape(g, t, -1, HEAD_DIM)

    logf = jax.nn.log_sigmoid((ff + b_f).astype(jnp.float32))
    y_fox = fox_fn(heads(fq), heads(fk), heads(fv), logf)
    y_moba = moba_fn(heads(mq), heads(mk), heads(mv))
    mixed = jnp.concatenate([y_conv, y_fox.astype(x.dtype), y_moba.astype(x.dtype)], axis=-1) @ w_o
    x = layer_norm(DN_ALPHA * x + (1 + gt_a) * mixed, ln1_g, ln1_b)
    h = x * (1 + sc_f) + sh_f
    up, ffn_state = causal_dwconv(h @ w_up, ffn_prev, ffn_conv_w)
    gate, val = jnp.split(up + ffn_conv_b, 2, axis=-1)
    y_ffn = (jax.nn.silu(gate) * val) @ w_down
    x = layer_norm(DN_ALPHA * x + (1 + gt_f) * y_ffn, ln2_g, ln2_b)
    new_state = (heads(fk), heads(fv), logf.astype(x.dtype), heads(mk), heads(mv), conv_state, ffn_state)
    return x, new_state

def setup_inputs(seed: int = 0) -> dict:
    key = jax.random.key(seed)
    ks = jax.random.split(key, 32)
    n_pages = PAST_LEN // PAGE_SIZE
    n_used = DEC_BATCH * n_pages
    n_pool = n_used + max(1, n_used // 4)

    def nrm(k, shape, s=1.0):
        return s * jax.random.normal(k, shape, jnp.float32)

    x_prompt = nrm(ks[0], (BATCH, SEQ, D_MODEL))
    x_sample = nrm(ks[1], (DEC_BATCH, DEC_SEQ, D_MODEL))
    cache_fox_k = nrm(ks[2], (DEPTH, n_pool, PAGE_SIZE, FOX_HEADS, HEAD_DIM))
    cache_fox_v = nrm(ks[3], (DEPTH, n_pool, PAGE_SIZE, FOX_HEADS, HEAD_DIM))
    cache_fox_logf = jax.nn.log_sigmoid(3.0 + nrm(ks[4], (DEPTH, n_pool, PAGE_SIZE, FOX_HEADS)))
    cache_moba_k = nrm(ks[5], (DEPTH, n_pool, PAGE_SIZE, MOBA_HEADS, HEAD_DIM))
    cache_moba_v = nrm(ks[6], (DEPTH, n_pool, PAGE_SIZE, MOBA_HEADS, HEAD_DIM))
    state_conv = nrm(ks[7], (DEPTH, DEC_BATCH, SHORT_CONV_W - 1, CONV_WIDTH))
    state_ffn = nrm(ks[8], (DEPTH, DEC_BATCH, FFN_CONV_W - 1, 2 * D_FF))
    page_table = jax.random.permutation(ks[9], n_pool)[:n_used].reshape(DEC_BATCH, n_pages).astype(jnp.int32)
    c_prompt = nrm(ks[10], (BATCH, D_MODEL))
    c_sample = nrm(ks[11], (DEC_BATCH, D_MODEL))
    w_ada = nrm(ks[12], (DEPTH, D_MODEL, 6 * D_MODEL), 0.2 * D_MODEL ** -0.5)
    b_ada = nrm(ks[13], (DEPTH, 6 * D_MODEL), 0.02)
    w_in = nrm(ks[14], (DEPTH, D_MODEL, N_IN), D_MODEL ** -0.5)
    b_f = 3.0 + nrm(ks[15], (DEPTH, FOX_HEADS), 0.5)
    conv_w = nrm(ks[16], (DEPTH, SHORT_CONV_W, CONV_WIDTH), SHORT_CONV_W ** -0.5)
    w_o = nrm(ks[17], (DEPTH, MIX_WIDTH, D_MODEL), DN_BETA * MIX_WIDTH ** -0.5)
    ln1_g = 1.0 + nrm(ks[18], (DEPTH, D_MODEL), 0.05)
    ln1_b = nrm(ks[19], (DEPTH, D_MODEL), 0.02)
    w_up = nrm(ks[20], (DEPTH, D_MODEL, 2 * D_FF), D_MODEL ** -0.5)
    ffn_conv_w = nrm(ks[21], (DEPTH, FFN_CONV_W, 2 * D_FF), FFN_CONV_W ** -0.5)
    ffn_conv_b = nrm(ks[22], (DEPTH, 2 * D_FF), 0.02)
    w_down = nrm(ks[23], (DEPTH, D_FF, D_MODEL), DN_BETA * D_FF ** -0.5)
    ln2_g = 1.0 + nrm(ks[24], (DEPTH, D_MODEL), 0.05)
    ln2_b = nrm(ks[25], (DEPTH, D_MODEL), 0.02)
    return {"x_prompt": x_prompt, "x_sample": x_sample,
            "cache_fox_k": cache_fox_k, "cache_fox_v": cache_fox_v, "cache_fox_logf": cache_fox_logf,
            "cache_moba_k": cache_moba_k, "cache_moba_v": cache_moba_v,
            "state_conv": state_conv, "state_ffn": state_ffn, "page_table": page_table,
            "c_prompt": c_prompt, "c_sample": c_sample,
            "w_ada": w_ada, "b_ada": b_ada, "w_in": w_in, "b_f": b_f, "conv_w": conv_w, "w_o": w_o,
            "ln1_g": ln1_g, "ln1_b": ln1_b, "w_up": w_up, "ffn_conv_w": ffn_conv_w,
            "ffn_conv_b": ffn_conv_b, "w_down": w_down, "ln2_g": ln2_g, "ln2_b": ln2_b}

def reference(x_prompt, x_sample, cache_fox_k, cache_fox_v, cache_fox_logf, cache_moba_k, cache_moba_v,
              state_conv, state_ffn, page_table, c_prompt, c_sample,
              w_ada, b_ada, w_in, b_f, conv_w, w_o, ln1_g, ln1_b,
              w_up, ffn_conv_w, ffn_conv_b, w_down, ln2_g, ln2_b):
    xp, xs = x_prompt, x_sample
    states_p, states_s = [], []
    for l in range(DEPTH):
        params = (w_ada[l], b_ada[l], w_in[l], b_f[l], conv_w[l], w_o[l], ln1_g[l], ln1_b[l],
                  w_up[l], ffn_conv_w[l], ffn_conv_b[l], w_down[l], ln2_g[l], ln2_b[l])
        zc = jnp.zeros((xp.shape[0], SHORT_CONV_W - 1, CONV_WIDTH), xp.dtype)
        zf = jnp.zeros((xp.shape[0], FFN_CONV_W - 1, 2 * D_FF), xp.dtype)
        xp, st_p = trunk_layer(xp, c_prompt, zc, zf, fox_prompt, moba_prompt, *params)
        states_p.append(st_p)
        fox_fn = functools.partial(fox_sample,
                                   k_past=gather_pages(cache_fox_k[l], page_table),
                                   v_past=gather_pages(cache_fox_v[l], page_table),
                                   logf_past=gather_pages(cache_fox_logf[l], page_table))
        moba_fn = functools.partial(moba_sample,
                                    k_past=gather_pages(cache_moba_k[l], page_table),
                                    v_past=gather_pages(cache_moba_v[l], page_table))
        xs, st_s = trunk_layer(xs, c_sample, state_conv[l], state_ffn[l], fox_fn, moba_fn, *params)
        states_s.append(st_s)
    fk_p, fv_p, flf_p, mk_p, mv_p, conv_p, ffn_p = [jnp.stack([s[i] for s in states_p]) for i in range(7)]
    fk_s, fv_s, flf_s, mk_s, mv_s, conv_s, ffn_s = [jnp.stack([s[i] for s in states_s]) for i in range(7)]
    return (xp, xs, fk_p, fv_p, flf_p, mk_p, mv_p, conv_p, ffn_p,
            fk_s, fv_s, flf_s, mk_s, mv_s, conv_s, ffn_s)


_drawn_inputs = setup_inputs


def setup_inputs(seed=0):
    import zlib

    import numpy as np

    out = dict(_drawn_inputs(seed))
    spreads = {}
    factors = {'cache_fox_logf': 5.074, 'ln1_b': 2.693, 'ffn_conv_b': 6.814, 'ln2_b': 2.812}
    for name, (base, spread) in spreads.items():
        noise = np.random.default_rng([zlib.crc32(name.encode()), seed]).standard_normal(out[name].shape)
        drawn = base * np.exp(spread * noise) if base else spread * noise
        out[name] = __import__('jax').numpy.asarray(drawn.astype(out[name].dtype))
    for name, factor in factors.items():
        out[name] = (out[name] * factor).astype(out[name].dtype)
    return out
```

```python
from contextlib import ExitStack

import numpy as np

import concourse.bass as bass
from concourse import mybir

F32 = mybir.dt.float32
F32R = mybir.dt.float32r
I32 = mybir.dt.int32
ALU = mybir.AluOpType
ACT = mybir.ActivationFunctionType
AX = mybir.AxisListType

P = 128
D = 1024
KD = D // P
TP, SEQS, TS = 256, 8, 8
TSA = SEQS * TS
TOK = TP + TSA
HEADS, HD = 6, 64
AW = HEADS * HD
PAIRS = HEADS // 2
CW = D // 4
PAST, PAGE = 1024, 128
PAGES = PAST // PAGE
POOL = 80
DFF = 2816
FT = DFF // P
MBLK, NBLK = 256, PAST // 256
NEG = -1.0e30
SCALE = HD ** -0.5
ALPHA = 2.0 ** 0.25
EPS = 1e-5
BP = SEQS // 2
ROWS = 112

CH = 256
N_ADA, N_IN, N_O, N_UP, N_DOWN = 6 * D // CH, 12, KD // 2, FT, FT // 2
CHB = KD * CH * 4
AT_IN = N_ADA
AT_O = AT_IN + N_IN
AT_UP = AT_O + N_O
AT_DOWN = AT_UP + N_UP

CB, CC, CX, FQ, FK, FV, MQ, MK, MV = 0, 2, 4, 6, 9, 12, 15, 18, 21
N_PROJ = 24
MIXED = [0, 1, 6, 7, 8, 15, 16, 17]

C_IDENT, C_TRI, C_ONES, C_DIAG = 0, 128, 256, 384
C_ALIBI = 512
C_SELB = C_ALIBI + 256
C_PAGEM = C_SELB + 128
C_FOXNEW = C_PAGEM + PAGES
C_MOBANEW = C_FOXNEW + BP * TSA
C_MOBAPAST = C_MOBANEW + BP * TSA
C_SELTOK = C_MOBAPAST + PAST
C_SCAN = C_SELTOK + 2 * P
C_RANK = C_SCAN + TOK
C_ROWB = C_RANK + NBLK
C_ALL = C_ROWB + 18


def slopes():
    return 2.0 ** (-8.0 * np.arange(1, HEADS + 1) / HEADS)


def constants():
    c = np.zeros((P, C_ALL), np.float64)
    i = np.arange(P)
    c[:, C_IDENT:C_IDENT + P] = np.eye(P)
    c[:, C_TRI:C_TRI + P] = i[:, None] > i[None, :]
    c[:, C_ONES:C_ONES + P] = 1
    c[:, C_DIAG:C_DIAG + P] = np.where(i[None, :] <= i[:, None], 0, NEG)
    c[:, C_ALIBI:C_ALIBI + P] = i[None, :] - i[:, None] - P
    c[:, C_ALIBI + P:C_ALIBI + 2 * P] = np.where(i[None, :] <= i[:, None], i[None, :] - i[:, None], NEG)
    par, x = i // 64, i % 64
    for r in range(P):
        if x[r] < PAGES * HEADS:
            page, h = x[r] // HEADS, x[r] % HEADS
            c[r, C_SELB + 64 * par[r] + TS * h:C_SELB + 64 * par[r] + TS * h + TS] = 1
            c[r, C_PAGEM + page] = 1 / SCALE
        if x[r] < HEADS * TS:
            h, q = x[r] // TS, x[r] % TS
            sl = slopes()[h] / SCALE
            c[r, C_MOBAPAST:C_MOBAPAST + PAST] = sl * (np.arange(PAST) - PAST - q)
            for bp in range(BP):
                at = C_FOXNEW + bp * TSA
                am = C_MOBANEW + bp * TSA
                for s in range(TSA):
                    ok = s // TS == 2 * bp + par[r] and s % TS <= q
                    c[r, at + s] = 0 if ok else NEG
                    c[r, am + s] = sl * (s % TS - q) if ok else NEG
    for r in range(18):
        b = r % 9
        if b == 0:
            c[r, C_SELTOK:C_SELTOK + P] = 1
        else:
            c[r, C_SELTOK + P + (b - 1) * TS:C_SELTOK + P + b * TS] = 1
    c[:, C_SCAN:C_SCAN + TOK] = 1
    c[:, C_SCAN] = 0
    c[:, C_SCAN + TP:C_SCAN + TOK:TS] = 0
    c[:, C_RANK:C_RANK + NBLK] = 1 + np.arange(NBLK)
    c[:, C_ROWB:C_ROWB + 9] = 1
    return c.astype(np.float32)


class Chain:

    def __init__(self, eng, sem):
        self.eng, self.sem, self.start, self.turn, self.per, self.k = eng, sem, 0, 0, 0, 0

    def link(self, instruction):
        self.k += 1
        instruction.then_inc(self.sem, 1)
        self.eng.wait_ge(self.sem, self.turn * self.per + (self.start + self.k))

    def enter(self, turn, per):
        self.turn, self.per, self.k = turn, per, 0

    def close(self, turns):
        assert self.k == self.per
        self.start, self.turn, self.per, self.k = self.start + turns * self.per, 0, 0, 0


class Chunk:

    def __init__(self, base, turn, k):
        self.j = turn * 4 + k
        self.n = turn * 4 + (base + k)
        self.raw, self.slot = (base + k) % 4, (base + k) % 2
        self.loads = turn + ((base + k) // 4 + 1)
        self.base, self.turn, self.k = base, turn, k

    def before(self):
        return Chunk(self.base, self.turn, self.k - 1) if self.k else Chunk(self.base, self.turn - 1, 3)


def ring(eng, base, count, step):
    turns = count // 4

    def turn(i):
        for k in range(4):
            step(Chunk(base, i, k))

    turn(0)
    if turns == 2:
        turn(1)
    elif turns > 2:
        with eng.Fori(1, turns) as i:
            turn(i)
    for k in range(count % 4):
        step(Chunk(base, turns, k))


def after(eng, semaphore, count):
    if not isinstance(count, int) or count > 0:
        eng.wait_ge(semaphore, count)


EVACS = "AAAAAAVVAVAV" + "VAV"
BEFORE = {"A": 8, "V": 4}
PER = {e: EVACS.count(e) for e in "AV"}


def evacs(stage, position, engine):
    return stage * PER[engine] + (BEFORE[engine] + EVACS[:position + 1].count(engine))


def build(nc, a, o):
    ctx = ExitStack()
    with ctx:
        sem = lambda n: ctx.enter_context(nc.semaphore(n))
        place = [1152]

        def region(size):
            at = place[0]
            place[0] += -(-size // 32) * 32
            return at

        def sb(name, shape, dt=F32, at=None):
            if at is None:
                at = region(int(np.prod(shape[1:])) * 4)
            return nc.alloc_sbuf_tensor_at(name, shape, dt, offset=at)

        const = sb("const", [P, C_ALL])
        xt = sb("x_tokens", [P, 3, D])
        st_t = sb("states_t", [P, 46, 32])
        conv_last = sb("conv_last", [P, 2, 32])
        conv_last_t = sb("conv_last_t", [P, 2, 32])
        ch = sb("silu_c_hi_lo", [P, KD, 18], F32R)
        sel_tok = sb("select_tokens", [18, 2 * P], F32R)
        wff = sb("w_forget", [P, KD, HEADS])
        wff_h = sb("w_forget_hi", [P, KD, HEADS], F32R)
        wff_l = sb("w_forget_lo", [P, KD, HEADS], F32R)
        b_f = sb("b_forget", [HEADS, 1])
        pages = sb("page_numbers", [1, SEQS * PAGES], I32)
        ada_h = [sb(f"ada_hi{i}", [18, CH], F32R) for i in range(2)]
        ada_l = [sb(f"ada_lo{i}", [18, CH], F32R) for i in range(2)]
        p_max, p_nb, p_sum, p_inv = (sb(n, [P, 12, 2]) for n in ("p_max", "p_nb", "p_sum", "p_inv"))
        u_max, u_nb, u_sum, u_inv = (sb(n, [P, 8]) for n in ("u_max", "u_nb", "u_sum", "u_inv"))
        gates, pen, pick = sb("gates", [P, 8]), sb("penalty", [P, 8]), sb("pick", [P, 8])
        bn = sb("bn", [P, 3, 2, 6])
        ln_mv = sb("ln_mean_var", [P, 3, 4])
        ncum = sb("minus_8_cum", [HEADS, TOK])
        lf_out = sb("logf_tokens", [P, 3, HEADS])
        H = region(2 * KD * TOK * 4)
        h_h = sb("h_hi", [P, KD, TOK], F32R, at=H)
        h_l = sb("h_lo", [P, KD, TOK], F32R, at=H + KD * TOK * 4)
        state_raw = sb("state_raw", [P, 46, 32], at=H)
        c_rows = sb("c_rows", [9, D], at=H + 8192)
        c_silu = sb("c_silu", [9, D], at=H + 12288)
        u_ext = sb("u_ext", [P, 2, 338], at=H)
        u_acc = sb("u_acc", [P, 2, 336], at=H + 2816)
        lf_sum = sb("lf_sum", [P, 2, SEQS, 64], at=H)
        probs = sb("probs", [P, PAST + TSA], at=H)
        probs_t = sb("probs_t", [P, PAGES + 1, P], at=H + 4352)
        v_tok = sb("v_tok", [P, 2, 3, AW], at=H + 4352 + 4608)
        c_suffix = sb("c_suffix", [P, BP, P], at=H + 4352 + 4608 + 9216)
        y_t = sb("y_t", [P, KD, TOK], at=H)
        ff_last_t = sb("ff_last_t", [P, 44, 32], at=H + KD * TOK * 4)
        T = region(10496)
        bias_r = sb("bias_rows", [P, PAST + TSA], at=T)
        lf_rows = sb("lf_rows", [SEQS * PAGES, PAGE * HEADS], at=T)
        qblk = [sb(f"q_blocks{i}", [P, 2, 3, 64], at=T + 4352 + 1536 * i) for i in range(2)]
        y_row = sb("y_row", [P, AW], at=T + 7424)
        forget = sb("forget", [HEADS, 4, TOK], at=T + 4352)
        ext = [sb(f"ext{i}", [P, 2, 338], at=T + 2720 * i) for i in range(2)]
        acc = sb("acc", [P, 2, 336], at=T + 5440)
        act_f = sb("act_f", [P, TOK], at=T + 8128)
        R = region(8 * CHB)
        raw = [sb(f"raw{i}", [P, KD * CH], at=R + CHB * i) for i in range(4)]
        w_h = [sb(f"w_hi{i}", [P, KD * CH], F32R, at=R + CHB * (4 + i)) for i in range(2)]
        w_l = [sb(f"w_lo{i}", [P, KD * CH], F32R, at=R + CHB * (6 + i)) for i in range(2)]
        k_pages = [sb(f"k_pages{i}", [P, PAGES, AW], at=R + 2 * CHB + PAGES * AW * 4 * i) for i in range(2)]
        k_t = sb("k_t", [P, 2, PAIRS, PAST], at=R + 5 * CHB)
        k_tok = sb("k_tok", [P, 2, 3, AW], at=R + 5 * CHB)
        XS = N_PROJ * TOK * 4
        X = region(56320)
        proj = sb("proj", [P, N_PROJ, TOK], at=X)
        v_pages = sb("v_pages", [P, 2, PAGES, AW], at=X + XS)
        b_row = sb("b_ada_row", [P, 6 * D], at=X)
        rows = sb("rows", [P, 3, D], at=X + 24576)
        c_t = sb("silu_c_t", [P, KD * 9], at=X + 24576 + 12288)
        ln_rows = sb("ln_rows", [P, 3, D], at=X)
        ln_gb1 = sb("ln1_g_b", [P, 2, D], at=X + XS)
        act_h = sb("act_hi", [P, FT, TOK], F32R, at=X)
        act_l = sb("act_lo", [P, FT, TOK], F32R, at=X + FT * TOK * 4)
        M = X + 56320 - 16384
        region(32768)
        mods = sb("mods", [P, 6, 2, D], at=M)
        ff_last = sb("ff_last", [P, 44, 32], at=M + 16384)
        ln_gb2 = sb("ln2_g_b", [P, 2, D], at=M + 16384 + 5632)
        SH_A, SC_A, GT_A, SH_F, SC_F, GT_F = range(6)
        ps = ctx.enter_context(nc.psum_tensor("ps", [P, 8, 512], F32))
        psf = ps[:, :, :].rearrange("p b c -> p (b c)")

        ident = const[:, C_IDENT:C_IDENT + P]
        NT = [P, P, TSA]
        PR = [0, 0, 1]

        const_in, x_in, c_in, bada_in, small_in = (sem(n) for n in ("const_in", "x_in", "c_in", "bada_in", "small_in"))
        brow_zeroed, state_zeroed, state_in, lf_in = sem("brow_zeroed"), sem("state_zeroed"), sem("state_in"), sem("lf_in")
        raw_in = [sem(f"raw_in{i}") for i in range(4)]
        hi_made, lo_made, w_used = sem("hi_made"), sem("lo_made"), sem("w_used")
        silu_made, ct_ready, ct_copied, ch_hi, ch_lo = (
            sem(n) for n in ("silu_made", "ct_ready", "ct_copied", "ch_hi", "ch_lo"))
        adah_made, adal_made, ex_ready, mods_made = (
            sem(n) for n in ("adah_made", "adal_made", "ex_ready", "mods_made"))
        rows_made, ht_ready, hh_made, hl_made = (sem(n) for n in ("rows_made", "ht_ready", "hh_made", "hl_made"))
        tile_ready, tile_moved = sem("tile_ready"), sem("tile_moved")
        wff_hi, wff_lo, ff_ready, absz_made, softplus_made, logf_made, cum_made = (
            sem(n) for n in ("wff_hi", "wff_lo", "ff_ready", "absz_made", "softplus_made", "logf_made", "cum_made"))
        tok_ready, tok_moved, lft_ready, lfsum_zeroed, lfsum_made, suffix_ready, suffix_made = (
            sem(n) for n in ("tok_ready", "tok_moved", "lft_ready", "lfsum_zeroed", "lfsum_made", "suffix_ready",
                             "suffix_made"))
        logft_ready, logft_moved, convlast_made = sem("logft_ready"), sem("logft_moved"), sem("convlast_made")
        kv_stored, stored = sem("kv_stored"), sem("stored")
        ps_ready, pnb_made, pexp_made, pnorm_made, ppt_ready, ppt_moved, py_ready, py_moved = (
            sem(n) for n in ("ps_ready", "pnb_made", "pexp_made", "pnorm_made", "ppt_ready", "ppt_moved", "py_ready",
                             "py_moved"))
        newbias_zeroed, newbias_made, q_built, bias_built = (
            sem(n) for n in ("newbias_zeroed", "newbias_made", "q_built", "bias_built"))
        k_in = [sem(f"k_in{i}") for i in range(2)]
        v_in = [sem(f"v_in{i}") for i in range(4)]
        v_read, s_ready, stats_made, exp_made, inv_made = (
            sem(n) for n in ("v_read", "s_ready", "stats_made", "exp_made", "inv_made"))
        t_ready, moved_a, moved_v, pv_ready, yrow_made, yt_ready, yt_moved = (
            sem(n) for n in ("t_ready", "moved_a", "moved_v", "pv_ready", "yrow_made", "yt_ready", "yt_moved"))
        mixh_made, mixl_made = sem("mixh_made"), sem("mixl_made")
        outa_moved, outv_moved, back_ready = (
            sem(n) for n in ("outa_moved", "outv_moved", "back_ready"))
        ln_in, var_made, std_made, stat_made, normed, gain_made, scaled = (
            sem(n) for n in ("ln_in", "var_made", "std_made", "stat_made", "normed", "gain_made", "scaled"))
        fflast_zeroed, tap_made, gate_made, actf_made, acth_made, actl_made, last_kept, fflast_made = (
            sem(n) for n in ("fflast_zeroed", "tap_made", "gate_made", "actf_made", "acth_made", "actl_made",
                             "last_kept", "fflast_made"))
        dve_step, pool_step, act_step, dve_misc = (sem(n) for n in ("dve_step", "pool_step", "act_step", "dve_misc"))
        ext_moved, past_in, conv_made = sem("ext_moved"), sem("past_in"), sem("conv_made")

        w_ada, w_in, w_o, w_up, w_down = (a[n].rearrange("l r c -> (l r) c").rearrange("(k p) c -> p k c", p=P)
                                          for n in ("w_ada", "w_in", "w_o", "w_up", "w_down"))
        in_at = [P * t + (HEADS if t >= 15 else 0) for t in range(N_PROJ)]

        def raw_k(c):
            return raw[c.raw][:, :].rearrange("p (k c) -> p k c", k=KD)

        def hi_lo(c):
            return (w[c.slot][:, :].rearrange("p (k c) -> p k c", k=KD) for w in (w_h, w_l))

        block = ctx.enter_context(nc.Block())

        @block.sync
        def _(sp):
            sp.dma_start(c_rows[0:1, :], a["c_prompt"]).then_inc(c_in, 16)
            sp.dma_start(c_rows[1:9, :], a["c_sample"]).then_inc(c_in, 16)
            sp.dma_start(const[:, :], a["const"]).then_inc(const_in, 16)

            def slot_free(c):
                after(sp, lo_made, c.n - 3)

            def load_ada(c):
                slot_free(c)
                for k in (0, 4):
                    sp.dma_start(raw_k(c)[:, k:k + 4, :],
                                 w_ada[:, k:k + 4, bass.ds(c.j * CH, CH)]).then_inc(raw_in[c.raw], 16)

            def small_loads():
                sp.wait_ge(brow_zeroed, 1)
                sp.dma_start(b_row[0:1, :], a["b_ada"]).then_inc(bada_in, 16)
                sp.dma_start(xt[:, 0:2, :], a["x_prompt"].rearrange("g (t p) d -> p (g t) d", p=P)).then_inc(x_in, 16)
                sp.dma_start(xt[0:TSA, 2, :], a["x_sample"].rearrange("b t d -> (b t) d")).then_inc(x_in, 16)
                sp.dma_start(b_f[:, :], a["b_f"].rearrange("l h -> h l")).then_inc(small_in, 16)
                sp.dma_start(pages[:, :], a["page_table"].rearrange("b (o p) -> o (b p)", o=1)).then_inc(small_in, 16)
                sp.dma_start(wff[:, :, :], w_in[:, :, 15 * P:15 * P + HEADS]).then_inc(small_in, 16)
                sp.wait_ge(state_zeroed, 1)
                for g in range(4):
                    for at, n, src in ((0, 16, a["state_ffn"].rearrange("l b r (t g j) -> g (l b r) t j", g=4, j=32)),
                                       (16, 3, a["ffn_conv_w"].rearrange("l w (t g j) -> g (l w) t j", g=4, j=32)),
                                       (19, 1, a["ffn_conv_b"].rearrange("l (t g j) -> g l t j", g=4, j=32))):
                        sp.dma_start(state_raw[32 * g + at:32 * g + at + n, 0:44, :], src[g]).then_inc(state_in, 16)
                    for at, n, src in ((0, 16, a["state_conv"].rearrange("l b r (t g j) -> g (l b r) t j", g=4, j=32)),
                                       (16, 3, a["conv_w"].rearrange("l w (t g j) -> g (l w) t j", g=4, j=32))):
                        sp.dma_start(state_raw[32 * g + at:32 * g + at + n, 44:46, :], src[g]).then_inc(state_in, 16)

            for k in range(4):
                load_ada(Chunk(0, 0, k))
                if k == 1:
                    small_loads()
            with sp.Fori(1, N_ADA // 4) as i:
                for k in range(4):
                    load_ada(Chunk(0, i, k))
            for t in range(0, N_PROJ, 2):
                c = Chunk(AT_IN, 0, t // 2)
                slot_free(c)
                for m in range(2):
                    sp.dma_start(raw_k(c)[:, :, m * P:m * P + P],
                                 w_in[:, :, in_at[t + m]:in_at[t + m] + P]).then_inc(raw_in[c.raw], 16)
            sp.wait_ge(small_in, 48)
            for n in range(SEQS * PAGES):
                page = sp.value_load(pages[0:1, n:n + 1], min_val=0, max_val=POOL - 1)
                sp.dma_start(lf_rows[n:n + 1, :],
                             a["cache_fox_logf"][0, bass.ds(page, 1)].rearrange("o s h -> o (s h)")).then_inc(lf_in, 16)

            caches = [(a["cache_fox_k"], a["cache_fox_v"]), (a["cache_moba_k"], a["cache_moba_v"])]

            def page_number(bp, par, page):
                return sp.value_load(pages[0:1, bass.ds(bp * (2 * PAGES) + (par * PAGES + page), 1)],
                                     min_val=0, max_val=POOL - 1)

            def page_of(cache, n):
                return cache[0, bass.ds(n, 1)].rearrange("o s h d -> (o s) (h d)")

            def load_k(bp, kind):
                u = bp * 2 + kind
                for par in range(2):
                    first = page_number(bp, par, 0)
                    if not isinstance(u, int):
                        sp.wait_ge(t_ready, u * 15 + (6 * par - 12))
                    elif u == 1:
                        sp.wait_ge(t_ready, 6 * par + 6)
                    for page in range(PAGES):
                        sp.dma_start(k_pages[par][:, page, :],
                                     page_of(caches[kind][0], page_number(bp, par, page) if page else first)).then_inc(k_in[par], 16)

            def load_v(bp, kind):
                u = bp * 2 + kind
                for g in range(4):
                    first = page_number(bp, 0, 2 * g)
                    after(sp, v_read, u * 4 + (g - 3))
                    for page in (2 * g, 2 * g + 1):
                        for par in range(2):
                            sp.dma_start(v_pages[:, par, page, :],
                                         page_of(caches[kind][1], page_number(bp, par, page)
                                                   if (page, par) != (2 * g, 0) else first)).then_inc(v_in[g], 16)

            sp.wait_ge(w_used, AT_O)
            load_k(0, 0)
            load_v(0, 0)
            load_k(0, 1)
            with sp.Fori(0, BP - 1) as bp:
                load_k(bp + 1, 0)
                load_v(bp, 1)
                load_k(bp + 1, 1)
                load_v(bp + 1, 0)
            load_v(BP - 1, 1)

            def load_rows(w):
                def load(c):
                    slot_free(c)
                    for kk in range(2):
                        sp.dma_start(raw[c.raw][:, kk * D:kk * D + D],
                                     w[:, bass.ds(c.j * 2 + kk, 1), :].rearrange("p o c -> p (o c)"))\
                            .then_inc(raw_in[c.raw], 16)
                return load

            for k in range(N_O):
                if k == 2:
                    sp.wait_ge(t_ready, 15 * (2 * BP - 1) + 9)
                load_rows(w_o)(Chunk(AT_O, 0, k))
            sp.wait_ge(v_read, 8 * BP)
            sp.dma_start(ln_gb1[:, 0, :], a["ln1_g"].to_broadcast([P, D])).then_inc(ln_in, 16)
            sp.dma_start(ln_gb1[:, 1, :], a["ln1_b"].to_broadcast([P, D])).then_inc(ln_in, 16)

            def load_up(c):
                slot_free(c)
                for m in range(2):
                    sp.dma_start(raw_k(c)[:, :, m * P:m * P + P],
                                 w_up[:, :, bass.ds(c.j * P + m * DFF, P)]).then_inc(raw_in[c.raw], 16)

            ring(sp, AT_UP, N_UP, load_up)
            sp.wait_ge(hl_made, 6 * 2)
            sp.dma_start(ln_gb2[:, 0, :], a["ln2_g"].to_broadcast([P, D])).then_inc(ln_in, 16)
            sp.dma_start(ln_gb2[:, 1, :], a["ln2_b"].to_broadcast([P, D])).then_inc(ln_in, 16)
            ring(sp, AT_DOWN, N_DOWN, load_rows(w_down))
            sp.wait_ge(fflast_made, 1)
            for g in range(4):
                for at, n, dst in ((0, 16, o["ffn_s"]), (16, 2, o["ffn_p"])):
                    sp.dma_start(dst.rearrange("l b r (t g j) -> g (l b r) t j", g=4, j=32)[g],
                                 ff_last_t[32 * g + at:32 * g + at + n, :, :]).then_inc(stored, 16)
            sp.wait_ge(scaled, 6)
            sp.dma_start(o["y_p"].rearrange("g (t p) d -> p (g t) d", p=P), xt[:, 0:2, :]).then_inc(stored, 16)
            sp.dma_start(o["y_s"].rearrange("b t d -> (b t) d"), xt[0:TSA, 2, :]).then_inc(stored, 16)
            sp.wait_ge(stored, 16 * (3 + 8 + 8 + 2))
            sp.wait_ge(kv_stored, 16 * 8)

        @block.tensor
        def _(pe):
            mm = pe.matmul

            def product(out, lhs, rhs, start, stop):
                mm(out, lhs[0], rhs[0], start=start, stop=False)
                mm(out, lhs[0], rhs[1], start=False, stop=False)
                return mm(out, lhs[1], rhs[0], start=False, stop=stop)

            pe.wait_ge(const_in, 16)
            pe.wait_ge(silu_made, 1)
            for k in range(KD):
                t = pe.transpose(ps[:, 6, 9 * k:9 * k + 9], c_silu[:, k * P:k * P + P], ident[0:9, 0:9])
            t.then_inc(ct_ready, 1)
            pe.wait_ge(ch_lo, 1)
            pe.wait_ge(bada_in, 16)

            def ada(c):
                pe.wait_ge(lo_made, c.n + 1)
                after(pe, adal_made, c.n - 1)
                out = ps[0:18, c.slot, 0:CH]
                mm(out, const[:, C_ROWB:C_ROWB + 18], b_row[:, bass.ds(c.j * CH, CH)], start=True, stop=False)
                hi, lo = hi_lo(c)
                for k in range(KD):
                    mm(out, ch[:, k, :], hi[:, k, :], start=False, stop=False)
                for k in range(KD):
                    t = mm(out, ch[:, k, :], lo[:, k, :], start=False, stop=k == KD - 1)
                t.then_inc(w_used, 1)

            def spread(c):
                pe.wait_ge(adal_made, c.n + 1)
                after(pe, mods_made, c.n - 1)
                for m in range(2):
                    out = ps[:, 2 + c.slot, m * CH:m * CH + CH]
                    mm(out, sel_tok[:, m * P:m * P + P], ada_h[c.slot][:, :], start=True, stop=False)
                    t = mm(out, sel_tok[:, m * P:m * P + P], ada_l[c.slot][:, :], start=False, stop=True)
                t.then_inc(ex_ready, 1)

            def ada_step(c):
                ada(c)
                if not (isinstance(c.n, int) and c.n == 0):
                    spread(c.before())
            ring(pe, 0, N_ADA, ada_step)
            spread(Chunk(0, N_ADA // 4 - 1, 3))

            def to_features(base):
                for tt in range(3):
                    pe.wait_ge(rows_made, base // 2 + tt + 1)
                    src = rows if base == 0 else ln_rows
                    for half in range(2):
                        for k in range(4):
                            kk = 4 * half + k
                            t = pe.transpose(ps[:, 2 * tt + half, k * P:k * P + NT[tt]],
                                             src[0:NT[tt], tt, kk * P:kk * P + P], ident[0:NT[tt], 0:NT[tt]])
                        t.then_inc(ht_ready, 1)

            to_features(0)

            h = (h_h, h_l)

            def product_tiles(c, bank, count_before):
                hi, lo = hi_lo(c)
                for m in range(2):
                    after(pe, tile_moved, c.j * 2 + (count_before + m - 7))
                    for k in range(KD):
                        t = product(ps[:, bank + m, 0:TOK], [w[:, k, m * P:m * P + P] for w in (hi, lo)],
                                    [x[:, k, :] for x in h], k == 0, k == KD - 1)
                    t.then_inc(w_used if m else tile_ready, 1)

            pe.wait_ge(hl_made, 6)

            def in_step(c):
                pe.wait_ge(lo_made, c.n + 1)
                product_tiles(c, 2 * c.raw, 0)
            ring(pe, AT_IN, N_IN, in_step)
            pe.wait_ge(wff_lo, 1)
            pe.wait_ge(tile_moved, N_PROJ)
            for k in range(KD):
                t = product(ps[0:HEADS, 0, 0:TOK], [wff_h[:, k, :], wff_l[:, k, :]], [x[:, k, :] for x in h],
                            k == 0, k == KD - 1)
            t.then_inc(ff_ready, 1)

            for n, (at, tt) in enumerate((at, tt) for at in (FV, MV, FK, MK) for tt in range(3)):
                after(pe, tok_moved, n - 3)
                for p in range(PAIRS):
                    t = pe.transpose(ps[0:NT[tt], 4 + n % 4, p * P:p * P + P],
                                     proj[:, at + p, tt * P:tt * P + NT[tt]], ident)
                t.then_inc(tok_ready, 1)
            pe.wait_ge(lf_in, 16 * SEQS * PAGES)
            for hh in range(HEADS):
                t = pe.transpose(ps[:, 1, 64 * hh:64 * hh + 64], lf_rows[:, hh:PAGE * HEADS:HEADS], ident[0:64, 0:64])
            t.then_inc(lft_ready, 1)
            pe.wait_ge(logf_made, 1)
            for tt in range(3):
                t = pe.transpose(ps[0:NT[tt], 2, 8 * tt:8 * tt + HEADS], forget[:, 1, tt * P:tt * P + NT[tt]],
                                 ident[0:HEADS, 0:HEADS])
            t.then_inc(logft_ready, 1)
            pe.wait_ge(lfsum_made, 1)
            for bp in range(BP):
                out = ps[:, 3, bp * P:bp * P + P]
                flat = [lf_sum[:, n, 2 * bp:2 * bp + 2, :].rearrange("p b c -> p (b c)") for n in range(2)]
                mm(out, flat[0], const[:, C_TRI:C_TRI + P], start=True, stop=False)
                t = mm(out, flat[1], const[:, C_ONES:C_ONES + P], start=False, stop=True)
            t.then_inc(suffix_ready, 1)

            pe.wait_ge(cum_made, 1)
            pe.wait_ge(tok_moved, 12)
            pe.wait_ge(suffix_made, 1)
            pe.wait_ge(logft_moved, 1)

            def prompt_scores(n):
                kind, hh = n // HEADS, n % HEADS
                q, k = ((FQ, FK), (MQ, MK))[kind]
                r = slice(HD * (hh % 2), HD * (hh % 2) + HD)
                for qt, at in ((0, 0), (1, P)):
                    keys = P * (qt + 1)
                    out = ps[:, n % 2, at:at + keys]
                    t = mm(out, proj[r, q + hh // 2, qt * P:qt * P + P], proj[r, k + hh // 2, 0:keys],
                           start=True, stop=kind == 1)
                    if kind == 0:
                        t = mm(out, const[0:HEADS, C_IDENT + hh:C_IDENT + hh + 1].to_broadcast([HEADS, P]),
                               ncum[:, 0:keys], start=False, stop=True)
                t.then_inc(ps_ready, 1)

            prompt_scores(0)
            for n in range(2 * HEADS):
                kind, hh = n // HEADS, n % HEADS
                if n + 1 < 2 * HEADS:
                    prompt_scores(n + 1)
                pe.wait_ge(pnorm_made, n + 1)
                after(pe, ppt_moved, n - 1)
                base = 384 * (n % 2)
                for b, at in enumerate((0, P, 2 * P)):
                    t = pe.transpose(ps[:, 2 + n % 2, b * P:b * P + P], probs[:, base + at:base + at + P], ident)
                t.then_inc(ppt_ready, 1)
                pe.wait_ge(ppt_moved, n + 1)
                if hh % 2 == 0:
                    after(pe, py_moved, n // 2 - 1)
                bank, r = 4 + (n // 2) % 2, HD * (hh % 2)
                pt = probs_t[:, 3 * (n % 2):3 * (n % 2) + 3, :]
                mm(ps[r:r + HD, bank, 0:TP], v_tok[:, kind, 0, HD * hh:HD * hh + HD],
                   pt[:, 0:2, :].rearrange("p a b -> p (a b)"), start=True, stop=True)
                t = mm(ps[r:r + HD, bank, P:TP], v_tok[:, kind, 1, HD * hh:HD * hh + HD], pt[:, 2, :],
                       start=False, stop=True, skip_group_check=True)
                if hh % 2:
                    t.then_inc(py_ready, 1)

            def move_free(stage, position):
                if position >= 3 and stage is not None:
                    e = EVACS[position - 3]
                    pe.wait_ge(moved_a if e == "A" else moved_v, evacs(stage, position - 3, e))
                elif stage is not None:
                    for e, s in (("A", moved_a), ("V", moved_v)):
                        pe.wait_ge(s, stage * PER[e] + BEFORE[e])

            def first_free(position):
                if position >= 3:
                    e = EVACS[position - 3]
                    pe.wait_ge(moved_a if e == "A" else moved_v, EVACS[:position - 2].count(e))

            def transpose_k(stage, u):
                position = 0
                for par in range(2):
                    pe.wait_ge(k_in[par], u * (16 * PAGES) + 16 * PAGES)
                    for p in range(PAIRS):
                        for half in range(2):
                            if stage is None:
                                first_free(position)
                            else:
                                move_free(stage, position)
                            for g in range(4):
                                t = pe.transpose(ps[:, 3 + position % 3, g * P:g * P + P],
                                                 k_pages[par][:, 4 * half + g, p * P:p * P + P], ident)
                            t.then_inc(t_ready, 1)
                            position += 1

            def scores(bp, kind, u):
                pe.wait_ge(q_built, u + 1)
                if kind == 0:
                    pe.wait_ge(bias_built, bp + 1)
                pe.wait_ge(moved_a, u * PER["A"] + BEFORE["A"])
                pe.wait_ge(moved_v, u * PER["V"] + BEFORE["V"])
                knew = (FK, MK)[kind]
                q = qblk[kind][:, :, :, :].rearrange("p a b c -> p (a b c)")
                for c in range(3):
                    for p in range(PAIRS):
                        for par in range(2):
                            out = ps[64 * par:64 * par + 64, c, 0:512 if c < 2 else TSA]
                            keys = k_t[:, par, p, c * 512:c * 512 + 512] if c < 2 else proj[:, knew + p, TP:TOK]
                            t = mm(out, q[:, 192 * par + 48 * p:192 * par + 48 * p + 64], keys,
                                   start=p == 0, stop=p == PAIRS - 1 and kind == 1)
                    if kind == 0:
                        for par in range(2):
                            out = ps[64 * par:64 * par + 64, c, 0:512 if c < 2 else TSA]
                            t = mm(out, selb[par], bias_r[:, c * 512:c * 512 + (512 if c < 2 else TSA)],
                                   start=False, stop=True)
                t.then_inc(s_ready, 1)

            def transpose_p(stage, u, last):
                pe.wait_ge(exp_made, u + 1)
                for position in (12, 13, 14):
                    bank = 3 + position % 3
                    if position < 14:
                        move_free(stage, position - 12 if last else position)
                        for g in range(4):
                            at = (4 * (position - 12) + g) * P
                            if position == 13 and g == 3:
                                move_free(stage, 2 if last else 14)
                            t = pe.transpose(ps[:, bank, g * P:g * P + P], probs[:, at:at + P], ident)
                    else:
                        t = pe.transpose(ps[0:TSA, bank, 0:P], probs[:, PAST:PAST + TSA], ident)
                    t.then_inc(t_ready, 1)

            def values(stage, kind, u, last):
                if last:
                    pe.wait_ge(moved_a, stage * PER["A"] + BEFORE["A"] + 1)
                    pe.wait_ge(moved_v, stage * PER["V"] + BEFORE["V"] + 2)
                else:
                    pe.wait_ge(moved_a, evacs(stage, 14, "A"))
                    pe.wait_ge(moved_v, evacs(stage, 14, "V"))
                if not (isinstance(u, int) and u == 0):
                    pe.wait_ge(yrow_made, u)
                for page in range(PAGES):
                    if page % 2 == 0:
                        pe.wait_ge(v_in[page // 2], u * 64 + 64)
                    for par in range(2):
                        t = mm(ps[64 * par:64 * par + 64, 6, 0:AW], probs_t[:, page, 64 * par:64 * par + 64],
                               v_pages[:, par, page, :], start=page == 0, stop=False)
                    if page % 2:
                        t.then_inc(v_read, 1)
                for par in range(2):
                    t = mm(ps[64 * par:64 * par + 64, 6, 0:AW], probs_t[0:TSA, PAGES, 64 * par:64 * par + 64],
                           v_tok[0:TSA, kind, 2, :], start=False, stop=True)
                t.then_inc(pv_ready, 1)

            def transpose_y(u):
                pe.wait_ge(yrow_made, u + 1)
                after(pe, yt_moved, u)
                for p in range(PAIRS):
                    t = pe.transpose(ps[:, 7, ROWS * p:ROWS * p + ROWS], y_row[0:ROWS, p * P:p * P + P],
                                     ident[0:ROWS, 0:ROWS])
                t.then_inc(yt_ready, 1)

            selb = [const[:, C_SELB + 64 * par:C_SELB + 64 * par + 64] for par in range(2)]
            pe.wait_ge(py_moved, HEADS)
            transpose_k(None, 0)

            def units(bp, first, last):
                for kind in range(2):
                    u = bp * 2 + kind
                    scores(bp, kind, u)
                    if not (first and kind == 0):
                        transpose_y(u - 1)
                    end = last and kind == 1
                    if not end:
                        transpose_k(u, u + 1)
                    transpose_p(u, u, end)
                    values(u, kind, u, end)

            units(0, True, False)
            with pe.Fori(1, BP - 1) as bp:
                units(bp, False, False)
            units(BP - 1, False, True)
            transpose_y(2 * BP - 1)

            def project_step(c, x, k_of, start, stop):
                pe.wait_ge(lo_made, c.n + 1)
                for kk in range(2):
                    for m in range(KD):
                        at = kk * D + m * P
                        t = product(ps[:, m, 0:TOK], [w[c.slot][:, at:at + P] for w in (w_h, w_l)],
                                    [y[:, bass.ds(k_of + kk, 1), :].rearrange("p o t -> p (o t)") for y in x],
                                    start and kk == 0, stop and kk == 1)
                t.then_inc(w_used, 1)

            def back_to_tokens(n):
                pe.wait_ge(outa_moved, 4 * n + 4)
                pe.wait_ge(outv_moved, 4 * n + 4)
                for tt in range(3):
                    for k in range(KD):
                        t = pe.transpose(ps[0:NT[tt], 2 * tt + k // 4, (k % 4) * P:(k % 4) * P + P],
                                         y_t[:, k, tt * P:tt * P + NT[tt]], ident)
                    t.then_inc(back_ready, 1)

            pe.wait_ge(mixl_made, 3)
            pe.wait_ge(yt_moved, 2 * BP)
            for k in range(N_O):
                project_step(Chunk(AT_O, 0, k), (h_h, h_l), 2 * k, k == 0, k == N_O - 1)
            back_to_tokens(0)
            to_features(6)

            pe.wait_ge(hl_made, 12)

            def up_step(c):
                pe.wait_ge(lo_made, c.n + 1)
                product_tiles(c, 2 * c.raw, N_PROJ)
            ring(pe, AT_UP, N_UP, up_step)
            pe.wait_ge(tile_moved, N_PROJ + 2 * N_UP)
            pe.wait_ge(actl_made, FT)
            x = (act_h, act_l)
            project_step(Chunk(AT_DOWN, 0, 0), x, 0, True, False)
            with pe.Fori(0, N_DOWN // 2 - 1) as i:
                for k in (1, 2):
                    c = Chunk(AT_DOWN, 0, k)
                    c.n = i * 2 + (AT_DOWN + k)
                    project_step(c, x, i * 4 + 2 * k, False, False)
            for k in (N_DOWN - 2, N_DOWN - 1):
                project_step(Chunk(AT_DOWN, 0, k), x, 2 * k, False, k == N_DOWN - 1)
            back_to_tokens(1)

        @block.scalar
        def _(act):
            cp = ACT.Copy
            do = act.activation

            def round_hi(c, n):
                act.wait_ge(raw_in[c.raw], c.loads * 32)
                after(act, w_used, c.n - 1)
                do(w_h[c.slot][:, 0:n], raw[c.raw][:, 0:n], cp).then_inc(hi_made, 1)

            act.wait_ge(c_in, 32)
            do(c_silu[:, :], c_rows[:, :], ACT.Silu).then_inc(silu_made, 1)
            act.wait_ge(const_in, 16)
            do(sel_tok[:, :], const[0:18, C_SELTOK:C_SELTOK + 2 * P], cp).then_inc(silu_made, 1)
            act.wait_ge(ct_copied, 1)
            ct3 = c_t[:, :].rearrange("p (k b) -> p k b", k=KD)
            do(ch[:, :, 0:9], ct3, cp).then_inc(ch_hi, 1)

            def ada_rows(c):
                act.wait_ge(w_used, c.n + 1)
                after(act, ex_ready, c.n - 1)
                do(ada_h[c.slot][:, :], ps[0:18, c.slot, 0:CH], cp).then_inc(adah_made, 1)

            def ada_mods(c, k):
                act.wait_ge(ex_ready, c.n + 1)
                part = c.turn
                do(mods[:, bass.ds(part, 1), :, k * CH:k * CH + CH].rearrange("p o a c -> p (o a) c"),
                   ps[:, 2 + c.slot, :].rearrange("p (a c) -> p a c", a=2), cp).then_inc(mods_made, 1)

            def ada_step(c):
                round_hi(c, KD * CH)
                known = isinstance(c.n, int)
                if not known or c.n >= 1:
                    ada_rows(c.before())
                if not known or c.n >= 2:
                    c2 = c.before().before()
                    ada_mods(c2, c2.k)
            ring(act, 0, N_ADA, ada_step)
            last = Chunk(0, N_ADA // 4 - 1, 3)
            ada_rows(last)
            ada_mods(last.before(), last.before().k)
            ada_mods(last, 3)

            def features_hi(base):
                for tt in range(3):
                    for half in range(2):
                        act.wait_ge(ht_ready, base + 2 * tt + half + 1)
                        do(h_h[:, 4 * half:4 * half + 4, tt * P:tt * P + NT[tt]],
                           ps[:, 2 * tt + half, :].rearrange("p (k t) -> p k t", k=4)[:, :, 0:NT[tt]],
                           cp).then_inc(hh_made, 1)

            features_hi(0)
            act.wait_ge(small_in, 48)
            do(wff_h[:, :, :], wff[:, :, :], cp).then_inc(wff_hi, 1)

            def move_tiles(c, bank):
                for m in range(2):
                    act.wait_ge(w_used if m else tile_ready, c.n + 1 if m else c.j + 1)
                    do(proj[:, bass.ds(c.j * 2 + m, 1), :].rearrange("p o t -> p (o t)"),
                       ps[:, bank + m, 0:TOK], cp).then_inc(tile_moved, 1)

            def in_step(c):
                round_hi(c, KD * CH)
                if not (isinstance(c.j, int) and c.j == 0):
                    move_tiles(c.before(), 2 * c.before().raw)
            ring(act, AT_IN, N_IN, in_step)
            last = Chunk(AT_IN, N_IN // 4 - 1, 3)
            move_tiles(last, 2 * last.raw)

            act.wait_ge(absz_made, 1)
            do(forget[:, 2, :], forget[:, 1, :], ACT.Exp, scale=-1.0).then_inc(act_step, 1)
            act.wait_ge(act_step, 1)
            do(forget[:, 3, :], forget[:, 2, :], ACT.Ln, bias=1.0).then_inc(softplus_made, 1)

            for n, (kv, tt) in enumerate((kv, tt) for kv in ((v_tok, 0), (v_tok, 1), (k_tok, 0), (k_tok, 1))
                                         for tt in range(3)):
                act.wait_ge(tok_ready, n + 1)
                do(kv[0][0:NT[tt], kv[1], tt, :], ps[0:NT[tt], 4 + n % 4, 0:AW], cp).then_inc(tok_moved, 1)
            act.wait_ge(tok_moved, 12)
            for src, kind, po, so in ((v_tok, 0, "fv_p", "fv_s"), (v_tok, 1, "mv_p", "mv_s"),
                                         (k_tok, 0, "fk_p", "fk_s"), (k_tok, 1, "mk_p", "mk_s")):
                act.dma_start(o[po].rearrange("l g (t p) h d -> p (l g t) (h d)", p=P),
                              src[:, kind, 0:2, :]).then_inc(kv_stored, 16)
                act.dma_start(o[so].rearrange("l b t h d -> (l b t) (h d)"), src[0:TSA, kind, 2, :])\
                    .then_inc(kv_stored, 16)
            act.wait_ge(logft_moved, 1)
            for tt in range(2):
                act.dma_start(o["lf_p"][0, 0, tt * P:tt * P + P, :], lf_out[:, tt, :]).then_inc(stored, 16)
            act.dma_start(o["lf_s"].rearrange("l b t h -> (l b t) h"), lf_out[0:TSA, 2, :]).then_inc(stored, 16)
            act.wait_ge(convlast_made, 1)
            for g in range(4):
                for at, n, dst in ((0, 16, o["conv_s"]), (16, 2, o["conv_p"])):
                    act.dma_start(dst.rearrange("l b r (t g j) -> g (l b r) t j", g=4, j=32)[g],
                                  conv_last_t[32 * g + at:32 * g + at + n, :, :]).then_inc(stored, 16)

            def prompt_exp(n):
                act.wait_ge(pnb_made, n + 1)
                after(act, ppt_ready, n - 1)
                for qt, at, w in ((0, 0, P), (1, P, TP)):
                    t = do(probs[:, 384 * (n % 2) + at:384 * (n % 2) + at + w], ps[:, n % 2, at:at + w], ACT.Exp,
                           bias=p_nb[:, n, qt:qt + 1], scale=SCALE, accum_out=p_sum[:, n, qt:qt + 1])
                t.then_inc(pexp_made, 1)

            prompt_exp(0)
            for n in range(2 * HEADS):
                if n + 1 < 2 * HEADS:
                    prompt_exp(n + 1)
                act.wait_ge(ppt_ready, n + 1)
                do(probs_t[:, 3 * (n % 2):3 * (n % 2) + 3, :],
                   ps[:, 2 + n % 2, 0:384].rearrange("p (b q) -> p b q", b=3), cp).then_inc(ppt_moved, 1)
                if n % 2:
                    act.wait_ge(py_ready, n // 2 + 1)
                    q = (FQ, MQ)[n // HEADS] + (n % HEADS) // 2
                    do(proj[:, q, 0:TP], ps[:, 4 + (n // 2) % 2, 0:TP], cp).then_inc(py_moved, 1)

            def move(position, stage_ready):
                act.wait_ge(t_ready, stage_ready)
                bank = 3 + position % 3
                if position < 12:
                    par, p, half = position // 6, position % 6 // 2, position % 2
                    do(k_t[:, par, p, 512 * half:512 * half + 512], ps[:, bank, :], cp).then_inc(moved_a, 1)
                else:
                    g = 4 * (position - 12)
                    do(probs_t[:, g:g + 4, :], ps[:, bank, :].rearrange("p (g r) -> p g r", g=4), cp)\
                        .then_inc(moved_a, 1)

            act.wait_ge(kv_stored, 16 * 8)
            for position in range(12):
                if EVACS[position] == "A":
                    move(position, position + 1)

            def unit_exp(kind, u):
                act.wait_ge(stats_made, u + 1)
                if kind == 0:
                    do(probs[:, :], psf[:, 0:PAST + TSA], ACT.Exp, bias=u_nb[:, 0:1], scale=SCALE,
                       accum_out=u_sum[:, 0:1]).then_inc(exp_made, 1)
                else:
                    for b in range(NBLK + 1):
                        at = slice(MBLK * b, min(MBLK * (b + 1), PAST + TSA))
                        t = do(probs[:, at], probs[:, at], ACT.Exp, bias=u_nb[:, b:b + 1], scale=SCALE,
                               accum_out=u_sum[:, b:b + 1])
                    t.then_inc(exp_made, 1)

            def unit(kind, u, last):
                base = u * 15 + (12 + 1)
                if not last:
                    for position in range(6):
                        move(position, base + position)
                unit_exp(kind, u)
                if not last:
                    move(8, base + 8)
                    move(10, base + 10)
                move(13, base + (1 if last else 13))
                act.wait_ge(pv_ready, u + 1)
                act.wait_ge(inv_made, u + 1)
                do(y_row[:, :], ps[:, 6, 0:AW], cp, scale=u_inv[:, 0:1]).then_inc(yrow_made, 1)

            unit(0, 0, False)
            unit(1, 1, False)
            with act.Fori(1, BP - 1) as bp:
                unit(0, bp * 2, False)
                unit(1, bp * 2 + 1, False)
            unit(0, 2 * BP - 2, False)
            unit(1, 2 * BP - 1, True)

            act.wait_ge(yt_moved, 2 * BP)
            for at, frm, n in ((0, CB, 2), (2, FQ, 3), (5, MQ, 3)):
                do(h_h[:, at:at + n, :], proj[:, frm:frm + n, :], cp).then_inc(mixh_made, 1)
            for k in range(N_O):
                round_hi(Chunk(AT_O, 0, k), 2 * D)

            def move_out(n):
                act.wait_ge(w_used, (AT_UP, AT_DOWN + N_DOWN)[n])
                for m in range(0, KD, 2):
                    do(y_t[:, m, :], ps[:, m, 0:TOK], cp).then_inc(outa_moved, 1)

            move_out(0)

            def norm(n):
                for tt in range(3):
                    act.wait_ge(var_made, 3 * n + tt + 1)
                    do(ln_mv[0:NT[tt], tt, 2:3], ln_mv[0:NT[tt], tt, 1:2], ACT.Sqrt).then_inc(std_made, 1)
                    act.wait_ge(stat_made, 3 * n + tt + 1)
                    r = slice(0, NT[tt])
                    do(xt[r, tt, :], ln_rows[r, tt, :], ACT.Identity, scale=ln_mv[r, tt, 2:3],
                       bias=ln_mv[r, tt, 3:4]).then_inc(normed, 1)

            norm(0)
            features_hi(6)

            def conv_in(c):
                e = ext[c.slot]
                after(act, conv_made, c.j - 1)
                after(act, last_kept, c.j - 1)
                t = None
                for m in range(2):
                    act.wait_ge(w_used if m else tile_ready, c.n + 1 if m else c.j + (N_IN + 1))
                    bank = 2 * c.raw + m
                    do(e[:, m, 2:2 + TP], ps[:, bank, 0:TP], cp).then_inc(ext_moved, 1)
                    do(e[:, m, 258:338].rearrange("p (b t) -> p b t", b=SEQS)[:, :, 2:10],
                       ps[:, bank, TP:TOK].rearrange("p (b t) -> p b t", b=SEQS), cp).then_inc(tile_moved, 1)
                act.wait_ge(past_in, c.j + 1)
                act.wait_ge(tile_moved, c.j * 2 + (N_PROJ + 2))
                act.wait_ge(ext_moved, c.j * 2 + 2)
                after(act, actf_made, c.j)
                for m in range(2):
                    tile = st_t[:, bass.ds(c.j + m * FT, 1), :].rearrange("p o r -> p (o r)")
                    t = do(acc[:, m, :], e[:, m, 0:336], ACT.Identity, scale=tile[:, 16:17], bias=tile[:, 19:20])
                t.then_inc(tap_made, 1)

            def silu_gate(c):
                act.wait_ge(conv_made, c.j + 1)
                do(acc[:, 0, :], acc[:, 0, :], ACT.Silu).then_inc(gate_made, 1)

            def act_hi(c):
                act.wait_ge(actf_made, c.j + 1)
                do(act_h[:, bass.ds(c.j, 1), :].rearrange("p o t -> p (o t)"), act_f[:, :], cp).then_inc(acth_made, 1)

            def up_step(c):
                round_hi(c, KD * CH)
                if not (isinstance(c.j, int) and c.j == 0):
                    b = c.before()
                    conv_in(b)
                    silu_gate(b)
                    act_hi(b)
            ring(act, AT_UP, N_UP, up_step)
            last = Chunk(AT_UP, N_UP // 4, N_UP % 4 - 1)
            conv_in(last)
            silu_gate(last)
            act_hi(last)
            ring(act, AT_DOWN, N_DOWN, lambda c: round_hi(c, 2 * D))
            move_out(1)
            norm(1)

        @block.vector
        def _(dve):
            chain = Chain(dve, dve_step)
            link = chain.link
            stt = dve.scalar_tensor_tensor

            def make_lo(c, n):
                dve.wait_ge(hi_made, c.n + 1)
                after(dve, w_used, c.n - 1)
                dve.tensor_sub(w_l[c.slot][:, 0:n], raw[c.raw][:, 0:n], w_h[c.slot][:, 0:n].bitcast(F32))\
                    .then_inc(lo_made, 1)

            dve.wait_ge(ct_ready, 1)
            dve.tensor_copy(c_t[:, :], ps[:, 6, 0:KD * 9]).then_inc(ct_copied, 1)
            ct3 = c_t[:, :].rearrange("p (k b) -> p k b", k=KD)
            dve.wait_ge(ct_copied, 1)
            dve.wait_ge(ch_hi, 1)
            dve.tensor_sub(ch[:, :, 9:18], ct3, ch[:, :, 0:9].bitcast(F32)).then_inc(ch_lo, 1)

            def ada_lo(c):
                dve.wait_ge(adah_made, c.n + 1)
                dve.tensor_sub(ada_l[c.slot][:, :], ps[0:18, c.slot, 0:CH], ada_h[c.slot][:, :].bitcast(F32))\
                    .then_inc(adal_made, 1)

            def ada_step(c):
                make_lo(c, KD * CH)
                if not (isinstance(c.n, int) and c.n == 0):
                    ada_lo(c.before())
            for k in range(4):
                ada_step(Chunk(0, 0, k))
            dve.wait_ge(state_in, 16 * 4 * 5)
            dve.transpose(st_t[:, :, :], state_raw[:, :, :]).then_inc(dve_misc, 1)
            with dve.Fori(1, N_ADA // 4) as i:
                for k in range(4):
                    ada_step(Chunk(0, i, k))
            ada_lo(Chunk(0, N_ADA // 4 - 1, 3))

            def modulate(src, dst, tt, shift, scale):
                r = slice(0, NT[tt])
                link(stt(dst[r, tt, :], mods[r, scale, PR[tt], :], 1.0, src[r, tt, :], ALU.add, ALU.mult))
                dve.tensor_add(dst[r, tt, :], dst[r, tt, :], mods[r, shift, PR[tt], :]).then_inc(rows_made, 1)

            def features_lo(base, tts):
                for tt in tts:
                    for half in range(2):
                        n = base + 2 * tt + half + 1
                        dve.wait_ge(hh_made, n)
                        s = (slice(None), slice(4 * half, 4 * half + 4), slice(tt * P, tt * P + NT[tt]))
                        dve.tensor_sub(h_l[s], ps[:, 2 * tt + half, :].rearrange("p (k t) -> p k t", k=4)
                                       [:, :, 0:NT[tt]], h_h[s].bitcast(F32)).then_inc(hl_made, 1)

            dve.wait_ge(mods_made, N_ADA)
            dve.wait_ge(x_in, 32)
            dve.wait_ge(dve_misc, 1)
            for tt in range(3):
                modulate(xt, rows, tt, SH_A, SC_A)
            features_lo(0, range(3))
            dve.wait_ge(wff_hi, 1)
            dve.tensor_sub(wff_l[:, :, :], wff[:, :, :], wff_h[:, :, :].bitcast(F32)).then_inc(wff_lo, 1)
            ring(dve, AT_IN, N_IN, lambda c: make_lo(c, KD * CH))

            dve.wait_ge(ff_ready, 1)
            link(dve.tensor_scalar(forget[:, 0, :], ps[0:HEADS, 0, 0:TOK], b_f[:, 0:1], None, ALU.add))
            stt(forget[:, 1, :], forget[:, 0, :], -1.0, forget[:, 0, :], ALU.mult, ALU.max).then_inc(absz_made, 1)
            dve.wait_ge(softplus_made, 1)
            stt(forget[:, 1, :], forget[:, 0, :], 0.0, forget[:, 3, :], ALU.min, ALU.subtract).then_inc(logf_made, 1)
            dve.wait_ge(logf_made, 1)
            link(dve.tensor_tensor_scan(forget[:, 2, :], const[0:HEADS, C_SCAN:C_SCAN + TOK], forget[:, 1, :], 0.0,
                                        ALU.mult, ALU.add))
            dve.tensor_scalar(ncum[:, :], forget[:, 2, :], -1.0 / SCALE, None, ALU.mult).then_inc(cum_made, 1)

            dve.wait_ge(lfsum_zeroed, 1)
            dve.wait_ge(lft_ready, 1)
            lf = [lf_sum[:, n, :, 0:PAGES * HEADS].rearrange("p b (g h) -> p b g h", h=HEADS) for n in range(2)]
            for hh in range(HEADS):
                t = dve.tensor_copy(lf[0][:, :, :, hh],
                                    ps[:, 1, 64 * hh:64 * hh + 64].rearrange("p (b g) -> p b g", g=PAGES))
            link(t)
            for g in range(PAGES - 2, -1, -1):
                t = dve.tensor_add(lf[1][:, :, g, :], lf[1][:, :, g + 1, :], lf[0][:, :, g + 1, :])
                if g:
                    link(t)
            t.then_inc(lfsum_made, 1)
            dve.wait_ge(logft_ready, 1)
            for tt in range(3):
                t = dve.tensor_copy(lf_out[0:NT[tt], tt, :], ps[0:NT[tt], 2, 8 * tt:8 * tt + HEADS])
            t.then_inc(logft_moved, 1)
            dve.wait_ge(suffix_ready, 1)
            dve.tensor_copy(c_suffix[:, :, :], ps[:, 3, :].rearrange("p (b s) -> p b s", b=BP))\
                .then_inc(suffix_made, 1)
            dve.wait_ge(newbias_zeroed, 1)
            for par in range(2):
                t = dve.tensor_copy(bias_r[64 * par:64 * par + HEADS, PAST:PAST + TSA], ncum[:, TP:TOK])
                t.then_inc(newbias_made, 1)

            u_s = u_ext[:, :, 258:338].rearrange("p c (b t) -> p c b t", b=SEQS)
            link(dve.memset(u_ext[:, :, 0:2], 0.0))
            for c in range(2):
                past = st_t[:, 44 + c, 0:16].rearrange("p (b r) -> p b r", r=2)
                dve.tensor_copy(u_s[:, c, :, 0:2], past)
                dve.tensor_mul(u_s[:, c, :, 2:10], proj[:, CC + c, TP:TOK].rearrange("p (b t) -> p b t", b=SEQS),
                               proj[:, CX + c, TP:TOK].rearrange("p (b t) -> p b t", b=SEQS))
                t = dve.tensor_mul(u_ext[:, c, 2:258], proj[:, CC + c, 0:TP], proj[:, CX + c, 0:TP])
            link(t)
            for c in range(2):
                link(dve.tensor_scalar(u_acc[:, c, :], u_ext[:, c, 0:336], st_t[:, 44 + c, 16:17], None, ALU.mult))
                for j in (1, 2):
                    link(stt(u_acc[:, c, :], u_ext[:, c, j:j + 336], st_t[:, 44 + c, 16 + j:17 + j], u_acc[:, c, :],
                             ALU.mult, ALU.add))
                dve.tensor_mul(proj[:, CB + c, 0:TP], proj[:, CB + c, 0:TP], u_acc[:, c, 0:TP])
                new = proj[:, CB + c, TP:TOK].rearrange("p (b t) -> p b t", b=SEQS)
                got = u_acc[:, c, 256:336].rearrange("p (b t) -> p b t", b=SEQS)[:, :, 2:10]
                dve.tensor_mul(new, new, got)
                dve.tensor_copy(conv_last[:, c, 0:16].rearrange("p (b r) -> p b r", r=2), u_s[:, c, :, 8:10])
                t = dve.tensor_copy(conv_last[:, c, 16:18], u_ext[:, c, 256:258])
            link(t)
            dve.transpose(conv_last_t[:, :, :], conv_last[:, :, :]).then_inc(convlast_made, 1)

            def prompt_stats(n):
                kind, hh = n // HEADS, n % HEADS
                dve.wait_ge(ps_ready, n + 1)
                s = ps[:, n % 2, :]
                if kind == 0:
                    v = s[:, 0:384].rearrange("p (b k) -> p b k", b=3)[:, 0:3:2, :]
                    mask = const[:, C_DIAG:C_DIAG + P].unsqueeze(1).to_broadcast([P, 2, P])
                    link(dve.tensor_add(v, v, mask))
                else:
                    sl = float(slopes()[hh] / SCALE)
                    stt(s[:, 0:P], const[:, C_ALIBI + P:C_ALIBI + 2 * P], sl, s[:, 0:P], ALU.mult, ALU.add)
                    link(stt(s[:, P:3 * P], const[:, C_ALIBI:C_ALIBI + 2 * P], sl, s[:, P:3 * P], ALU.mult, ALU.add))
                dve.tensor_reduce(p_max[:, n, 0:1], s[:, 0:P], AX.X, ALU.max)
                link(dve.tensor_reduce(p_max[:, n, 1:2], s[:, P:3 * P], AX.X, ALU.max))
                dve.tensor_scalar(p_nb[:, n, :], p_max[:, n, :], -SCALE, None, ALU.mult).then_inc(pnb_made, 1)

            prompt_stats(0)
            for n in range(2 * HEADS):
                if n + 1 < 2 * HEADS:
                    prompt_stats(n + 1)
                dve.wait_ge(pexp_made, n + 1)
                link(dve.reciprocal(p_inv[:, n, :], p_sum[:, n, :]))
                base = 384 * (n % 2)
                dve.tensor_scalar(probs[:, base:base + P], probs[:, base:base + P], p_inv[:, n, 0:1], None, ALU.mult)
                dve.tensor_scalar(probs[:, base + P:base + 384], probs[:, base + P:base + 384], p_inv[:, n, 1:2], None,
                                  ALU.mult).then_inc(pnorm_made, 1)

            def move(position, stage_ready):
                dve.wait_ge(t_ready, stage_ready)
                bank = 3 + position % 3
                if position < 12:
                    par, p, half = position // 6, position % 6 // 2, position % 2
                    dve.tensor_copy(k_t[:, par, p, 512 * half:512 * half + 512], ps[:, bank, :]).then_inc(moved_v, 1)
                elif position == 12:
                    dve.tensor_copy(probs_t[:, 0:4, :], ps[:, bank, :].rearrange("p (g r) -> p g r", g=4))\
                        .then_inc(moved_v, 1)
                else:
                    dve.tensor_copy(probs_t[0:TSA, PAGES, :], ps[0:TSA, bank, 0:P]).then_inc(moved_v, 1)

            dve.wait_ge(kv_stored, 16 * 8)
            for position in range(12):
                if EVACS[position] == "V":
                    move(position, position + 1)

            def unit_stats(bp, kind, u):
                dve.wait_ge(s_ready, u + 1)
                new = psf[:, PAST:PAST + TSA]
                at = (C_FOXNEW, C_MOBANEW)[kind]
                mask = const[:, bass.ds(bp * TSA + at, TSA)]
                if kind == 0:
                    link(dve.tensor_add(new, new, mask))
                    link(dve.tensor_reduce(u_max[:, 0:1], psf[:, 0:PAST + TSA], AX.X, ALU.max))
                    dve.tensor_scalar(u_nb[:, 0:1], u_max[:, 0:1], -SCALE, None, ALU.mult).then_inc(stats_made, 1)
                    return
                link(dve.tensor_reduce(gates[:, 0:NBLK], psf[:, 0:PAST].rearrange("p (b k) -> p b k", b=NBLK), AX.X,
                                       ALU.add))
                link(dve.tensor_reduce(gates[:, 4:5], gates[:, 0:NBLK], AX.X, ALU.min))
                link(stt(pick[:, 0:NBLK], gates[:, 0:NBLK], gates[:, 4:5], const[:, C_RANK:C_RANK + NBLK],
                         ALU.is_equal, ALU.mult))
                link(dve.tensor_reduce(pick[:, 4:5], pick[:, 0:NBLK], AX.X, ALU.max))
                link(dve.tensor_scalar(pen[:, 0:NBLK], pick[:, 0:NBLK], pick[:, 4:5], NEG, ALU.is_equal, ALU.mult))
                dve.tensor_add(probs[:, PAST:PAST + TSA], new, mask)
                link(dve.tensor_add(probs[:, 0:PAST], psf[:, 0:PAST], const[:, C_MOBAPAST:C_MOBAPAST + PAST]))
                dve.tensor_reduce(u_max[:, 4:5], probs[:, PAST:PAST + TSA], AX.X, ALU.max)
                link(dve.tensor_reduce(u_max[:, 0:NBLK], probs[:, 0:PAST].rearrange("p (b k) -> p b k", b=NBLK), AX.X,
                                       ALU.max))
                link(dve.tensor_add(u_max[:, 0:NBLK], u_max[:, 0:NBLK], pen[:, 0:NBLK]))
                link(dve.tensor_reduce(u_max[:, 5:6], u_max[:, 0:5], AX.X, ALU.max))
                dve.tensor_scalar(u_nb[:, 0:5], pen[:, 0:5], u_max[:, 5:6], SCALE, ALU.subtract, ALU.mult)\
                    .then_inc(stats_made, 1)

            def take_y(bp, kind):
                q = (FQ, MQ)[kind]
                for half in range(2):
                    r = slice(HD * half, HD * half + HD)
                    src = ps[r, 7, 0:384].rearrange("p (a b c) -> p a b c", a=3, b=2)[:, :, :, TS * half:TS * half + TS]
                    for p in range(PAIRS):
                        t = dve.tensor_copy(proj[r, q + p, bass.ds(bp * (2 * TS) + TP, 2 * TS)]
                                            .rearrange("p (b t) -> p b t", b=2), src[:, p])
                t.then_inc(yt_moved, 1)

            def unit(bp, kind, u, first, last):
                base = u * 15 + (12 + 1)
                unit_stats(bp, kind, u)
                if not first:
                    dve.wait_ge(yt_ready, u)
                    take_y(bp if kind else bp - 1, 1 - kind)
                if not last:
                    for position in (6, 7, 9, 11):
                        move(position, base + position)
                dve.wait_ge(exp_made, u + 1)
                if kind == 1:
                    link(dve.tensor_reduce(u_sum[:, 5:6], u_sum[:, 0:5], AX.X, ALU.add))
                dve.reciprocal(u_inv[:, 0:1], u_sum[:, 0:1] if kind == 0 else u_sum[:, 5:6]).then_inc(inv_made, 1)
                move(12, base + (0 if last else 12))
                move(14, base + (2 if last else 14))

            LINKS = 2 + 10
            chain.start += chain.k
            chain.k = 0
            dve.memset(pen[:, :], 0.0).then_inc(dve_misc, 1)
            dve.wait_ge(dve_misc, 2)
            chain.enter(0, LINKS)
            unit(0, 0, 0, True, False)
            unit(0, 1, 1, False, False)
            with dve.Fori(1, BP - 1) as bp:
                chain.enter(bp, LINKS)
                unit(bp, 0, bp * 2, False, False)
                unit(bp, 1, bp * 2 + 1, False, False)
            chain.enter(BP - 1, LINKS)
            unit(BP - 1, 0, 2 * BP - 2, False, False)
            unit(BP - 1, 1, 2 * BP - 1, False, True)
            chain.close(BP)
            dve.wait_ge(yt_ready, 2 * BP)
            take_y(BP - 1, 1)

            for n, (at, frm, cnt) in enumerate(((0, CB, 2), (2, FQ, 3), (5, MQ, 3))):
                dve.wait_ge(mixh_made, n + 1)
                dve.wait_ge(yt_moved, 2 * BP)
                dve.tensor_sub(h_l[:, at:at + cnt, :], proj[:, frm:frm + cnt, :],
                               h_h[:, at:at + cnt, :].bitcast(F32)).then_inc(mixl_made, 1)
            for k in range(N_O):
                make_lo(Chunk(AT_O, 0, k), 2 * D)

            def move_out(n):
                dve.wait_ge(w_used, (AT_UP, AT_DOWN + N_DOWN)[n])
                for m in range(1, KD, 2):
                    dve.tensor_copy(y_t[:, m, :], ps[:, m, 0:TOK]).then_inc(outv_moved, 1)

            move_out(0)

            def ln_stats(n, tt, gate):
                r = slice(0, NT[tt])
                dve.wait_ge(back_ready, 3 * n + tt + 1)
                row, mv = ln_rows[r, tt, :], ln_mv[r, tt, :]
                link(stt(row, mods[r, gate, PR[tt], :], 1.0, psf[r, 1024 * tt:1024 * tt + D], ALU.add, ALU.mult))
                link(stt(row, xt[r, tt, :], ALPHA, row, ALU.mult, ALU.add))
                for hf in range(2):
                    t = dve.bn_stats(bn[r, tt, hf, :], ln_rows[r, tt, 512 * hf:512 * hf + 512])
                link(t)
                link(dve.bn_aggr(mv[:, 0:2], bn[r, tt, :, :].rearrange("p a b -> p (a b)")))
                dve.tensor_scalar(mv[:, 1:2], mv[:, 1:2], EPS, None, ALU.add).then_inc(var_made, 1)

            def inverse_std(n, tt):
                mv = ln_mv[0:NT[tt], tt, :]
                dve.wait_ge(std_made, 3 * n + tt + 1)
                link(dve.reciprocal(mv[:, 2:3], mv[:, 2:3]))
                stt(mv[:, 3:4], mv[:, 0:1], -1.0, mv[:, 2:3], ALU.mult, ALU.mult).then_inc(stat_made, 1)

            def ffn_rows(tt):
                dve.wait_ge(scaled, tt + 1)
                modulate(xt, ln_rows, tt, SH_F, SC_F)

            ln_stats(0, 0, GT_A)
            inverse_std(0, 0)
            ln_stats(0, 1, GT_A)
            inverse_std(0, 1)
            ffn_rows(0)
            ln_stats(0, 2, GT_A)
            inverse_std(0, 2)
            ffn_rows(1)
            ffn_rows(2)
            features_lo(6, range(3))

            for e in ext:
                t = dve.memset(e[:, :, 0:2], 0.0)
            link(t)
            chain.start += chain.k
            chain.k = 0

            def past_rows(c):
                for m in range(2):
                    src = st_t[:, bass.ds(c.j + m * FT, 1), 0:16].rearrange("p o (b r) -> p (o b) r", r=2)
                    t = dve.tensor_copy(ext[c.slot][:, m, 258:338].rearrange("p (b t) -> p b t", b=SEQS)[:, :, 0:2],
                                        src)
                t.then_inc(past_in, 1)

            def conv(c):
                e = ext[c.slot]
                dve.wait_ge(tap_made, c.j + 1)
                for m in range(2):
                    tile = st_t[:, bass.ds(c.j + m * FT, 1), :].rearrange("p o r -> p (o r)")
                    for j in (1, 2):
                        t = stt(acc[:, m, :], e[:, m, j:j + 336], tile[:, 16 + j:17 + j], acc[:, m, :],
                                ALU.mult, ALU.add)
                        if m == 0 or j == 1:
                            link(t)
                t.then_inc(conv_made, 1)
                dve.wait_ge(conv_made, c.j + 1)
                dve.wait_ge(gate_made, c.j + 1)
                after(dve, acth_made, c.j)
                link(dve.tensor_mul(act_f[:, 0:TP], acc[:, 0, 0:TP], acc[:, 1, 0:TP]))
                s = [acc[:, m, 256:336].rearrange("p (b t) -> p b t", b=SEQS)[:, :, 2:10] for m in range(2)]
                dve.tensor_mul(act_f[:, TP:TOK].rearrange("p (b t) -> p b t", b=SEQS), s[0], s[1])\
                    .then_inc(actf_made, 1)
                dve.wait_ge(actf_made, c.j + 1)
                dve.wait_ge(acth_made, c.j + 1)
                dve.tensor_sub(act_l[:, bass.ds(c.j, 1), :].rearrange("p o t -> p (o t)"), act_f[:, :],
                               act_h[:, bass.ds(c.j, 1), :].rearrange("p o t -> p (o t)").bitcast(F32))\
                    .then_inc(actl_made, 1)

            def up_step(c):
                if c.k == 0:
                    chain.start = links if isinstance(c.turn, int) and c.turn == 0 else links - 4
                    chain.enter(c.turn, 16)
                make_lo(c, KD * CH)
                if not (isinstance(c.j, int) and c.j == 0):
                    b = c.before()
                    past_rows(b)
                    conv(b)
            links = chain.start
            ring(dve, AT_UP, N_UP, up_step)
            last = Chunk(AT_UP, N_UP // 4, N_UP % 4 - 1)
            past_rows(last)
            conv(last)
            chain.start, chain.turn, chain.per, chain.k = chain.start + 16 * (N_UP // 4) + chain.k, 0, 0, 0
            dve.wait_ge(last_kept, N_UP)
            dve.transpose(ff_last_t[:, :, :], ff_last[:, :, :]).then_inc(fflast_made, 1)
            ring(dve, AT_DOWN, N_DOWN, lambda c: make_lo(c, 2 * D))
            move_out(1)
            for tt in range(3):
                ln_stats(1, tt, GT_F)
                inverse_std(1, tt)

        @block.gpsimd
        def _(pool):
            pool.memset(b_row[:, :], 0.0).then_inc(brow_zeroed, 1)
            pool.memset(state_raw[:, :, :], 0.0).then_inc(state_zeroed, 1)
            pool.memset(conv_last[:, :, :], 0.0).then_inc(pool_step, 1)
            pool.wait_ge(ff_ready, 1)
            pool.memset(lf_sum[:, :, :, :], 0.0).then_inc(lfsum_zeroed, 1)
            pool.wait_ge(lft_ready, 1)
            pool.memset(bias_r[:, PAST:PAST + TSA], 0.0).then_inc(newbias_zeroed, 1)
            pool.wait_ge(cum_made, 1)
            pool.wait_ge(logft_ready, 1)
            for q in qblk:
                pool.memset(q[:, :, :, :], 0.0).then_inc(pool_step, 1)
            pool.wait_ge(pool_step, 3)

            def build_q(bp, kind, u):
                after(pool, s_ready, u - 1)
                at = (FQ, MQ)[kind]
                for half in range(2):
                    r = slice(HD * half, HD * half + HD)
                    for p in range(PAIRS):
                        t = pool.tensor_copy(qblk[kind][r, :, p, TS * half:TS * half + TS],
                                             proj[r, at + p, bass.ds(bp * (2 * TS) + TP, 2 * TS)]
                                             .rearrange("p (b t) -> p b t", b=2))
                t.then_inc(q_built, 1)

            def build_bias(bp):
                after(pool, s_ready, bp * 2 - 1)
                pool.tensor_tensor(bias_r[:, 0:PAST].rearrange("p (g s) -> p g s", g=PAGES),
                                   c_suffix[:, bass.ds(bp, 1), :].to_broadcast([P, PAGES, P]),
                                   const[:, C_PAGEM:C_PAGEM + PAGES].unsqueeze(2).to_broadcast([P, PAGES, P]),
                                   ALU.mult).then_inc(bias_built, 1)

            pool.wait_ge(tile_moved, N_PROJ)
            pool.wait_ge(suffix_made, 1)
            pool.wait_ge(newbias_made, 2)

            def units(bp):
                after(pool, q_built, bp * 2)
                build_bias(bp)
                pool.wait_ge(bias_built, bp + 1)
                build_q(bp, 0, bp * 2)
                build_q(bp, 1, bp * 2 + 1)
            units(0)
            with pool.Fori(1, BP) as bp:
                units(bp)

            def scale_row(n, gb, tt):
                r = slice(0, NT[tt])
                pool.wait_ge(normed, 3 * n + tt + 1)
                pool.tensor_mul(xt[r, tt, :], xt[r, tt, :], gb[r, 0, :]).then_inc(gain_made, 1)
                pool.wait_ge(gain_made, 3 * n + tt + 1)
                pool.tensor_add(xt[r, tt, :], xt[r, tt, :], gb[r, 1, :]).then_inc(scaled, 1)

            def scale_rows(n, gb):
                pool.wait_ge(ln_in, 32 * (n + 1))
                for tt in range(3):
                    scale_row(n, gb, tt)

            scale_rows(0, ln_gb1)
            pool.memset(ff_last[:, :, :], 0.0).then_inc(fflast_zeroed, 1)
            pool.wait_ge(fflast_zeroed, 1)

            def keep_last(c):
                pool.wait_ge(tap_made, c.j + 1)
                e = ext[c.slot]
                for m in range(2):
                    dst = ff_last[:, bass.ds(c.j + m * FT, 1), :].rearrange("p o r -> p (o r)")
                    pool.tensor_copy(dst[:, 0:16].rearrange("p (b r) -> p b r", r=2),
                                     e[:, m, 258:338].rearrange("p (b t) -> p b t", b=SEQS)[:, :, 8:10])
                    t = pool.tensor_copy(dst[:, 16:18], e[:, m, 256:258])
                t.then_inc(last_kept, 1)
            ring(pool, AT_UP, N_UP, keep_last)
            scale_rows(1, ln_gb2)


NAMES = ["x_prompt", "x_sample", "cache_fox_k", "cache_fox_v", "cache_fox_logf", "cache_moba_k", "cache_moba_v",
         "state_conv", "state_ffn", "page_table", "c_prompt", "c_sample", "w_ada", "b_ada", "w_in", "b_f", "conv_w",
         "w_o", "ln1_g", "ln1_b", "w_up", "ffn_conv_w", "ffn_conv_b", "w_down", "ln2_g", "ln2_b"]


def outputs():
    out = [("y_p", (1, TP, D)), ("y_s", (SEQS, TS, D))]
    for s, g, t in (("p", 1, TP), ("s", SEQS, TS)):
        out += [(f"fk_{s}", (1, g, t, HEADS, HD)), (f"fv_{s}", (1, g, t, HEADS, HD)), (f"lf_{s}", (1, g, t, HEADS)),
                (f"mk_{s}", (1, g, t, HEADS, HD)), (f"mv_{s}", (1, g, t, HEADS, HD)), (f"conv_{s}", (1, g, 2, CW)),
                (f"ffn_{s}", (1, g, 2, 2 * DFF))]
    return out


def kernel(**inputs):
    import concourse.bacc as bacc
    from concourse.bass_utils import run_bass_kernel_spmd

    nc = bacc.Bacc("TRN2", target_bir_lowering=False, num_devices=1, dynamic_dma_scratch_size=1024)
    arrays = {n: np.ascontiguousarray(inputs[n]) for n in NAMES}
    arrays["const"] = constants()
    a = {n: nc.dram_tensor(f"in_{n}", x.shape, mybir.dt.from_np(x.dtype), kind="ExternalInput").ap()
         for n, x in arrays.items()}
    o = {n: nc.dram_tensor(f"out_{n}", s, F32, kind="ExternalOutput").ap() for n, s in outputs()}
    build(nc, a, o)
    r = run_bass_kernel_spmd(nc, [{f"in_{n}": x for n, x in arrays.items()}], core_ids=[0])
    return tuple(r.results[0][f"out_{n}"] for n, _ in outputs())
```

```python
from contextlib import ExitStack

import numpy as np

import concourse.bass as bass
from concourse import mybir

F32 = mybir.dt.float32
F32R = mybir.dt.float32r
I32 = mybir.dt.int32
ALU = mybir.AluOpType
ACT = mybir.ActivationFunctionType
AX = mybir.AxisListType

P = 128
D = 1024
KD = D // P
TP, SEQS, TS = 256, 8, 8
TSA = SEQS * TS
TOK = TP + TSA
HEADS, HD = 6, 64
AW = HEADS * HD
PAIRS = HEADS // 2
CW = D // 4
PAST, PAGE = 1024, 128
PAGES = PAST // PAGE
POOL = 80
DFF = 2816
FT = DFF // P
MBLK, NBLK = 256, PAST // 256
NEG = -1.0e30
SCALE = HD ** -0.5
ALPHA = 2.0 ** 0.25
EPS = 1e-5
BP = SEQS // 2
ROWS = 112

CH = 256
BLK = D // CH
N_ADA1, N_ADA2 = 2 * BLK, 4 * BLK
N_IN, N_O, N_UP, N_DOWN = 12, KD // 2, FT, FT // 2
CHB = KD * CH * 4
AT_IN = N_ADA1
AT_ADA2 = AT_IN + N_IN
AT_O = AT_ADA2 + N_ADA2
AT_UP = AT_O + N_O
AT_DOWN = AT_UP + N_UP

CB, CC, CX, FQ, FK, FV, MQ, MK, MV = 0, 2, 4, 6, 9, 12, 15, 18, 21
N_PROJ = 24
MIXED = [0, 1, 6, 7, 8, 15, 16, 17]

C_IDENT, C_SELTOK = 0, 128
C_EARLY = C_SELTOK + 2 * P
C_TRI, C_ONES, C_DIAG, C_ALIBI = (C_EARLY + P * i for i in range(4))
C_SELB = C_ALIBI + 256
C_PAGEM = C_SELB + 128
C_FOXNEW = C_PAGEM + PAGES
C_MOBANEW = C_FOXNEW + BP * TSA
C_MOBAPAST = C_MOBANEW + BP * TSA
C_SCAN = C_MOBAPAST + PAST
C_RANK = C_SCAN + TOK
C_ALL = C_RANK + NBLK


def slopes():
    return 2.0 ** (-8.0 * np.arange(1, HEADS + 1) / HEADS)


def constants():
    c = np.zeros((P, C_ALL), np.float64)
    i = np.arange(P)
    c[:, C_IDENT:C_IDENT + P] = np.eye(P)
    c[:, C_TRI:C_TRI + P] = i[:, None] > i[None, :]
    c[:, C_ONES:C_ONES + P] = 1
    c[:, C_DIAG:C_DIAG + P] = np.where(i[None, :] <= i[:, None], 0, NEG)
    c[:, C_ALIBI:C_ALIBI + P] = i[None, :] - i[:, None] - P
    c[:, C_ALIBI + P:C_ALIBI + 2 * P] = np.where(i[None, :] <= i[:, None], i[None, :] - i[:, None], NEG)
    par, x = i // 64, i % 64
    for r in range(P):
        if x[r] < PAGES * HEADS:
            page, h = x[r] // HEADS, x[r] % HEADS
            c[r, C_SELB + 64 * par[r] + TS * h:C_SELB + 64 * par[r] + TS * h + TS] = 1
            c[r, C_PAGEM + page] = 1 / SCALE
        if x[r] < HEADS * TS:
            h, q = x[r] // TS, x[r] % TS
            sl = slopes()[h] / SCALE
            c[r, C_MOBAPAST:C_MOBAPAST + PAST] = sl * (np.arange(PAST) - PAST - q)
            for bp in range(BP):
                at = C_FOXNEW + bp * TSA
                am = C_MOBANEW + bp * TSA
                for s in range(TSA):
                    ok = s // TS == 2 * bp + par[r] and s % TS <= q
                    c[r, at + s] = 0 if ok else NEG
                    c[r, am + s] = sl * (s % TS - q) if ok else NEG
    for r in range(18):
        b = r % 9
        if b == 0:
            c[r, C_SELTOK:C_SELTOK + P] = 1
        else:
            c[r, C_SELTOK + P + (b - 1) * TS:C_SELTOK + P + b * TS] = 1
    c[:, C_SCAN:C_SCAN + TOK] = 1
    c[:, C_SCAN] = 0
    c[:, C_SCAN + TP:C_SCAN + TOK:TS] = 0
    c[:, C_RANK:C_RANK + NBLK] = 1 + np.arange(NBLK)
    return c.astype(np.float32)


class Chain:

    def __init__(self, eng, sem):
        self.eng, self.sem, self.start, self.turn, self.per, self.k = eng, sem, 0, 0, 0, 0

    def link(self, instruction):
        self.k += 1
        instruction.then_inc(self.sem, 1)
        self.eng.wait_ge(self.sem, self.turn * self.per + (self.start + self.k))

    def enter(self, turn, per):
        self.turn, self.per, self.k = turn, per, 0

    def close(self, turns):
        assert self.k == self.per
        self.start, self.turn, self.per, self.k = self.start + turns * self.per, 0, 0, 0


class Chunk:

    def __init__(self, base, turn, k):
        self.j = turn * 4 + k
        self.n = turn * 4 + (base + k)
        self.raw, self.slot = (base + k) % 4, (base + k) % 2
        self.loads = turn + ((base + k) // 4 + 1)
        self.base, self.turn, self.k = base, turn, k

    def before(self):
        return Chunk(self.base, self.turn, self.k - 1) if self.k else Chunk(self.base, self.turn - 1, 3)


def ring(eng, base, count, step):
    turns = count // 4

    def turn(i):
        for k in range(4):
            step(Chunk(base, i, k))

    turn(0)
    if turns > 1:
        with eng.Fori(1, turns) as i:
            turn(i)
    for k in range(count % 4):
        step(Chunk(base, turns, k))


class Ada:

    def __init__(self, a):
        self.a = a
        self.late = a >= N_ADA1
        j = a - N_ADA1 if self.late else a
        self.chunk = Chunk(AT_ADA2 if self.late else 0, j // 4, j % 4)
        self.part, self.block = (a // BLK, a % BLK) if self.late else (a % 2, a // 2)
        self.column = self.part * D + self.block * CH
        self.bank, self.spread_bank, self.back = (5, 6, 1) if self.late else (a % 2, 2 + a % 2, 2)


ADA1 = [Ada(a) for a in range(N_ADA1)]
ADA2 = [Ada(a) for a in range(N_ADA1, N_ADA1 + N_ADA2)]
WITH_HEAD = [range(N_ADA2 * n // (2 * HEADS), N_ADA2 * (n + 1) // (2 * HEADS)) for n in range(2 * HEADS)]


def after(eng, semaphore, count):
    if not isinstance(count, int) or count > 0:
        eng.wait_ge(semaphore, count)


EVACS = "AAAAAAVVAVAV" + "VAV"
BEFORE = {"A": 8, "V": 4}
PER = {e: EVACS.count(e) for e in "AV"}


def evacs(stage, position, engine):
    return stage * PER[engine] + (BEFORE[engine] + EVACS[:position + 1].count(engine))


def build(nc, a, o):
    ctx = ExitStack()
    with ctx:
        sem = lambda n: ctx.enter_context(nc.semaphore(n))
        place = [1152]

        def region(size):
            at = place[0]
            place[0] += -(-size // 32) * 32
            return at

        def sb(name, shape, dt=F32, at=None):
            if at is None:
                at = region(int(np.prod(shape[1:])) * 4)
            return nc.alloc_sbuf_tensor_at(name, shape, dt, offset=at)

        const = sb("const", [P, C_ALL])
        xt = sb("x_tokens", [P, 3, D])
        st_t = sb("states_t", [P, 46, 32])
        conv_last = sb("conv_last", [P, 2, 32])
        conv_last_t = sb("conv_last_t", [P, 2, 32])
        ch = sb("silu_c_hi_lo", [P, KD, 18], F32R)
        wff = sb("w_forget", [P, KD, HEADS])
        wff_h = sb("w_forget_hi", [P, KD, HEADS], F32R)
        wff_l = sb("w_forget_lo", [P, KD, HEADS], F32R)
        b_f = sb("b_forget", [HEADS, 1])
        pages = sb("page_numbers", [1, SEQS * PAGES], I32)
        ada_row = [sb(f"ada_rows{i}", [18, CH]) for i in range(2)]
        b_ada = [sb(f"b_ada{i}", [18, CH]) for i in range(4)]
        p_max, p_nb, p_sum, p_inv = (sb(n, [P, 12, 2]) for n in ("p_max", "p_nb", "p_sum", "p_inv"))
        u_max, u_nb, u_sum, u_inv = (sb(n, [P, 8]) for n in ("u_max", "u_nb", "u_sum", "u_inv"))
        gates, pen, pick = sb("gates", [P, 8]), sb("penalty", [P, 8]), sb("pick", [P, 8])
        bn = sb("bn", [P, 3, 2, 6])
        ln_mv = sb("ln_mean_var", [P, 3, 4])
        ncum = sb("minus_8_cum", [HEADS, TOK])
        lf_out = sb("logf_tokens", [P, 3, HEADS])
        H = region(2 * KD * TOK * 4)
        h_h = sb("h_hi", [P, KD, TOK], F32R, at=H)
        h_l = sb("h_lo", [P, KD, TOK], F32R, at=H + KD * TOK * 4)
        c_rows = sb("c_rows", [9, D], at=H + 8192)
        c_silu = sb("c_silu", [9, D], at=H + 12288)
        lf_sum = sb("lf_sum", [P, 2, SEQS, 64], at=H)
        probs = sb("probs", [P, PAST + TSA], at=H)
        probs_t = sb("probs_t", [P, PAGES + 1, P], at=H + 4352)
        v_tok = sb("v_tok", [P, 2, 3, AW], at=H + 4352 + 4608)
        c_suffix = sb("c_suffix", [P, BP, P], at=H + 4352 + 4608 + 9216)
        y_t = sb("y_t", [P, KD, TOK], at=H)
        ff_last_t = sb("ff_last_t", [P, 44, 32], at=H + KD * TOK * 4)
        T = region(10496)
        bias_r = sb("bias_rows", [P, PAST + TSA], at=T)
        lf_rows = sb("lf_rows", [SEQS * PAGES, PAGE * HEADS], at=T)
        state_raw = sb("state_raw", [P, 46, 32], at=T + 3072)
        qblk = [sb(f"q_blocks{i}", [P, 2, 3, 64], at=T + 4352 + 1536 * i) for i in range(2)]
        y_row = sb("y_row", [P, AW], at=T + 7424)
        forget = sb("forget", [HEADS, 4, TOK], at=T + 4352)
        ext = [sb(f"ext{i}", [P, 2, 338], at=T + 2720 * i) for i in range(2)]
        acc = sb("acc", [P, 2, 336], at=T + 5440)
        act_f = sb("act_f", [P, TOK], at=T + 8128)
        R = region(8 * CHB)
        raw = [sb(f"raw{i}", [P, KD * CH], at=R + CHB * i) for i in range(4)]
        w_h = [sb(f"w_hi{i}", [P, KD * CH], F32R, at=R + CHB * (4 + i)) for i in range(2)]
        w_l = [sb(f"w_lo{i}", [P, KD * CH], F32R, at=R + CHB * (6 + i)) for i in range(2)]
        k_pages = [sb(f"k_pages{i}", [P, PAGES, AW], at=R + 2 * CHB + PAGES * AW * 4 * i) for i in range(2)]
        k_t = sb("k_t", [P, 2, PAIRS, PAST], at=R + 5 * CHB)
        XS = N_PROJ * TOK * 4
        X = region(56320)
        proj = sb("proj", [P, N_PROJ, TOK], at=X)
        v_pages = sb("v_pages", [P, 2, PAGES, AW], at=X + XS)
        k_tok = sb("k_tok", [P, 2, 3, AW], at=X + XS)
        u_ext = sb("u_ext", [P, 2, 338], at=X + XS + 9216)
        u_acc = sb("u_acc", [P, 2, 336], at=X + XS + 9216 + 2816)
        rows = sb("rows", [P, 3, D], at=X + 24576)
        c_t = sb("silu_c_t", [P, KD * 9], at=X + 24576 + 12288)
        ln_rows = sb("ln_rows", [P, 3, D], at=X)
        ln_gb1 = sb("ln1_g_b", [P, 2, D], at=X + XS)
        act_h = sb("act_hi", [P, FT, TOK], F32R, at=X)
        act_l = sb("act_lo", [P, FT, TOK], F32R, at=X + FT * TOK * 4)
        M = X + 56320 - 16384
        region(32768)
        mods = sb("mods", [P, 6, 2, D], at=M)
        ff_last = sb("ff_last", [P, 44, 32], at=M + 16384)
        ln_gb2 = sb("ln2_g_b", [P, 2, D], at=M + 16384 + 5632)
        SH_A, SC_A, GT_A, SH_F, SC_F, GT_F = range(6)
        ps = ctx.enter_context(nc.psum_tensor("ps", [P, 8, 512], F32))
        psf = ps[:, :, :].rearrange("p b c -> p (b c)")

        ident = const[:, C_IDENT:C_IDENT + P]
        NT = [P, P, TSA]
        PR = [0, 0, 1]

        const_in, tables_in, x_in, c_in, small_in = (
            sem(n) for n in ("const_in", "tables_in", "x_in", "c_in", "small_in"))
        bias_in = [sem(f"bias_in{i}") for i in range(4)]
        bias_zeroed, state_zeroed, state_in, lf_in = sem("bias_zeroed"), sem("state_zeroed"), sem("state_in"), sem("lf_in")
        raw_in = [sem(f"raw_in{i}") for i in range(4)]
        hi_made, lo_made, w_used = sem("hi_made"), sem("lo_made"), sem("w_used")
        silu_made, ct_ready, ct_copied, ch_hi, ch_lo = (
            sem(n) for n in ("silu_made", "ct_ready", "ct_copied", "ch_hi", "ch_lo"))
        ada_made, ex_ready, mods_made, x_scaled = (
            sem(n) for n in ("ada_made", "ex_ready", "mods_made", "x_scaled"))
        rows_made, ht_ready, hh_made, hl_made = (sem(n) for n in ("rows_made", "ht_ready", "hh_made", "hl_made"))
        tile_ready, tile_moved = sem("tile_ready"), sem("tile_moved")
        wff_hi, wff_lo, ff_ready, absz_made, softplus_made, logf_made, cum_made = (
            sem(n) for n in ("wff_hi", "wff_lo", "ff_ready", "absz_made", "softplus_made", "logf_made", "cum_made"))
        tok_ready, tok_moved, lft_ready, lfsum_zeroed, lfsum_made, suffix_ready, suffix_made = (
            sem(n) for n in ("tok_ready", "tok_moved", "lft_ready", "lfsum_zeroed", "lfsum_made", "suffix_ready",
                             "suffix_made"))
        logft_ready, logft_moved, convlast_made = sem("logft_ready"), sem("logft_moved"), sem("convlast_made")
        kv_stored, stored = sem("kv_stored"), sem("stored")
        ps_ready, pnb_made, pexp_made, pnorm_made, ppt_ready, ppt_moved, py_ready, py_moved = (
            sem(n) for n in ("ps_ready", "pnb_made", "pexp_made", "pnorm_made", "ppt_ready", "ppt_moved", "py_ready",
                             "py_moved"))
        newbias_zeroed, newbias_made, q_built, bias_built = (
            sem(n) for n in ("newbias_zeroed", "newbias_made", "q_built", "bias_built"))
        k_in = [sem(f"k_in{i}") for i in range(2)]
        v_in = [sem(f"v_in{i}") for i in range(4)]
        v_read, s_ready, stats_made, exp_made, inv_made = (
            sem(n) for n in ("v_read", "s_ready", "stats_made", "exp_made", "inv_made"))
        t_ready, moved_a, moved_v, pv_ready, yrow_made, yt_ready, yt_moved = (
            sem(n) for n in ("t_ready", "moved_a", "moved_v", "pv_ready", "yrow_made", "yt_ready", "yt_moved"))
        mixh_made, mixl_made = sem("mixh_made"), sem("mixl_made")
        outa_moved, outv_moved, back_ready = (
            sem(n) for n in ("outa_moved", "outv_moved", "back_ready"))
        ln_in, var_made, std_made, stat_made, normed, gain_made, scaled = (
            sem(n) for n in ("ln_in", "var_made", "std_made", "stat_made", "normed", "gain_made", "scaled"))
        fflast_zeroed, tap_made, gate_made, actf_made, acth_made, actl_made, last_kept, fflast_made = (
            sem(n) for n in ("fflast_zeroed", "tap_made", "gate_made", "actf_made", "acth_made", "actl_made",
                             "last_kept", "fflast_made"))
        dve_step, pool_step, act_step, dve_misc = (sem(n) for n in ("dve_step", "pool_step", "act_step", "dve_misc"))
        ext_moved, past_in, conv_made = sem("ext_moved"), sem("past_in"), sem("conv_made")

        w_ada, w_in, w_o, w_up, w_down = (a[n].rearrange("l r c -> (l r) c").rearrange("(k p) c -> p k c", p=P)
                                          for n in ("w_ada", "w_in", "w_o", "w_up", "w_down"))
        in_at = [P * t + (HEADS if t >= 15 else 0) for t in range(N_PROJ)]

        def raw_k(c):
            return raw[c.raw][:, :].rearrange("p (k c) -> p k c", k=KD)

        def hi_lo(c):
            return (w[c.slot][:, :].rearrange("p (k c) -> p k c", k=KD) for w in (w_h, w_l))

        block = ctx.enter_context(nc.Block())

        @block.sync
        def _(sp):
            sp.dma_start(c_rows[0:1, :], a["c_prompt"]).then_inc(c_in, 16)
            sp.dma_start(c_rows[1:9, :], a["c_sample"]).then_inc(c_in, 16)
            sp.dma_start(const[:, 0:C_EARLY], a["const"][:, 0:C_EARLY]).then_inc(const_in, 16)
            sp.wait_ge(bias_zeroed, 1)

            def slot_free(c):
                after(sp, lo_made, c.n - 3)

            def load_ada(d):
                c = d.chunk
                slot_free(c)
                for k in (0, 4):
                    sp.dma_start(raw_k(c)[:, k:k + 4, :],
                                 w_ada[:, k:k + 4, d.column:d.column + CH]).then_inc(raw_in[c.raw], 16)
                after(sp, ada_made, d.a - 3)
                sp.dma_start(b_ada[d.a % 4][0:9, :], a["b_ada"][:, d.column:d.column + CH].to_broadcast([9, CH]))\
                    .then_inc(bias_in[d.a % 4], 16)

            for d in ADA1[:6]:
                load_ada(d)
            sp.dma_start(xt[:, 0:2, :], a["x_prompt"].rearrange("g (t p) d -> p (g t) d", p=P)).then_inc(x_in, 16)
            sp.dma_start(xt[0:TSA, 2, :], a["x_sample"].rearrange("b t d -> (b t) d")).then_inc(x_in, 16)
            for d in ADA1[6:]:
                load_ada(d)

            def other_loads():
                sp.dma_start(const[:, C_EARLY:C_ALL], a["const"][:, C_EARLY:C_ALL]).then_inc(tables_in, 16)
                sp.wait_ge(state_zeroed, 1)
                for g in range(4):
                    for at, n, src in ((0, 16, a["state_ffn"].rearrange("l b r (t g j) -> g (l b r) t j", g=4, j=32)),
                                       (16, 3, a["ffn_conv_w"].rearrange("l w (t g j) -> g (l w) t j", g=4, j=32)),
                                       (19, 1, a["ffn_conv_b"].rearrange("l (t g j) -> g l t j", g=4, j=32))):
                        sp.dma_start(state_raw[32 * g + at:32 * g + at + n, 0:44, :], src[g]).then_inc(state_in, 16)
                    for at, n, src in ((0, 16, a["state_conv"].rearrange("l b r (t g j) -> g (l b r) t j", g=4, j=32)),
                                       (16, 3, a["conv_w"].rearrange("l w (t g j) -> g (l w) t j", g=4, j=32))):
                        sp.dma_start(state_raw[32 * g + at:32 * g + at + n, 44:46, :], src[g]).then_inc(state_in, 16)

            some = -(-SEQS * PAGES // (N_IN - 3))
            for j in range(N_IN):
                c = Chunk(AT_IN, 0, j)
                slot_free(c)
                for m in range(2):
                    at = in_at[2 * j + m]
                    sp.dma_start(raw_k(c)[:, :, m * P:m * P + P], w_in[:, :, at:at + P]).then_inc(raw_in[c.raw], 16)
                if j == 0:
                    sp.dma_start(b_f[:, :], a["b_f"].rearrange("l h -> h l")).then_inc(small_in, 16)
                    sp.dma_start(pages[:, :], a["page_table"].rearrange("b (o p) -> o (b p)", o=1))\
                        .then_inc(small_in, 16)
                    sp.dma_start(wff[:, :, :], w_in[:, :, 15 * P:15 * P + HEADS]).then_inc(small_in, 16)
                if j == 2:
                    other_loads()
                    sp.wait_ge(small_in, 48)
                for n in range(some * max(j - 3, 0), min(some * max(j - 2, 0), SEQS * PAGES)):
                    page = sp.value_load(pages[0:1, n:n + 1], min_val=0, max_val=POOL - 1)
                    sp.dma_start(lf_rows[n:n + 1, :], a["cache_fox_logf"][0, bass.ds(page, 1)]
                                 .rearrange("o s h -> o (s h)")).then_inc(lf_in, 16)

            caches = [(a["cache_fox_k"], a["cache_fox_v"]), (a["cache_moba_k"], a["cache_moba_v"])]

            def page_numbers(bp):
                return [[sp.value_load(pages[0:1, bass.ds(bp * (2 * PAGES) + (par * PAGES + page), 1)],
                                       min_val=0, max_val=POOL - 1) for page in range(PAGES)] for par in range(2)]

            def page_of(cache, number):
                return cache[0, bass.ds(number, 1)].rearrange("o s h d -> (o s) (h d)")

            def load_k(bp, kind, numbers):
                u = bp * 2 + kind
                for par in range(2):
                    if u:
                        sp.wait_ge(t_ready, u * 15 - 12 + 6 * par if u > 1 else 6 * par + 6)
                    for page in range(PAGES):
                        sp.dma_start(k_pages[par][:, page, :],
                                     page_of(caches[kind][0], numbers[par][page])).then_inc(k_in[par], 16)

            def load_v(bp, kind, numbers):
                u = bp * 2 + kind
                for g in range(4):
                    after(sp, v_read, u * 4 + (g - 3))
                    for page in (2 * g, 2 * g + 1):
                        for par in range(2):
                            sp.dma_start(v_pages[:, par, page, :],
                                         page_of(caches[kind][1], numbers[par][page])).then_inc(v_in[g], 16)

            def store_new():
                sp.wait_ge(tok_moved, 12)
                for src, kind, po, so in ((v_tok, 0, "fv_p", "fv_s"), (v_tok, 1, "mv_p", "mv_s"),
                                             (k_tok, 0, "fk_p", "fk_s"), (k_tok, 1, "mk_p", "mk_s")):
                    sp.dma_start(o[po].rearrange("l g (t p) h d -> p (l g t) (h d)", p=P),
                                  src[:, kind, 0:2, :]).then_inc(kv_stored, 16)
                    sp.dma_start(o[so].rearrange("l b t h d -> (l b t) (h d)"), src[0:TSA, kind, 2, :])\
                        .then_inc(kv_stored, 16)
                sp.wait_ge(logft_moved, 1)
                for tt in range(2):
                    sp.dma_start(o["lf_p"][0, 0, tt * P:tt * P + P, :], lf_out[:, tt, :]).then_inc(stored, 16)
                sp.dma_start(o["lf_s"].rearrange("l b t h -> (l b t) h"), lf_out[0:TSA, 2, :]).then_inc(stored, 16)

            def store_conv():
                sp.wait_ge(convlast_made, 1)
                for g in range(4):
                    for at, n, dst in ((0, 16, o["conv_s"]), (16, 2, o["conv_p"])):
                        sp.dma_start(dst.rearrange("l b r (t g j) -> g (l b r) t j", g=4, j=32)[g],
                                      conv_last_t[32 * g + at:32 * g + at + n, :, :]).then_inc(stored, 16)

            for d in ADA2[:5]:
                load_ada(d)
            store_new()
            for d in ADA2[5:8]:
                load_ada(d)
            store_conv()
            for d in ADA2[8:]:
                load_ada(d)
            numbers = page_numbers(0)
            sp.wait_ge(ht_ready, BLK)
            sp.wait_ge(kv_stored, 16 * 8)
            load_v(0, 0, numbers)
            sp.wait_ge(w_used, AT_O)
            load_k(0, 0, numbers)
            load_k(0, 1, numbers)
            for bp in range(1, BP):
                before, numbers = numbers, page_numbers(bp)
                load_k(bp, 0, numbers)
                load_v(bp - 1, 1, before)
                load_k(bp, 1, numbers)
                load_v(bp, 0, numbers)
            load_v(BP - 1, 1, numbers)

            def load_rows(w):
                def load(c):
                    slot_free(c)
                    for kk in range(2):
                        sp.dma_start(raw[c.raw][:, kk * D:kk * D + D],
                                     w[:, bass.ds(c.j * 2 + kk, 1), :].rearrange("p o c -> p (o c)"))\
                            .then_inc(raw_in[c.raw], 16)
                return load

            for k in range(N_O):
                if k == 2:
                    sp.wait_ge(t_ready, 15 * (2 * BP - 1) + 9)
                load_rows(w_o)(Chunk(AT_O, 0, k))
            sp.wait_ge(v_read, 8 * BP)
            sp.dma_start(ln_gb1[:, 0, :], a["ln1_g"].to_broadcast([P, D])).then_inc(ln_in, 16)
            sp.dma_start(ln_gb1[:, 1, :], a["ln1_b"].to_broadcast([P, D])).then_inc(ln_in, 16)

            def load_up(c):
                slot_free(c)
                for m in range(2):
                    sp.dma_start(raw_k(c)[:, :, m * P:m * P + P],
                                 w_up[:, :, bass.ds(c.j * P + m * DFF, P)]).then_inc(raw_in[c.raw], 16)

            ring(sp, AT_UP, N_UP, load_up)
            sp.wait_ge(hl_made, BLK + 6)
            sp.dma_start(ln_gb2[:, 0, :], a["ln2_g"].to_broadcast([P, D])).then_inc(ln_in, 16)
            sp.dma_start(ln_gb2[:, 1, :], a["ln2_b"].to_broadcast([P, D])).then_inc(ln_in, 16)
            ring(sp, AT_DOWN, N_DOWN, load_rows(w_down))
            sp.wait_ge(fflast_made, 1)
            for g in range(4):
                for at, n, dst in ((0, 16, o["ffn_s"]), (16, 2, o["ffn_p"])):
                    sp.dma_start(dst.rearrange("l b r (t g j) -> g (l b r) t j", g=4, j=32)[g],
                                 ff_last_t[32 * g + at:32 * g + at + n, :, :]).then_inc(stored, 16)
            sp.wait_ge(scaled, 6)
            sp.dma_start(o["y_p"].rearrange("g (t p) d -> p (g t) d", p=P), xt[:, 0:2, :]).then_inc(stored, 16)
            sp.dma_start(o["y_s"].rearrange("b t d -> (b t) d"), xt[0:TSA, 2, :]).then_inc(stored, 16)
            sp.wait_ge(stored, 16 * (3 + 8 + 8 + 2))
            sp.wait_ge(kv_stored, 16 * 8)

        @block.tensor
        def _(pe):
            mm = pe.matmul

            def product(out, lhs, rhs, start, stop):
                mm(out, lhs[0], rhs[0], start=start, stop=False)
                mm(out, lhs[0], rhs[1], start=False, stop=False)
                return mm(out, lhs[1], rhs[0], start=False, stop=stop)

            pe.wait_ge(const_in, 16)
            pe.wait_ge(silu_made, 1)
            for k in range(KD):
                t = pe.transpose(ps[:, 6, 9 * k:9 * k + 9], c_silu[:, k * P:k * P + P], ident[0:9, 0:9])
            t.then_inc(ct_ready, 1)
            pe.wait_ge(ch_lo, 1)

            def ada(d):
                c = d.chunk
                pe.wait_ge(lo_made, c.n + 1)
                after(pe, ada_made, d.a + 1 - d.back)
                out = ps[0:18, d.bank, 0:CH]
                hi, lo = hi_lo(c)
                for k in range(KD):
                    mm(out, ch[:, k, :], hi[:, k, :], start=k == 0, stop=False)
                for k in range(KD):
                    t = mm(out, ch[:, k, :], lo[:, k, :], start=False, stop=k == KD - 1)
                t.then_inc(w_used, 1)

            def spread(d):
                pe.wait_ge(ada_made, d.a + 1)
                after(pe, mods_made, d.a + 1 - d.back)
                for m in range(2):
                    at = C_SELTOK + m * P
                    t = mm(ps[:, d.spread_bank, m * CH:m * CH + CH], const[0:18, at:at + P], ada_row[d.a % 2][:, :],
                           start=True, stop=True)
                t.then_inc(ex_ready, 1)

            def block_to_features(b):
                pe.wait_ge(rows_made, b + 1)
                after(pe, hl_made, b - 1)
                for kk in range(2):
                    k = 2 * b + kk
                    for tt in range(3):
                        t = pe.transpose(ps[:, 4 + k % 4, tt * P:tt * P + NT[tt]],
                                         rows[0:NT[tt], tt, k * P:k * P + P], ident[0:NT[tt], 0:NT[tt]])
                t.then_inc(ht_ready, 1)

            for d in ADA1:
                ada(d)
                if d.a:
                    spread(ADA1[d.a - 1])
                if d.a % 2 and d.a >= 3:
                    block_to_features((d.a - 3) // 2)
            spread(ADA1[-1])
            block_to_features(BLK - 1)

            def to_features():
                for tt in range(3):
                    pe.wait_ge(rows_made, BLK + tt + 1)
                    for half in range(2):
                        for k in range(4):
                            kk = 4 * half + k
                            t = pe.transpose(ps[:, 2 * tt + half, k * P:k * P + NT[tt]],
                                             ln_rows[0:NT[tt], tt, kk * P:kk * P + P], ident[0:NT[tt], 0:NT[tt]])
                        t.then_inc(ht_ready, 1)

            h = (h_h, h_l)

            def product_tiles(c, bank, count_before):
                hi, lo = hi_lo(c)
                for m in range(2):
                    after(pe, tile_moved, c.j * 2 + (count_before + m - 7))
                    for k in range(KD):
                        t = product(ps[:, bank + m, 0:TOK], [w[:, k, m * P:m * P + P] for w in (hi, lo)],
                                    [x[:, k, :] for x in h], k == 0, k == KD - 1)
                    t.then_inc(w_used if m else tile_ready, 1)

            pe.wait_ge(hl_made, BLK)

            def in_step(c):
                pe.wait_ge(lo_made, c.n + 1)
                product_tiles(c, 2 * c.raw, 0)
            ring(pe, AT_IN, N_IN, in_step)
            pe.wait_ge(wff_lo, 1)
            pe.wait_ge(tile_moved, N_PROJ)
            for k in range(KD):
                t = product(ps[0:HEADS, 0, 0:TOK], [wff_h[:, k, :], wff_l[:, k, :]], [x[:, k, :] for x in h],
                            k == 0, k == KD - 1)
            t.then_inc(ff_ready, 1)

            for n, (at, tt) in enumerate((at, tt) for at in (FV, MV, FK, MK) for tt in range(3)):
                after(pe, tok_moved, n - 3)
                for p in range(PAIRS):
                    t = pe.transpose(ps[0:NT[tt], 4 + n % 4, p * P:p * P + P],
                                     proj[:, at + p, tt * P:tt * P + NT[tt]], ident)
                t.then_inc(tok_ready, 1)
            pe.wait_ge(tables_in, 16)
            pe.wait_ge(lf_in, 16 * SEQS * PAGES)
            for hh in range(HEADS):
                t = pe.transpose(ps[:, 1, 64 * hh:64 * hh + 64], lf_rows[:, hh:PAGE * HEADS:HEADS], ident[0:64, 0:64])
            t.then_inc(lft_ready, 1)
            pe.wait_ge(logf_made, 1)
            for tt in range(3):
                t = pe.transpose(ps[0:NT[tt], 2, 8 * tt:8 * tt + HEADS], forget[:, 1, tt * P:tt * P + NT[tt]],
                                 ident[0:HEADS, 0:HEADS])
            t.then_inc(logft_ready, 1)
            pe.wait_ge(lfsum_made, 1)
            for bp in range(BP):
                out = ps[:, 3, bp * P:bp * P + P]
                flat = [lf_sum[:, n, 2 * bp:2 * bp + 2, :].rearrange("p b c -> p (b c)") for n in range(2)]
                mm(out, flat[0], const[:, C_TRI:C_TRI + P], start=True, stop=False)
                t = mm(out, flat[1], const[:, C_ONES:C_ONES + P], start=False, stop=True)
            t.then_inc(suffix_ready, 1)

            pe.wait_ge(cum_made, 1)
            pe.wait_ge(tok_moved, 12)
            pe.wait_ge(suffix_made, 1)
            pe.wait_ge(logft_moved, 1)

            def prompt_scores(n):
                kind, hh = n // HEADS, n % HEADS
                q, k = ((FQ, FK), (MQ, MK))[kind]
                r = slice(HD * (hh % 2), HD * (hh % 2) + HD)
                for qt, at in ((0, 0), (1, P)):
                    keys = P * (qt + 1)
                    out = ps[:, n % 2, at:at + keys]
                    t = mm(out, proj[r, q + hh // 2, qt * P:qt * P + P], proj[r, k + hh // 2, 0:keys],
                           start=True, stop=kind == 1)
                    if kind == 0:
                        t = mm(out, const[0:HEADS, C_IDENT + hh:C_IDENT + hh + 1].to_broadcast([HEADS, P]),
                               ncum[:, 0:keys], start=False, stop=True)
                t.then_inc(ps_ready, 1)

            def with_ada(chunks):
                for i in chunks:
                    ada(ADA2[i])
                    if i:
                        spread(ADA2[i - 1])

            prompt_scores(0)
            for n in range(2 * HEADS):
                kind, hh = n // HEADS, n % HEADS
                if n + 1 < 2 * HEADS:
                    prompt_scores(n + 1)
                with_ada(WITH_HEAD[n][:1])
                pe.wait_ge(pnorm_made, n + 1)
                after(pe, ppt_moved, n - 1)
                base = 384 * (n % 2)
                for b, at in enumerate((0, P, 2 * P)):
                    t = pe.transpose(ps[:, 2 + n % 2, b * P:b * P + P], probs[:, base + at:base + at + P], ident)
                t.then_inc(ppt_ready, 1)
                with_ada(WITH_HEAD[n][1:])
                pe.wait_ge(ppt_moved, n + 1)
                if hh % 2 == 0:
                    after(pe, py_moved, n // 2 - 1)
                bank, r = 4 + 3 * ((n // 2) % 2), HD * (hh % 2)
                pt = probs_t[:, 3 * (n % 2):3 * (n % 2) + 3, :]
                mm(ps[r:r + HD, bank, 0:TP], v_tok[:, kind, 0, HD * hh:HD * hh + HD],
                   pt[:, 0:2, :].rearrange("p a b -> p (a b)"), start=True, stop=True)
                t = mm(ps[r:r + HD, bank, P:TP], v_tok[:, kind, 1, HD * hh:HD * hh + HD], pt[:, 2, :],
                       start=False, stop=True, skip_group_check=True)
                if hh % 2:
                    t.then_inc(py_ready, 1)

            def move_free(stage, position):
                if position >= 3 and stage is not None:
                    e = EVACS[position - 3]
                    pe.wait_ge(moved_a if e == "A" else moved_v, evacs(stage, position - 3, e))
                elif stage is not None:
                    for e, s in (("A", moved_a), ("V", moved_v)):
                        pe.wait_ge(s, stage * PER[e] + BEFORE[e])

            def first_free(position):
                if position >= 3:
                    e = EVACS[position - 3]
                    pe.wait_ge(moved_a if e == "A" else moved_v, EVACS[:position - 2].count(e))

            def transpose_k(stage, u):
                position = 0
                for par in range(2):
                    pe.wait_ge(k_in[par], u * (16 * PAGES) + 16 * PAGES)
                    for p in range(PAIRS):
                        for half in range(2):
                            if stage is None:
                                first_free(position)
                            else:
                                move_free(stage, position)
                            for g in range(4):
                                t = pe.transpose(ps[:, 3 + position % 3, g * P:g * P + P],
                                                 k_pages[par][:, 4 * half + g, p * P:p * P + P], ident)
                            t.then_inc(t_ready, 1)
                            position += 1

            def scores(bp, kind, u):
                pe.wait_ge(q_built, u + 1)
                if kind == 0:
                    pe.wait_ge(bias_built, bp + 1)
                pe.wait_ge(moved_a, u * PER["A"] + BEFORE["A"])
                pe.wait_ge(moved_v, u * PER["V"] + BEFORE["V"])
                knew = (FK, MK)[kind]
                q = qblk[kind][:, :, :, :].rearrange("p a b c -> p (a b c)")
                for c in range(3):
                    for p in range(PAIRS):
                        for par in range(2):
                            out = ps[64 * par:64 * par + 64, c, 0:512 if c < 2 else TSA]
                            keys = k_t[:, par, p, c * 512:c * 512 + 512] if c < 2 else proj[:, knew + p, TP:TOK]
                            t = mm(out, q[:, 192 * par + 48 * p:192 * par + 48 * p + 64], keys,
                                   start=p == 0, stop=p == PAIRS - 1 and kind == 1)
                    if kind == 0:
                        for par in range(2):
                            out = ps[64 * par:64 * par + 64, c, 0:512 if c < 2 else TSA]
                            t = mm(out, selb[par], bias_r[:, c * 512:c * 512 + (512 if c < 2 else TSA)],
                                   start=False, stop=True)
                t.then_inc(s_ready, 1)

            def transpose_p(stage, u, last):
                pe.wait_ge(exp_made, u + 1)
                for position in (12, 13, 14):
                    bank = 3 + position % 3
                    if position < 14:
                        move_free(stage, position - 12 if last else position)
                        for g in range(4):
                            at = (4 * (position - 12) + g) * P
                            if position == 13 and g == 3:
                                move_free(stage, 2 if last else 14)
                            t = pe.transpose(ps[:, bank, g * P:g * P + P], probs[:, at:at + P], ident)
                    else:
                        t = pe.transpose(ps[0:TSA, bank, 0:P], probs[:, PAST:PAST + TSA], ident)
                    t.then_inc(t_ready, 1)

            def values(stage, kind, u, last):
                if last:
                    pe.wait_ge(moved_a, stage * PER["A"] + BEFORE["A"] + 1)
                    pe.wait_ge(moved_v, stage * PER["V"] + BEFORE["V"] + 2)
                else:
                    pe.wait_ge(moved_a, evacs(stage, 14, "A"))
                    pe.wait_ge(moved_v, evacs(stage, 14, "V"))
                if not (isinstance(u, int) and u == 0):
                    pe.wait_ge(yrow_made, u)
                for page in range(PAGES):
                    if page % 2 == 0:
                        pe.wait_ge(v_in[page // 2], u * 64 + 64)
                    for par in range(2):
                        t = mm(ps[64 * par:64 * par + 64, 6, 0:AW], probs_t[:, page, 64 * par:64 * par + 64],
                               v_pages[:, par, page, :], start=page == 0, stop=False)
                    if page % 2:
                        t.then_inc(v_read, 1)
                for par in range(2):
                    t = mm(ps[64 * par:64 * par + 64, 6, 0:AW], probs_t[0:TSA, PAGES, 64 * par:64 * par + 64],
                           v_tok[0:TSA, kind, 2, :], start=False, stop=True)
                t.then_inc(pv_ready, 1)

            def transpose_y(u):
                pe.wait_ge(yrow_made, u + 1)
                after(pe, yt_moved, u)
                for p in range(PAIRS):
                    t = pe.transpose(ps[:, 7, ROWS * p:ROWS * p + ROWS], y_row[0:ROWS, p * P:p * P + P],
                                     ident[0:ROWS, 0:ROWS])
                t.then_inc(yt_ready, 1)

            selb = [const[:, C_SELB + 64 * par:C_SELB + 64 * par + 64] for par in range(2)]
            spread(ADA2[-1])
            pe.wait_ge(py_moved, HEADS)
            pe.wait_ge(mods_made, N_ADA1 + N_ADA2)
            transpose_k(None, 0)

            def units(bp, first, last):
                for kind in range(2):
                    u = bp * 2 + kind
                    scores(bp, kind, u)
                    if not (first and kind == 0):
                        transpose_y(u - 1)
                    end = last and kind == 1
                    if not end:
                        transpose_k(u, u + 1)
                    transpose_p(u, u, end)
                    values(u, kind, u, end)

            units(0, True, False)
            with pe.Fori(1, BP - 1) as bp:
                units(bp, False, False)
            units(BP - 1, False, True)
            transpose_y(2 * BP - 1)

            def project_step(c, x, k_of, start, stop):
                pe.wait_ge(lo_made, c.n + 1)
                for kk in range(2):
                    for m in range(KD):
                        at = kk * D + m * P
                        t = product(ps[:, m, 0:TOK], [w[c.slot][:, at:at + P] for w in (w_h, w_l)],
                                    [y[:, bass.ds(k_of + kk, 1), :].rearrange("p o t -> p (o t)") for y in x],
                                    start and kk == 0, stop and kk == 1)
                t.then_inc(w_used, 1)

            def back_to_tokens(n):
                pe.wait_ge(outa_moved, 4 * n + 4)
                pe.wait_ge(outv_moved, 4 * n + 4)
                for tt in range(3):
                    for k in range(KD):
                        t = pe.transpose(ps[0:NT[tt], 2 * tt + k // 4, (k % 4) * P:(k % 4) * P + P],
                                         y_t[:, k, tt * P:tt * P + NT[tt]], ident)
                    t.then_inc(back_ready, 1)

            pe.wait_ge(mixl_made, 3)
            pe.wait_ge(yt_moved, 2 * BP)
            for k in range(N_O):
                project_step(Chunk(AT_O, 0, k), (h_h, h_l), 2 * k, k == 0, k == N_O - 1)
            back_to_tokens(0)
            to_features()

            pe.wait_ge(hl_made, BLK + 6)

            def up_step(c):
                pe.wait_ge(lo_made, c.n + 1)
                product_tiles(c, 2 * c.raw, N_PROJ)
            ring(pe, AT_UP, N_UP, up_step)
            pe.wait_ge(tile_moved, N_PROJ + 2 * N_UP)
            pe.wait_ge(actl_made, FT)
            x = (act_h, act_l)
            project_step(Chunk(AT_DOWN, 0, 0), x, 0, True, False)
            with pe.Fori(0, N_DOWN // 2 - 1) as i:
                for k in (1, 2):
                    c = Chunk(AT_DOWN, 0, k)
                    c.n = i * 2 + (AT_DOWN + k)
                    project_step(c, x, i * 4 + 2 * k, False, False)
            for k in (N_DOWN - 2, N_DOWN - 1):
                project_step(Chunk(AT_DOWN, 0, k), x, 2 * k, False, k == N_DOWN - 1)
            back_to_tokens(1)

        @block.scalar
        def _(act):
            cp = ACT.Copy
            do = act.activation

            def round_hi(c, n):
                act.wait_ge(raw_in[c.raw], c.loads * 32)
                after(act, w_used, c.n - 1)
                do(w_h[c.slot][:, 0:n], raw[c.raw][:, 0:n], cp).then_inc(hi_made, 1)

            act.wait_ge(c_in, 32)
            do(c_silu[:, :], c_rows[:, :], ACT.Silu).then_inc(silu_made, 1)
            act.wait_ge(ct_copied, 1)
            ct3 = c_t[:, :].rearrange("p (k b) -> p k b", k=KD)
            do(ch[:, :, 0:9], ct3, cp).then_inc(ch_hi, 1)

            def ada_mods(d):
                act.wait_ge(ex_ready, d.a + 1)
                do(mods[:, d.part, :, d.block * CH:d.block * CH + CH],
                   ps[:, d.spread_bank, :].rearrange("p (a c) -> p a c", a=2), cp,
                   bias=0.0 if d.part in (SH_A, SH_F) else 1.0).then_inc(mods_made, 1)

            def block_hi(b):
                act.wait_ge(ht_ready, b + 1)
                do(h_h[:, 2 * b:2 * b + 2, :], ps[:, 4 + 2 * b % 4:6 + 2 * b % 4, 0:TOK], cp).then_inc(hh_made, 1)

            for d in ADA1:
                round_hi(d.chunk, KD * CH)
                if d.a >= 2:
                    ada_mods(ADA1[d.a - 2])
                if d.a % 2 == 0 and d.a >= 4:
                    block_hi((d.a - 4) // 2)
            ada_mods(ADA1[-2])
            ada_mods(ADA1[-1])
            round_hi(Chunk(AT_IN, 0, 0), KD * CH)
            block_hi(BLK - 2)
            block_hi(BLK - 1)

            def features_hi():
                for tt in range(3):
                    for half in range(2):
                        act.wait_ge(ht_ready, BLK + 2 * tt + half + 1)
                        do(h_h[:, 4 * half:4 * half + 4, tt * P:tt * P + NT[tt]],
                           ps[:, 2 * tt + half, :].rearrange("p (k t) -> p k t", k=4)[:, :, 0:NT[tt]],
                           cp).then_inc(hh_made, 1)

            act.wait_ge(small_in, 48)
            do(wff_h[:, :, :], wff[:, :, :], cp).then_inc(wff_hi, 1)

            def move_tiles(c, bank):
                for m in range(2):
                    act.wait_ge(w_used if m else tile_ready, c.n + 1 if m else c.j + 1)
                    do(proj[:, bass.ds(c.j * 2 + m, 1), :].rearrange("p o t -> p (o t)"),
                       ps[:, bank + m, 0:TOK], cp).then_inc(tile_moved, 1)

            def in_step(c):
                if not (isinstance(c.j, int) and c.j == 0):
                    round_hi(c, KD * CH)
                    move_tiles(c.before(), 2 * c.before().raw)
            ring(act, AT_IN, N_IN, in_step)
            last = Chunk(AT_IN, N_IN // 4 - 1, 3)
            move_tiles(last, 2 * last.raw)
            round_hi(ADA2[0].chunk, KD * CH)

            act.wait_ge(absz_made, 1)
            do(forget[:, 2, :], forget[:, 1, :], ACT.Exp, scale=-1.0).then_inc(act_step, 1)
            act.wait_ge(act_step, 1)
            do(forget[:, 3, :], forget[:, 2, :], ACT.Ln, bias=1.0).then_inc(softplus_made, 1)

            for n, (kv, tt) in enumerate((kv, tt) for kv in ((v_tok, 0), (v_tok, 1), (k_tok, 0), (k_tok, 1))
                                         for tt in range(3)):
                act.wait_ge(tok_ready, n + 1)
                do(kv[0][0:NT[tt], kv[1], tt, :], ps[0:NT[tt], 4 + n % 4, 0:AW], cp).then_inc(tok_moved, 1)
            def prompt_exp(n):
                act.wait_ge(pnb_made, n + 1)
                after(act, ppt_ready, n - 1)
                for qt, at, w in ((0, 0, P), (1, P, TP)):
                    t = do(probs[:, 384 * (n % 2) + at:384 * (n % 2) + at + w], ps[:, n % 2, at:at + w], ACT.Exp,
                           bias=p_nb[:, n, qt:qt + 1], scale=SCALE, accum_out=p_sum[:, n, qt:qt + 1])
                t.then_inc(pexp_made, 1)

            def next_hi(chunks):
                for i in chunks:
                    if i + 1 < N_ADA2:
                        round_hi(ADA2[i + 1].chunk, KD * CH)

            prompt_exp(0)
            for n in range(2 * HEADS):
                next_hi(WITH_HEAD[n][:1])
                if n + 1 < 2 * HEADS:
                    prompt_exp(n + 1)
                act.wait_ge(ppt_ready, n + 1)
                do(probs_t[:, 3 * (n % 2):3 * (n % 2) + 3, :],
                   ps[:, 2 + n % 2, 0:384].rearrange("p (b q) -> p b q", b=3), cp).then_inc(ppt_moved, 1)
                next_hi(WITH_HEAD[n][1:])
                for i in WITH_HEAD[n]:
                    if i:
                        ada_mods(ADA2[i - 1])
                if n % 2:
                    act.wait_ge(py_ready, n // 2 + 1)
                    q = (FQ, MQ)[n // HEADS] + (n % HEADS) // 2
                    do(proj[:, q, 0:TP], ps[:, 4 + 3 * ((n // 2) % 2), 0:TP], cp).then_inc(py_moved, 1)

            def move(position, stage_ready):
                act.wait_ge(t_ready, stage_ready)
                bank = 3 + position % 3
                if position < 12:
                    par, p, half = position // 6, position % 6 // 2, position % 2
                    do(k_t[:, par, p, 512 * half:512 * half + 512], ps[:, bank, :], cp).then_inc(moved_a, 1)
                else:
                    g = 4 * (position - 12)
                    do(probs_t[:, g:g + 4, :], ps[:, bank, :].rearrange("p (g r) -> p g r", g=4), cp)\
                        .then_inc(moved_a, 1)

            ada_mods(ADA2[-1])
            for position in range(12):
                if EVACS[position] == "A":
                    move(position, position + 1)

            def unit_exp(kind, u):
                act.wait_ge(stats_made, u + 1)
                if kind == 0:
                    do(probs[:, :], psf[:, 0:PAST + TSA], ACT.Exp, bias=u_nb[:, 0:1], scale=SCALE,
                       accum_out=u_sum[:, 0:1]).then_inc(exp_made, 1)
                else:
                    for b in range(NBLK + 1):
                        at = slice(MBLK * b, min(MBLK * (b + 1), PAST + TSA))
                        t = do(probs[:, at], probs[:, at], ACT.Exp, bias=u_nb[:, b:b + 1], scale=SCALE,
                               accum_out=u_sum[:, b:b + 1])
                    t.then_inc(exp_made, 1)

            def unit(kind, u, last):
                base = u * 15 + (12 + 1)
                if not last:
                    for position in range(6):
                        move(position, base + position)
                unit_exp(kind, u)
                if not last:
                    move(8, base + 8)
                    move(10, base + 10)
                move(13, base + (1 if last else 13))
                act.wait_ge(pv_ready, u + 1)
                act.wait_ge(inv_made, u + 1)
                do(y_row[:, :], ps[:, 6, 0:AW], cp, scale=u_inv[:, 0:1]).then_inc(yrow_made, 1)

            unit(0, 0, False)
            unit(1, 1, False)
            with act.Fori(1, BP - 1) as bp:
                unit(0, bp * 2, False)
                unit(1, bp * 2 + 1, False)
            unit(0, 2 * BP - 2, False)
            unit(1, 2 * BP - 1, True)

            act.wait_ge(yt_moved, 2 * BP)
            for at, frm, n in ((0, CB, 2), (2, FQ, 3), (5, MQ, 3)):
                do(h_h[:, at:at + n, :], proj[:, frm:frm + n, :], cp).then_inc(mixh_made, 1)
            for k in range(N_O):
                round_hi(Chunk(AT_O, 0, k), 2 * D)

            def move_out(n):
                act.wait_ge(w_used, (AT_UP, AT_DOWN + N_DOWN)[n])
                for m in range(0, KD, 2):
                    do(y_t[:, m, :], ps[:, m, 0:TOK], cp).then_inc(outa_moved, 1)

            move_out(0)

            def norm(n):
                for tt in range(3):
                    act.wait_ge(var_made, 3 * n + tt + 1)
                    do(ln_mv[0:NT[tt], tt, 2:3], ln_mv[0:NT[tt], tt, 1:2], ACT.Sqrt).then_inc(std_made, 1)
                    act.wait_ge(stat_made, 3 * n + tt + 1)
                    r = slice(0, NT[tt])
                    do(xt[r, tt, :], ln_rows[r, tt, :], ACT.Identity, scale=ln_mv[r, tt, 2:3],
                       bias=ln_mv[r, tt, 3:4]).then_inc(normed, 1)

            norm(0)
            features_hi()

            def conv_in(c):
                e = ext[c.slot]
                after(act, conv_made, c.j - 1)
                after(act, last_kept, c.j - 1)
                for m in range(2):
                    act.wait_ge(w_used if m else tile_ready, c.n + 1 if m else c.j + (N_IN + 1))
                    bank = 2 * c.raw + m
                    do(e[:, m, 2:2 + TP], ps[:, bank, 0:TP], cp).then_inc(ext_moved, 1)
                    do(e[:, m, 258:338].rearrange("p (b t) -> p b t", b=SEQS)[:, :, 2:10],
                       ps[:, bank, TP:TOK].rearrange("p (b t) -> p b t", b=SEQS), cp).then_inc(tile_moved, 1)

            def first_tap(c):
                e = ext[c.slot]
                act.wait_ge(past_in, c.j + 1)
                act.wait_ge(tile_moved, c.j * 2 + (N_PROJ + 2))
                act.wait_ge(ext_moved, c.j * 2 + 2)
                after(act, actf_made, c.j)
                for m in range(2):
                    tile = st_t[:, bass.ds(c.j + m * FT, 1), :].rearrange("p o r -> p (o r)")
                    t = do(acc[:, m, :], e[:, m, 0:336], ACT.Identity, scale=tile[:, 16:17], bias=tile[:, 19:20])
                t.then_inc(tap_made, 1)

            def silu_gate(c):
                act.wait_ge(conv_made, c.j + 1)
                do(acc[:, 0, :], acc[:, 0, :], ACT.Silu).then_inc(gate_made, 1)

            def act_hi(c):
                act.wait_ge(actf_made, c.j + 1)
                do(act_h[:, bass.ds(c.j, 1), :].rearrange("p o t -> p (o t)"), act_f[:, :], cp).then_inc(acth_made, 1)

            def ffn_act(c):
                conv_in(c)
                if not isinstance(c.j, int) or c.j >= 1:
                    act_hi(c.before())
                first_tap(c)
                silu_gate(c)

            def up_step(c):
                round_hi(c, KD * CH)
                if not isinstance(c.j, int) or c.j >= 2:
                    ffn_act(c.before().before())
            ring(act, AT_UP, N_UP, up_step)
            last = Chunk(AT_UP, N_UP // 4, N_UP % 4 - 1)
            ffn_act(last.before())
            ffn_act(last)
            act_hi(last)
            ring(act, AT_DOWN, N_DOWN, lambda c: round_hi(c, 2 * D))
            move_out(1)
            norm(1)

        @block.vector
        def _(dve):
            chain = Chain(dve, dve_step)
            link = chain.link
            stt = dve.scalar_tensor_tensor

            def make_lo(c, n):
                dve.wait_ge(hi_made, c.n + 1)
                after(dve, w_used, c.n - 1)
                dve.tensor_sub(w_l[c.slot][:, 0:n], raw[c.raw][:, 0:n], w_h[c.slot][:, 0:n].bitcast(F32))\
                    .then_inc(lo_made, 1)

            dve.wait_ge(ct_ready, 1)
            dve.tensor_copy(c_t[:, :], ps[:, 6, 0:KD * 9]).then_inc(ct_copied, 1)
            ct3 = c_t[:, :].rearrange("p (k b) -> p k b", k=KD)
            dve.wait_ge(ct_copied, 1)
            dve.wait_ge(ch_hi, 1)
            dve.tensor_sub(ch[:, :, 9:18], ct3, ch[:, :, 0:9].bitcast(F32)).then_inc(ch_lo, 1)

            def ada_rows(d):
                dve.wait_ge(w_used, d.chunk.n + 1)
                dve.wait_ge(bias_in[d.a % 4], 16 * (d.a // 4 + 1))
                after(dve, ex_ready, d.a - 1)
                dve.tensor_add(ada_row[d.a % 2][:, :], ps[0:18, d.bank, 0:CH], b_ada[d.a % 4][:, :])\
                    .then_inc(ada_made, 1)

            def block_lo(b):
                dve.wait_ge(hh_made, b + 1)
                dve.tensor_sub(h_l[:, 2 * b:2 * b + 2, :], ps[:, 4 + 2 * b % 4:6 + 2 * b % 4, 0:TOK],
                               h_h[:, 2 * b:2 * b + 2, :].bitcast(F32)).then_inc(hl_made, 1)

            for d in ADA1:
                make_lo(d.chunk, KD * CH)
                if d.a:
                    ada_rows(ADA1[d.a - 1])
                if d.a % 2 == 0 and d.a >= 4:
                    block_lo((d.a - 4) // 2)
            ada_rows(ADA1[-1])
            make_lo(Chunk(AT_IN, 0, 0), KD * CH)
            block_lo(BLK - 2)
            block_lo(BLK - 1)

            def modulate(src, dst, tt, shift, scale):
                r = slice(0, NT[tt])
                link(dve.tensor_mul(dst[r, tt, :], mods[r, scale, PR[tt], :], src[r, tt, :]))
                dve.tensor_add(dst[r, tt, :], dst[r, tt, :], mods[r, shift, PR[tt], :]).then_inc(rows_made, 1)

            def features_lo():
                for tt in range(3):
                    for half in range(2):
                        dve.wait_ge(hh_made, BLK + 2 * tt + half + 1)
                        s = (slice(None), slice(4 * half, 4 * half + 4), slice(tt * P, tt * P + NT[tt]))
                        dve.tensor_sub(h_l[s], ps[:, 2 * tt + half, :].rearrange("p (k t) -> p k t", k=4)
                                       [:, :, 0:NT[tt]], h_h[s].bitcast(F32)).then_inc(hl_made, 1)

            dve.wait_ge(wff_hi, 1)
            dve.tensor_sub(wff_l[:, :, :], wff[:, :, :], wff_h[:, :, :].bitcast(F32)).then_inc(wff_lo, 1)
            for k in range(1, 4):
                make_lo(Chunk(AT_IN, 0, k), KD * CH)
            with dve.Fori(1, N_IN // 4) as i:
                for k in range(4):
                    make_lo(Chunk(AT_IN, i, k), KD * CH)
            make_lo(ADA2[0].chunk, KD * CH)
            dve.wait_ge(state_in, 16 * 4 * 5)
            dve.transpose(st_t[:, :, :], state_raw[:, :, :]).then_inc(dve_misc, 1)
            dve.wait_ge(tables_in, 16)
            dve.wait_ge(dve_misc, 1)

            dve.wait_ge(ff_ready, 1)
            link(dve.tensor_scalar(forget[:, 0, :], ps[0:HEADS, 0, 0:TOK], b_f[:, 0:1], None, ALU.add))
            stt(forget[:, 1, :], forget[:, 0, :], -1.0, forget[:, 0, :], ALU.mult, ALU.max).then_inc(absz_made, 1)
            dve.wait_ge(softplus_made, 1)
            stt(forget[:, 1, :], forget[:, 0, :], 0.0, forget[:, 3, :], ALU.min, ALU.subtract).then_inc(logf_made, 1)
            dve.wait_ge(logf_made, 1)
            link(dve.tensor_tensor_scan(forget[:, 2, :], const[0:HEADS, C_SCAN:C_SCAN + TOK], forget[:, 1, :], 0.0,
                                        ALU.mult, ALU.add))
            dve.tensor_scalar(ncum[:, :], forget[:, 2, :], -1.0 / SCALE, None, ALU.mult).then_inc(cum_made, 1)

            dve.wait_ge(lfsum_zeroed, 1)
            dve.wait_ge(lft_ready, 1)
            lf = [lf_sum[:, n, :, 0:PAGES * HEADS].rearrange("p b (g h) -> p b g h", h=HEADS) for n in range(2)]
            for hh in range(HEADS):
                t = dve.tensor_copy(lf[0][:, :, :, hh],
                                    ps[:, 1, 64 * hh:64 * hh + 64].rearrange("p (b g) -> p b g", g=PAGES))
            link(t)
            for g in range(PAGES - 2, -1, -1):
                t = dve.tensor_add(lf[1][:, :, g, :], lf[1][:, :, g + 1, :], lf[0][:, :, g + 1, :])
                if g:
                    link(t)
            t.then_inc(lfsum_made, 1)
            dve.wait_ge(logft_ready, 1)
            for tt in range(3):
                t = dve.tensor_copy(lf_out[0:NT[tt], tt, :], ps[0:NT[tt], 2, 8 * tt:8 * tt + HEADS])
            t.then_inc(logft_moved, 1)
            dve.wait_ge(suffix_ready, 1)
            dve.tensor_copy(c_suffix[:, :, :], ps[:, 3, :].rearrange("p (b s) -> p b s", b=BP))\
                .then_inc(suffix_made, 1)
            dve.wait_ge(newbias_zeroed, 1)
            for par in range(2):
                t = dve.tensor_copy(bias_r[64 * par:64 * par + HEADS, PAST:PAST + TSA], ncum[:, TP:TOK])
                t.then_inc(newbias_made, 1)

            def prompt_stats(n):
                kind, hh = n // HEADS, n % HEADS
                dve.wait_ge(ps_ready, n + 1)
                s = ps[:, n % 2, :]
                if kind == 0:
                    v = s[:, 0:384].rearrange("p (b k) -> p b k", b=3)[:, 0:3:2, :]
                    mask = const[:, C_DIAG:C_DIAG + P].unsqueeze(1).to_broadcast([P, 2, P])
                    link(dve.tensor_add(v, v, mask))
                else:
                    sl = float(slopes()[hh] / SCALE)
                    stt(s[:, 0:P], const[:, C_ALIBI + P:C_ALIBI + 2 * P], sl, s[:, 0:P], ALU.mult, ALU.add)
                    link(stt(s[:, P:3 * P], const[:, C_ALIBI:C_ALIBI + 2 * P], sl, s[:, P:3 * P], ALU.mult, ALU.add))
                dve.tensor_reduce(p_max[:, n, 0:1], s[:, 0:P], AX.X, ALU.max)
                link(dve.tensor_reduce(p_max[:, n, 1:2], s[:, P:3 * P], AX.X, ALU.max))
                dve.tensor_scalar(p_nb[:, n, :], p_max[:, n, :], -SCALE, None, ALU.mult).then_inc(pnb_made, 1)

            prompt_stats(0)

            u_s = u_ext[:, :, 258:338].rearrange("p c (b t) -> p c b t", b=SEQS)
            link(dve.memset(u_ext[:, :, 0:2], 0.0))
            for c in range(2):
                past = st_t[:, 44 + c, 0:16].rearrange("p (b r) -> p b r", r=2)
                dve.tensor_copy(u_s[:, c, :, 0:2], past)
                dve.tensor_mul(u_s[:, c, :, 2:10], proj[:, CC + c, TP:TOK].rearrange("p (b t) -> p b t", b=SEQS),
                               proj[:, CX + c, TP:TOK].rearrange("p (b t) -> p b t", b=SEQS))
                t = dve.tensor_mul(u_ext[:, c, 2:258], proj[:, CC + c, 0:TP], proj[:, CX + c, 0:TP])
            link(t)
            for c in range(2):
                link(dve.tensor_scalar(u_acc[:, c, :], u_ext[:, c, 0:336], st_t[:, 44 + c, 16:17], None, ALU.mult))
                for j in (1, 2):
                    link(stt(u_acc[:, c, :], u_ext[:, c, j:j + 336], st_t[:, 44 + c, 16 + j:17 + j], u_acc[:, c, :],
                             ALU.mult, ALU.add))
                dve.tensor_mul(proj[:, CB + c, 0:TP], proj[:, CB + c, 0:TP], u_acc[:, c, 0:TP])
                new = proj[:, CB + c, TP:TOK].rearrange("p (b t) -> p b t", b=SEQS)
                got = u_acc[:, c, 256:336].rearrange("p (b t) -> p b t", b=SEQS)[:, :, 2:10]
                dve.tensor_mul(new, new, got)
                dve.tensor_copy(conv_last[:, c, 0:16].rearrange("p (b r) -> p b r", r=2), u_s[:, c, :, 8:10])
                t = dve.tensor_copy(conv_last[:, c, 16:18], u_ext[:, c, 256:258])
            link(t)
            dve.transpose(conv_last_t[:, :, :], conv_last[:, :, :]).then_inc(convlast_made, 1)

            for n in range(2 * HEADS):
                if n + 1 < 2 * HEADS:
                    prompt_stats(n + 1)
                dve.wait_ge(pexp_made, n + 1)
                link(dve.reciprocal(p_inv[:, n, :], p_sum[:, n, :]))
                base = 384 * (n % 2)
                dve.tensor_scalar(probs[:, base:base + P], probs[:, base:base + P], p_inv[:, n, 0:1], None, ALU.mult)
                dve.tensor_scalar(probs[:, base + P:base + 384], probs[:, base + P:base + 384], p_inv[:, n, 1:2], None,
                                  ALU.mult).then_inc(pnorm_made, 1)
                for i in WITH_HEAD[n]:
                    if i + 1 < N_ADA2:
                        make_lo(ADA2[i + 1].chunk, KD * CH)
                    ada_rows(ADA2[i])

            def move(position, stage_ready):
                dve.wait_ge(t_ready, stage_ready)
                bank = 3 + position % 3
                if position < 12:
                    par, p, half = position // 6, position % 6 // 2, position % 2
                    dve.tensor_copy(k_t[:, par, p, 512 * half:512 * half + 512], ps[:, bank, :]).then_inc(moved_v, 1)
                elif position == 12:
                    dve.tensor_copy(probs_t[:, 0:4, :], ps[:, bank, :].rearrange("p (g r) -> p g r", g=4))\
                        .then_inc(moved_v, 1)
                else:
                    dve.tensor_copy(probs_t[0:TSA, PAGES, :], ps[0:TSA, bank, 0:P]).then_inc(moved_v, 1)

            for position in range(12):
                if EVACS[position] == "V":
                    move(position, position + 1)

            def unit_stats(bp, kind, u):
                dve.wait_ge(s_ready, u + 1)
                new = psf[:, PAST:PAST + TSA]
                at = (C_FOXNEW, C_MOBANEW)[kind]
                mask = const[:, bass.ds(bp * TSA + at, TSA)]
                if kind == 0:
                    link(dve.tensor_add(new, new, mask))
                    link(dve.tensor_reduce(u_max[:, 0:1], psf[:, 0:PAST + TSA], AX.X, ALU.max))
                    dve.tensor_scalar(u_nb[:, 0:1], u_max[:, 0:1], -SCALE, None, ALU.mult).then_inc(stats_made, 1)
                    return
                link(dve.tensor_reduce(gates[:, 0:NBLK], psf[:, 0:PAST].rearrange("p (b k) -> p b k", b=NBLK), AX.X,
                                       ALU.add))
                link(dve.tensor_reduce(gates[:, 4:5], gates[:, 0:NBLK], AX.X, ALU.min))
                link(stt(pick[:, 0:NBLK], gates[:, 0:NBLK], gates[:, 4:5], const[:, C_RANK:C_RANK + NBLK],
                         ALU.is_equal, ALU.mult))
                link(dve.tensor_reduce(pick[:, 4:5], pick[:, 0:NBLK], AX.X, ALU.max))
                link(dve.tensor_scalar(pen[:, 0:NBLK], pick[:, 0:NBLK], pick[:, 4:5], NEG, ALU.is_equal, ALU.mult))
                dve.tensor_add(probs[:, PAST:PAST + TSA], new, mask)
                link(dve.tensor_add(probs[:, 0:PAST], psf[:, 0:PAST], const[:, C_MOBAPAST:C_MOBAPAST + PAST]))
                dve.tensor_reduce(u_max[:, 4:5], probs[:, PAST:PAST + TSA], AX.X, ALU.max)
                link(dve.tensor_reduce(u_max[:, 0:NBLK], probs[:, 0:PAST].rearrange("p (b k) -> p b k", b=NBLK), AX.X,
                                       ALU.max))
                link(dve.tensor_add(u_max[:, 0:NBLK], u_max[:, 0:NBLK], pen[:, 0:NBLK]))
                link(dve.tensor_reduce(u_max[:, 5:6], u_max[:, 0:5], AX.X, ALU.max))
                dve.tensor_scalar(u_nb[:, 0:5], pen[:, 0:5], u_max[:, 5:6], SCALE, ALU.subtract, ALU.mult)\
                    .then_inc(stats_made, 1)

            def take_y(bp, kind):
                q = (FQ, MQ)[kind]
                for half in range(2):
                    r = slice(HD * half, HD * half + HD)
                    src = ps[r, 7, 0:384].rearrange("p (a b c) -> p a b c", a=3, b=2)[:, :, :, TS * half:TS * half + TS]
                    for p in range(PAIRS):
                        t = dve.tensor_copy(proj[r, q + p, bass.ds(bp * (2 * TS) + TP, 2 * TS)]
                                            .rearrange("p (b t) -> p b t", b=2), src[:, p])
                t.then_inc(yt_moved, 1)

            def unit(bp, kind, u, first, last):
                base = u * 15 + (12 + 1)
                unit_stats(bp, kind, u)
                if not first:
                    dve.wait_ge(yt_ready, u)
                    take_y(bp if kind else bp - 1, 1 - kind)
                if not last:
                    for position in (6, 7, 9, 11):
                        move(position, base + position)
                dve.wait_ge(exp_made, u + 1)
                if kind == 1:
                    link(dve.tensor_reduce(u_sum[:, 5:6], u_sum[:, 0:5], AX.X, ALU.add))
                dve.reciprocal(u_inv[:, 0:1], u_sum[:, 0:1] if kind == 0 else u_sum[:, 5:6]).then_inc(inv_made, 1)
                move(12, base + (0 if last else 12))
                move(14, base + (2 if last else 14))

            LINKS = 2 + 10
            chain.start += chain.k
            chain.k = 0
            dve.memset(pen[:, :], 0.0).then_inc(dve_misc, 1)
            dve.wait_ge(dve_misc, 2)
            chain.enter(0, LINKS)
            unit(0, 0, 0, True, False)
            unit(0, 1, 1, False, False)
            with dve.Fori(1, BP - 1) as bp:
                chain.enter(bp, LINKS)
                unit(bp, 0, bp * 2, False, False)
                unit(bp, 1, bp * 2 + 1, False, False)
            chain.enter(BP - 1, LINKS)
            unit(BP - 1, 0, 2 * BP - 2, False, False)
            unit(BP - 1, 1, 2 * BP - 1, False, True)
            chain.close(BP)
            dve.wait_ge(yt_ready, 2 * BP)
            take_y(BP - 1, 1)

            for n, (at, frm, cnt) in enumerate(((0, CB, 2), (2, FQ, 3), (5, MQ, 3))):
                dve.wait_ge(mixh_made, n + 1)
                dve.wait_ge(yt_moved, 2 * BP)
                dve.tensor_sub(h_l[:, at:at + cnt, :], proj[:, frm:frm + cnt, :],
                               h_h[:, at:at + cnt, :].bitcast(F32)).then_inc(mixl_made, 1)
            for k in range(N_O):
                make_lo(Chunk(AT_O, 0, k), 2 * D)

            def move_out(n):
                dve.wait_ge(w_used, (AT_UP, AT_DOWN + N_DOWN)[n])
                for m in range(1, KD, 2):
                    dve.tensor_copy(y_t[:, m, :], ps[:, m, 0:TOK]).then_inc(outv_moved, 1)

            move_out(0)

            def ln_stats(n, tt, gate):
                r = slice(0, NT[tt])
                dve.wait_ge(back_ready, 3 * n + tt + 1)
                row, mv = ln_rows[r, tt, :], ln_mv[r, tt, :]
                link(dve.tensor_mul(row, mods[r, gate, PR[tt], :], psf[r, 1024 * tt:1024 * tt + D]))
                link(stt(row, xt[r, tt, :], ALPHA, row, ALU.mult, ALU.add))
                for hf in range(2):
                    t = dve.bn_stats(bn[r, tt, hf, :], ln_rows[r, tt, 512 * hf:512 * hf + 512])
                link(t)
                link(dve.bn_aggr(mv[:, 0:2], bn[r, tt, :, :].rearrange("p a b -> p (a b)")))
                dve.tensor_scalar(mv[:, 1:2], mv[:, 1:2], EPS, None, ALU.add).then_inc(var_made, 1)

            def inverse_std(n, tt):
                mv = ln_mv[0:NT[tt], tt, :]
                dve.wait_ge(std_made, 3 * n + tt + 1)
                link(dve.reciprocal(mv[:, 2:3], mv[:, 2:3]))
                stt(mv[:, 3:4], mv[:, 0:1], -1.0, mv[:, 2:3], ALU.mult, ALU.mult).then_inc(stat_made, 1)

            def ffn_rows(tt):
                dve.wait_ge(scaled, tt + 1)
                modulate(xt, ln_rows, tt, SH_F, SC_F)

            ln_stats(0, 0, GT_A)
            inverse_std(0, 0)
            ln_stats(0, 1, GT_A)
            inverse_std(0, 1)
            ffn_rows(0)
            ln_stats(0, 2, GT_A)
            inverse_std(0, 2)
            ffn_rows(1)
            ffn_rows(2)
            features_lo()

            for e in ext:
                t = dve.memset(e[:, :, 0:2], 0.0)
            link(t)
            chain.start += chain.k
            chain.k = 0

            def past_rows(c):
                for m in range(2):
                    src = st_t[:, bass.ds(c.j + m * FT, 1), 0:16].rearrange("p o (b r) -> p (o b) r", r=2)
                    t = dve.tensor_copy(ext[c.slot][:, m, 258:338].rearrange("p (b t) -> p b t", b=SEQS)[:, :, 0:2],
                                        src)
                t.then_inc(past_in, 1)

            def conv(c):
                e = ext[c.slot]
                dve.wait_ge(tap_made, c.j + 1)
                for m in range(2):
                    tile = st_t[:, bass.ds(c.j + m * FT, 1), :].rearrange("p o r -> p (o r)")
                    for j in (1, 2):
                        t = stt(acc[:, m, :], e[:, m, j:j + 336], tile[:, 16 + j:17 + j], acc[:, m, :],
                                ALU.mult, ALU.add)
                        if m == 0 or j == 1:
                            link(t)
                t.then_inc(conv_made, 1)

            def gate_value(c):
                dve.wait_ge(conv_made, c.j + 1)
                dve.wait_ge(gate_made, c.j + 1)
                after(dve, acth_made, c.j)
                link(dve.tensor_mul(act_f[:, 0:TP], acc[:, 0, 0:TP], acc[:, 1, 0:TP]))
                s = [acc[:, m, 256:336].rearrange("p (b t) -> p b t", b=SEQS)[:, :, 2:10] for m in range(2)]
                dve.tensor_mul(act_f[:, TP:TOK].rearrange("p (b t) -> p b t", b=SEQS), s[0], s[1])\
                    .then_inc(actf_made, 1)

            def act_lo(c):
                dve.wait_ge(actf_made, c.j + 1)
                dve.wait_ge(acth_made, c.j + 1)
                dve.tensor_sub(act_l[:, bass.ds(c.j, 1), :].rearrange("p o t -> p (o t)"), act_f[:, :],
                               act_h[:, bass.ds(c.j, 1), :].rearrange("p o t -> p (o t)").bitcast(F32))\
                    .then_inc(actl_made, 1)

            def ffn_act(c):
                if not isinstance(c.j, int) or c.j >= 1:
                    act_lo(c.before())
                conv(c)
                gate_value(c)

            def up_step(c):
                if c.k == 0:
                    chain.start = links if isinstance(c.turn, int) and c.turn == 0 else links - 8
                    chain.enter(c.turn, 16)
                b = c.before().before() if not isinstance(c.j, int) or c.j >= 2 else None
                if b:
                    past_rows(b)
                make_lo(c, KD * CH)
                if b:
                    ffn_act(b)
            links = chain.start
            ring(dve, AT_UP, N_UP, up_step)
            last = Chunk(AT_UP, N_UP // 4, N_UP % 4 - 1)
            for c in (last.before(), last):
                past_rows(c)
                ffn_act(c)
            act_lo(last)
            chain.start, chain.turn, chain.per, chain.k = chain.start + 16 * (N_UP // 4) + chain.k, 0, 0, 0
            dve.wait_ge(last_kept, N_UP)
            dve.transpose(ff_last_t[:, :, :], ff_last[:, :, :]).then_inc(fflast_made, 1)
            ring(dve, AT_DOWN, N_DOWN, lambda c: make_lo(c, 2 * D))
            move_out(1)
            for tt in range(3):
                ln_stats(1, tt, GT_F)
                inverse_std(1, tt)

        @block.gpsimd
        def _(pool):
            for b in b_ada:
                t = pool.memset(b[:, :], 0.0)
            t.then_inc(bias_zeroed, 1)
            pool.memset(state_raw[:, :, :], 0.0).then_inc(state_zeroed, 1)
            pool.memset(conv_last[:, :, :], 0.0).then_inc(pool_step, 1)
            for b in range(BLK):
                at = slice(b * CH, b * CH + CH)
                pool.wait_ge(x_in, 32)
                pool.wait_ge(mods_made, 2 * b + 2)
                for tt in range(3):
                    n = NT[tt]
                    t = pool.tensor_mul(rows[0:n, tt, at], xt[0:n, tt, at], mods[0:n, SC_A, PR[tt], at])
                t.then_inc(x_scaled, 1)
                pool.wait_ge(x_scaled, b + 1)
                for tt in range(3):
                    n = NT[tt]
                    t = pool.tensor_add(rows[0:n, tt, at], rows[0:n, tt, at], mods[0:n, SH_A, PR[tt], at])
                t.then_inc(rows_made, 1)
            pool.wait_ge(tables_in, 16)
            pool.wait_ge(ff_ready, 1)
            pool.memset(lf_sum[:, :, :, :], 0.0).then_inc(lfsum_zeroed, 1)
            pool.wait_ge(lft_ready, 1)
            pool.memset(bias_r[:, PAST:PAST + TSA], 0.0).then_inc(newbias_zeroed, 1)
            pool.wait_ge(cum_made, 1)
            pool.wait_ge(logft_ready, 1)
            for q in qblk:
                pool.memset(q[:, :, :, :], 0.0).then_inc(pool_step, 1)
            pool.wait_ge(pool_step, 3)

            def build_q(bp, kind, u):
                after(pool, s_ready, u - 1)
                at = (FQ, MQ)[kind]
                for half in range(2):
                    r = slice(HD * half, HD * half + HD)
                    for p in range(PAIRS):
                        t = pool.tensor_copy(qblk[kind][r, :, p, TS * half:TS * half + TS],
                                             proj[r, at + p, bass.ds(bp * (2 * TS) + TP, 2 * TS)]
                                             .rearrange("p (b t) -> p b t", b=2))
                t.then_inc(q_built, 1)

            def build_bias(bp):
                after(pool, s_ready, bp * 2 - 1)
                pool.tensor_tensor(bias_r[:, 0:PAST].rearrange("p (g s) -> p g s", g=PAGES),
                                   c_suffix[:, bass.ds(bp, 1), :].to_broadcast([P, PAGES, P]),
                                   const[:, C_PAGEM:C_PAGEM + PAGES].unsqueeze(2).to_broadcast([P, PAGES, P]),
                                   ALU.mult).then_inc(bias_built, 1)

            pool.wait_ge(tile_moved, N_PROJ)
            pool.wait_ge(suffix_made, 1)
            pool.wait_ge(newbias_made, 2)

            def units(bp):
                after(pool, q_built, bp * 2)
                build_bias(bp)
                pool.wait_ge(bias_built, bp + 1)
                build_q(bp, 0, bp * 2)
                build_q(bp, 1, bp * 2 + 1)
            units(0)
            with pool.Fori(1, BP) as bp:
                units(bp)

            def scale_row(n, gb, tt):
                r = slice(0, NT[tt])
                pool.wait_ge(normed, 3 * n + tt + 1)
                pool.tensor_mul(xt[r, tt, :], xt[r, tt, :], gb[r, 0, :]).then_inc(gain_made, 1)
                pool.wait_ge(gain_made, 3 * n + tt + 1)
                pool.tensor_add(xt[r, tt, :], xt[r, tt, :], gb[r, 1, :]).then_inc(scaled, 1)

            def scale_rows(n, gb):
                pool.wait_ge(ln_in, 32 * (n + 1))
                for tt in range(3):
                    scale_row(n, gb, tt)

            scale_rows(0, ln_gb1)
            pool.memset(ff_last[:, :, :], 0.0).then_inc(fflast_zeroed, 1)
            pool.wait_ge(fflast_zeroed, 1)

            def keep_last(c):
                pool.wait_ge(tap_made, c.j + 1)
                e = ext[c.slot]
                for m in range(2):
                    dst = ff_last[:, bass.ds(c.j + m * FT, 1), :].rearrange("p o r -> p (o r)")
                    pool.tensor_copy(dst[:, 0:16].rearrange("p (b r) -> p b r", r=2),
                                     e[:, m, 258:338].rearrange("p (b t) -> p b t", b=SEQS)[:, :, 8:10])
                    t = pool.tensor_copy(dst[:, 16:18], e[:, m, 256:258])
                t.then_inc(last_kept, 1)
            ring(pool, AT_UP, N_UP, keep_last)
            scale_rows(1, ln_gb2)


NAMES = ["x_prompt", "x_sample", "cache_fox_k", "cache_fox_v", "cache_fox_logf", "cache_moba_k", "cache_moba_v",
         "state_conv", "state_ffn", "page_table", "c_prompt", "c_sample", "w_ada", "b_ada", "w_in", "b_f", "conv_w",
         "w_o", "ln1_g", "ln1_b", "w_up", "ffn_conv_w", "ffn_conv_b", "w_down", "ln2_g", "ln2_b"]


def outputs():
    out = [("y_p", (1, TP, D)), ("y_s", (SEQS, TS, D))]
    for s, g, t in (("p", 1, TP), ("s", SEQS, TS)):
        out += [(f"fk_{s}", (1, g, t, HEADS, HD)), (f"fv_{s}", (1, g, t, HEADS, HD)), (f"lf_{s}", (1, g, t, HEADS)),
                (f"mk_{s}", (1, g, t, HEADS, HD)), (f"mv_{s}", (1, g, t, HEADS, HD)), (f"conv_{s}", (1, g, 2, CW)),
                (f"ffn_{s}", (1, g, 2, 2 * DFF))]
    return out


def kernel(**inputs):
    import concourse.bacc as bacc
    from concourse.bass_utils import run_bass_kernel_spmd

    nc = bacc.Bacc("TRN2", target_bir_lowering=False, num_devices=1, dynamic_dma_scratch_size=1024)
    arrays = {n: np.ascontiguousarray(inputs[n]) for n in NAMES}
    arrays["const"] = constants()
    a = {n: nc.dram_tensor(f"in_{n}", x.shape, mybir.dt.from_np(x.dtype), kind="ExternalInput").ap()
         for n, x in arrays.items()}
    o = {n: nc.dram_tensor(f"out_{n}", s, F32, kind="ExternalOutput").ap() for n, s in outputs()}
    build(nc, a, o)
    r = run_bass_kernel_spmd(nc, [{f"in_{n}": x for n, x in arrays.items()}], core_ids=[0])
    return tuple(r.results[0][f"out_{n}"] for n, _ in outputs())
```

```python
from contextlib import ExitStack

import numpy as np

import concourse.bass as bass
from concourse import mybir

F32 = mybir.dt.float32
F32R = mybir.dt.float32r
I32 = mybir.dt.int32
ALU = mybir.AluOpType
ACT = mybir.ActivationFunctionType
AX = mybir.AxisListType

P = 128
D = 1024
KD = D // P
TP, SEQS, TS = 256, 8, 8
TSA = SEQS * TS
TOK = TP + TSA
HEADS, HD = 6, 64
AW = HEADS * HD
PAIRS = HEADS // 2
CW = D // 4
PAST, PAGE = 1024, 128
PAGES = PAST // PAGE
POOL = 80
DFF = 2816
FT = DFF // P
MBLK, NBLK = 256, PAST // 256
NEG = -1.0e30
SCALE = HD ** -0.5
ALPHA = 2.0 ** 0.25
EPS = 1e-5
BP = SEQS // 2
ROWS = 112

CH = 256
BLK = D // CH
N_ADA1, N_ADA2 = 2 * BLK, 4 * BLK
N_IN, N_O, N_UP, N_DOWN = 12, KD // 2, FT, FT // 2
CHB = KD * CH * 4
AT_IN = N_ADA1
AT_ADA2 = AT_IN + N_IN
AT_O = AT_ADA2 + N_ADA2
AT_UP = AT_O + N_O
AT_DOWN = AT_UP + N_UP

CB, CC, CX, FQ, FK, FV, MQ, MK, MV = 0, 2, 4, 6, 9, 12, 15, 18, 21
N_PROJ = 24

C_IDENT, C_SELTOK = 0, 128
C_EARLY = C_SELTOK + 2 * P
C_TRI, C_ONES, C_DIAG, C_ALIBI = (C_EARLY + P * i for i in range(4))
C_SELB = C_ALIBI + 256
C_PAGEM = C_SELB + 128
C_FOXNEW = C_PAGEM + PAGES
C_MOBANEW = C_FOXNEW + BP * TSA
C_MOBAPAST = C_MOBANEW + BP * TSA
C_SCAN = C_MOBAPAST + PAST
C_RANK = C_SCAN + TOK
C_ALL = C_RANK + NBLK


def slopes():
    return 2.0 ** (-8.0 * np.arange(1, HEADS + 1) / HEADS)


def constants():
    c = np.zeros((P, C_ALL), np.float64)
    i = np.arange(P)
    c[:, C_IDENT:C_IDENT + P] = np.eye(P)
    c[:, C_TRI:C_TRI + P] = i[:, None] > i[None, :]
    c[:, C_ONES:C_ONES + P] = 1
    c[:, C_DIAG:C_DIAG + P] = np.where(i[None, :] <= i[:, None], 0, NEG)
    c[:, C_ALIBI:C_ALIBI + P] = i[None, :] - i[:, None] - P
    c[:, C_ALIBI + P:C_ALIBI + 2 * P] = np.where(i[None, :] <= i[:, None], i[None, :] - i[:, None], NEG)
    par, x = i // 64, i % 64
    for r in range(P):
        if x[r] < PAGES * HEADS:
            page, h = x[r] // HEADS, x[r] % HEADS
            c[r, C_SELB + 64 * par[r] + TS * h:C_SELB + 64 * par[r] + TS * h + TS] = 1
            c[r, C_PAGEM + page] = 1 / SCALE
        if x[r] < HEADS * TS:
            h, q = x[r] // TS, x[r] % TS
            sl = slopes()[h] / SCALE
            c[r, C_MOBAPAST:C_MOBAPAST + PAST] = sl * (np.arange(PAST) - PAST - q)
            for bp in range(BP):
                at = C_FOXNEW + bp * TSA
                am = C_MOBANEW + bp * TSA
                for s in range(TSA):
                    ok = s // TS == 2 * bp + par[r] and s % TS <= q
                    c[r, at + s] = 0 if ok else NEG
                    c[r, am + s] = sl * (s % TS - q) if ok else NEG
    for r in range(18):
        b = r % 9
        if b == 0:
            c[r, C_SELTOK:C_SELTOK + P] = 1
        else:
            c[r, C_SELTOK + P + (b - 1) * TS:C_SELTOK + P + b * TS] = 1
    c[:, C_SCAN:C_SCAN + TOK] = 1
    c[:, C_SCAN] = 0
    c[:, C_SCAN + TP:C_SCAN + TOK:TS] = 0
    c[:, C_RANK:C_RANK + NBLK] = 1 + np.arange(NBLK)
    return c.astype(np.float32)


class Chain:

    def __init__(self, eng, sem):
        self.eng, self.sem, self.start, self.turn, self.per, self.k = eng, sem, 0, 0, 0, 0

    def link(self, instruction):
        self.k += 1
        instruction.then_inc(self.sem, 1)
        self.eng.wait_ge(self.sem, self.turn * self.per + (self.start + self.k))

    def enter(self, turn, per):
        self.turn, self.per, self.k = turn, per, 0

    def close(self, turns):
        assert self.k == self.per
        self.start, self.turn, self.per, self.k = self.start + turns * self.per, 0, 0, 0


class Chunk:

    def __init__(self, base, turn, k):
        self.j = turn * 4 + k
        self.n = turn * 4 + (base + k)
        self.raw, self.slot = (base + k) % 4, (base + k) % 2
        self.loads = turn + ((base + k) // 4 + 1)
        self.base, self.turn, self.k = base, turn, k

    def before(self):
        return Chunk(self.base, self.turn, self.k - 1) if self.k else Chunk(self.base, self.turn - 1, 3)


def ring(eng, base, count, step, done=0):
    turns = count // 4

    def turn(i, frm=0):
        for k in range(frm, 4):
            step(Chunk(base, i, k))

    turn(0, done)
    if turns > 1:
        with eng.Fori(1, turns) as i:
            turn(i)
    for k in range(count % 4):
        step(Chunk(base, turns, k))


class Ada:

    def __init__(self, a):
        self.a = a
        self.late = a >= N_ADA1
        j = a - N_ADA1 if self.late else a
        self.chunk = Chunk(AT_ADA2 if self.late else 0, j // 4, j % 4)
        self.part, self.block = (a // BLK, a % BLK) if self.late else (a % 2, a // 2)
        self.column = self.part * D + self.block * CH
        self.bank, self.spread_bank, self.back = (5, 6, 1) if self.late else (a % 2, 2 + a % 2, 2)


ADA1 = [Ada(a) for a in range(N_ADA1)]
ADA2 = [Ada(a) for a in range(N_ADA1, N_ADA1 + N_ADA2)]
ADA_HEADS = 2 * HEADS - 1
WITH_HEAD = [range(min(N_ADA2 * n // ADA_HEADS, N_ADA2), min(N_ADA2 * (n + 1) // ADA_HEADS, N_ADA2))
             for n in range(2 * HEADS)]


def after(eng, semaphore, count):
    if not isinstance(count, int) or count > 0:
        eng.wait_ge(semaphore, count)


EVACS = "AAAAAAVVAVAV" + "VAV"
BEFORE = {"A": 8, "V": 4}
PER = {e: EVACS.count(e) for e in "AV"}


def evacs(stage, position, engine):
    return stage * PER[engine] + (BEFORE[engine] + EVACS[:position + 1].count(engine))


def build(nc, a, o):
    ctx = ExitStack()
    with ctx:
        sem = lambda n: ctx.enter_context(nc.semaphore(n))
        place = [1152]

        def region(size):
            at = place[0]
            place[0] += -(-size // 32) * 32
            return at

        def sb(name, shape, dt=F32, at=None):
            if at is None:
                at = region(int(np.prod(shape[1:])) * 4)
            return nc.alloc_sbuf_tensor_at(name, shape, dt, offset=at)

        const = sb("const", [P, C_ALL])
        xt = sb("x_tokens", [P, 3, D])
        st_t = sb("states_t", [P, 46, 32])
        conv_last = sb("conv_last", [P, 2, 32])
        conv_last_t = sb("conv_last_t", [P, 2, 32])
        ch = sb("silu_c_hi_lo", [P, KD, 18], F32R)
        wff = sb("w_forget", [P, KD, HEADS])
        wff_h = sb("w_forget_hi", [P, KD, HEADS], F32R)
        wff_l = sb("w_forget_lo", [P, KD, HEADS], F32R)
        b_f = sb("b_forget", [HEADS, 1])
        pages = sb("page_numbers", [1, SEQS * PAGES], I32)
        ada_row = [sb(f"ada_rows{i}", [18, CH]) for i in range(2)]
        B = region(4 * CH * 4)
        b_ada = [sb(f"b_ada{i}", [18, CH], at=B + 4 * CH * i) for i in range(4)]
        ln_b = sb("ln1_b_row", [P, D], at=B)
        p_max, p_nb, p_sum, p_inv = (sb(n, [P, 12, 2]) for n in ("p_max", "p_nb", "p_sum", "p_inv"))
        u_max, u_nb, u_sum, u_inv = (sb(n, [P, 1]) for n in ("u_max", "u_nb", "u_sum", "u_inv"))
        gates, pen, pick = sb("gates", [P, 8]), sb("penalty", [P, 8]), sb("pick", [P, 8])
        ln_s = sb("ln_sums", [P, 3, 6])
        eps = sb("eps", [P, 1])
        ncum = sb("minus_8_cum", [HEADS, TOK])
        lf_out = sb("logf_tokens", [P, 3, HEADS])
        H = region(2 * KD * TOK * 4)
        h_h = sb("h_hi", [P, KD, TOK], F32R, at=H)
        h_l = sb("h_lo", [P, KD, TOK], F32R, at=H + KD * TOK * 4)
        c_rows = sb("c_rows", [9, D], at=H + 8192)
        c_silu = sb("c_silu", [9, D], at=H + 12288)
        probs = sb("probs", [P, PAST + TSA], at=H)
        probs_t = sb("probs_t", [P, PAGES + 1, P], at=H + 4352)
        v_tok = sb("v_tok", [P, 2, 3, AW], at=H + 4352 + 4608)
        c_suffix = sb("c_suffix", [P, BP, P], at=H + 4352 + 4608 + 9216)
        y_t = sb("y_t", [P, KD, TOK], at=H)
        ff_last_t = sb("ff_last_t", [P, 44, 32], at=H + KD * TOK * 4)
        T = region(12096)
        bias_r = sb("bias_rows", [P, PAST + TSA], at=T)
        lf_rows = sb("lf_rows", [SEQS * PAGES, PAGE * HEADS], at=T)
        state_raw = sb("state_raw", [P, 46, 32], at=T + 4352)
        qblk = [sb(f"q_blocks{i}", [P, 2, 3, 64], at=T + 4352 + 1536 * i) for i in range(2)]
        y_row = sb("y_row", [P, AW], at=T + 7424)
        forget = sb("forget", [HEADS, 4, TOK], at=T + 4352)
        ext = [sb(f"ext{i}", [P, 2, 338], at=T + 2720 * i) for i in range(2)]
        acc2 = [sb(f"acc{i}", [P, 2, 336], at=T + (5440, 9408)[i]) for i in range(2)]
        ln_waste = sb("ln_squares", [P, D], at=T)
        act_f = sb("act_f", [P, TOK], at=T + 8128)
        R = region(8 * CHB)
        raw = [sb(f"raw{i}", [P, KD * CH], at=R + CHB * i) for i in range(4)]
        ln_scaled = sb("ln1_b_scaled", [P, 2, D], at=R)
        w_h = [sb(f"w_hi{i}", [P, KD * CH], F32R, at=R + CHB * (4 + i)) for i in range(2)]
        w_l = [sb(f"w_lo{i}", [P, KD * CH], F32R, at=R + CHB * (6 + i)) for i in range(2)]
        k_pages = [sb(f"k_pages{i}", [P, PAGES, AW], at=R + 2 * CHB + PAGES * AW * 4 * i) for i in range(2)]
        k_t = sb("k_t", [P, 2, PAIRS, PAST], at=R + 5 * CHB)
        XS = N_PROJ * TOK * 4
        X = region(56320)
        proj = sb("proj", [P, N_PROJ, TOK], at=X)
        v_pages = sb("v_pages", [P, 2, PAGES, AW], at=X + XS)
        k_tok = sb("k_tok", [P, 2, 3, AW], at=X + XS)
        lf_sum = sb("lf_sum", [P, 2, SEQS, 64], at=X + XS + 9216 + 5632)
        u_ext = sb("u_ext", [P, 2, 338], at=X + XS + 9216)
        u_acc = sb("u_acc", [P, 2, 336], at=X + XS + 9216 + 2816)
        rows = sb("rows", [P, 3, D], at=X + 24576)
        c_t = sb("silu_c_t", [P, KD * 9], at=X + 24576 + 12288)
        ln_rows = sb("ln_rows", [P, 3, D], at=X)
        ln_g = sb("ln1_g_row", [P, D], at=X + CC * TOK * 4)
        ln_gb1 = sb("ln1_g_b", [P, 2, D], at=X + XS)
        act_h = sb("act_hi", [P, FT, TOK], F32R, at=X)
        act_l = sb("act_lo", [P, FT, TOK], F32R, at=X + FT * TOK * 4)
        M = X + 56320 - 16384
        region(32768)
        mods = sb("mods", [P, 6, 2, D], at=M)
        ff_last = sb("ff_last", [P, 44, 32], at=M + 16384)
        ln_gb2 = sb("ln2_g_b", [P, 2, D], at=M + 16384 + 5632)
        SH_A, SC_A, GT_A, SH_F, SC_F, GT_F = range(6)
        ps = ctx.enter_context(nc.psum_tensor("ps", [P, 8, 512], F32))
        psf = ps[:, :, :].rearrange("p b c -> p (b c)")

        ident = const[:, C_IDENT:C_IDENT + P]
        token_tiles = [(kv, kind, tt) for kv in (k_tok, v_tok) for kind in range(2) for tt in range(3)]
        NT = [P, P, TSA]
        PR = [0, 0, 1]

        const_in, tables_in, x_in, c_in, small_in = (
            sem(n) for n in ("const_in", "tables_in", "x_in", "c_in", "small_in"))
        bias_in = [sem(f"bias_in{i}") for i in range(4)]
        bias_zeroed, state_zeroed, state_in, lf_in = sem("bias_zeroed"), sem("state_zeroed"), sem("state_in"), sem("lf_in")
        raw_in = [sem(f"raw_in{i}") for i in range(4)]
        hi_made, lo_made, w_used = sem("hi_made"), sem("lo_made"), sem("w_used")
        silu_made, ct_ready, ct_copied, ch_hi, ch_lo = (
            sem(n) for n in ("silu_made", "ct_ready", "ct_copied", "ch_hi", "ch_lo"))
        ada_made, ex_ready, mods_made, x_scaled = (
            sem(n) for n in ("ada_made", "ex_ready", "mods_made", "x_scaled"))
        rows_made, ht_ready, hh_made, hl_made = (sem(n) for n in ("rows_made", "ht_ready", "hh_made", "hl_made"))
        tile_ready, tile_moved = sem("tile_ready"), sem("tile_moved")
        wff_hi, wff_lo, ff_ready, absz_made, softplus_made, logf_made, cum_made = (
            sem(n) for n in ("wff_hi", "wff_lo", "ff_ready", "absz_made", "softplus_made", "logf_made", "cum_made"))
        tok_ready, toka_moved, tokv_moved, lft_ready, lfsum_zeroed, lfsum_made, suffix_ready, suffix_made = (
            sem(n) for n in ("tok_ready", "toka_moved", "tokv_moved", "lft_ready", "lfsum_zeroed", "lfsum_made", "suffix_ready",
                             "suffix_made"))
        logft_ready, logft_moved, convlast_made = sem("logft_ready"), sem("logft_moved"), sem("convlast_made")
        kv_stored, stored = sem("kv_stored"), sem("stored")
        ps_ready, pnb_made, pexp_made, pnorm_made, ppt_ready, ppt_moved, py_ready, py_moved = (
            sem(n) for n in ("ps_ready", "pnb_made", "pexp_made", "pnorm_made", "ppt_ready", "ppt_moved", "py_ready",
                             "py_moved"))
        newbias_zeroed, newbias_made, q_built, bias_built = (
            sem(n) for n in ("newbias_zeroed", "newbias_made", "q_built", "bias_built"))
        k_in = [sem(f"k_in{i}") for i in range(2)]
        v_in = [sem(f"v_in{i}") for i in range(4)]
        v_read, s_ready, stats_made, exp_made, inv_made = (
            sem(n) for n in ("v_read", "s_ready", "stats_made", "exp_made", "inv_made"))
        t_ready, moved_a, moved_v, pv_ready, yrow_made, yt_ready, yt_moved = (
            sem(n) for n in ("t_ready", "moved_a", "moved_v", "pv_ready", "yrow_made", "yt_ready", "yt_moved"))
        mixh_made, mixl_made = sem("mixh_made"), sem("mixl_made")
        outa_moved, outv_moved, back_ready = (
            sem(n) for n in ("outa_moved", "outv_moved", "back_ready"))
        ln_in, res_made, std_made, stat_made, normed, gain_made, scaled = (
            sem(n) for n in ("ln_in", "res_made", "std_made", "stat_made", "normed", "gain_made", "scaled"))
        g_b_in, gb_step, gb_made, final_made = (sem(n) for n in ("g_b_in", "gb_step", "gb_made", "final_made"))
        row0_made = sem("row0_made")
        eps_set = sem("eps_set")
        fflast_zeroed, tap_made, gate_made, actf_made, acth_made, actl_made, last_kept, fflast_made = (
            sem(n) for n in ("fflast_zeroed", "tap_made", "gate_made", "actf_made", "acth_made", "actl_made",
                             "last_kept", "fflast_made"))
        dve_step, pool_step, act_step, act_link, dve_misc = (
            sem(n) for n in ("dve_step", "pool_step", "act_step", "act_link", "dve_misc"))
        ext_moved, past_in, conv_made = sem("ext_moved"), sem("past_in"), sem("conv_made")

        w_ada, w_in, w_o, w_up, w_down = (a[n].rearrange("l r c -> (l r) c").rearrange("(k p) c -> p k c", p=P)
                                          for n in ("w_ada", "w_in", "w_o", "w_up", "w_down"))
        in_at = [P * t + (HEADS if t >= 15 else 0) for t in range(N_PROJ)]

        def raw_k(c):
            return raw[c.raw][:, :].rearrange("p (k c) -> p k c", k=KD)

        def hi_lo(c):
            return (w[c.slot][:, :].rearrange("p (k c) -> p k c", k=KD) for w in (w_h, w_l))

        def load_logf(eng, n):
            page = eng.value_load(pages[0:1, n:n + 1], min_val=0, max_val=POOL - 1)
            eng.dma_start(lf_rows[n:n + 1, :], a["cache_fox_logf"][0, bass.ds(page, 1)]
                          .rearrange("o s h -> o (s h)")).then_inc(lf_in, 16)

        block = ctx.enter_context(nc.Block())

        @block.sync
        def _(sp):
            sp.dma_start(c_rows[0:1, :], a["c_prompt"]).then_inc(c_in, 16)
            sp.dma_start(c_rows[1:9, :], a["c_sample"]).then_inc(c_in, 16)
            sp.dma_start(const[:, 0:C_EARLY], a["const"][:, 0:C_EARLY]).then_inc(const_in, 16)
            sp.wait_ge(bias_zeroed, 1)

            def slot_free(c):
                after(sp, lo_made, c.n - 3)

            def load_ada(d):
                c = d.chunk
                slot_free(c)
                for k in (0, 4):
                    sp.dma_start(raw_k(c)[:, k:k + 4, :],
                                 w_ada[:, k:k + 4, d.column:d.column + CH]).then_inc(raw_in[c.raw], 16)
                after(sp, ada_made, d.a - 3)
                sp.dma_start(b_ada[d.a % 4][0:9, :], a["b_ada"][:, d.column:d.column + CH].to_broadcast([9, CH]))\
                    .then_inc(bias_in[d.a % 4], 16)

            for d in ADA1[:2]:
                load_ada(d)
            sp.dma_start(xt[:, 0:2, :], a["x_prompt"].rearrange("g (t p) d -> p (g t) d", p=P)).then_inc(x_in, 16)
            sp.dma_start(xt[0:TSA, 2, :], a["x_sample"].rearrange("b t d -> (b t) d")).then_inc(x_in, 16)
            for d in ADA1[2:]:
                load_ada(d)

            def other_loads():
                sp.dma_start(const[:, C_EARLY:C_ALL], a["const"][:, C_EARLY:C_ALL]).then_inc(tables_in, 16)
                sp.wait_ge(state_zeroed, 1)
                for g in range(4):
                    for at, n, src in ((0, 16, a["state_ffn"].rearrange("l b r (t g j) -> g (l b r) t j", g=4, j=32)),
                                       (16, 3, a["ffn_conv_w"].rearrange("l w (t g j) -> g (l w) t j", g=4, j=32)),
                                       (19, 1, a["ffn_conv_b"].rearrange("l (t g j) -> g l t j", g=4, j=32))):
                        sp.dma_start(state_raw[32 * g + at:32 * g + at + n, 0:44, :], src[g]).then_inc(state_in, 16)
                    for at, n, src in ((0, 16, a["state_conv"].rearrange("l b r (t g j) -> g (l b r) t j", g=4, j=32)),
                                       (16, 3, a["conv_w"].rearrange("l w (t g j) -> g (l w) t j", g=4, j=32))):
                        sp.dma_start(state_raw[32 * g + at:32 * g + at + n, 44:46, :], src[g]).then_inc(state_in, 16)

            some = SEQS * PAGES // 2 // (N_IN - 4)
            for j in range(N_IN):
                c = Chunk(AT_IN, 0, j)
                slot_free(c)
                for m in range(2):
                    at = in_at[2 * j + m]
                    sp.dma_start(raw_k(c)[:, :, m * P:m * P + P], w_in[:, :, at:at + P]).then_inc(raw_in[c.raw], 16)
                if j == 0:
                    sp.dma_start(b_f[:, :], a["b_f"].rearrange("l h -> h l")).then_inc(small_in, 16)
                    sp.dma_start(pages[:, :], a["page_table"].rearrange("b (o p) -> o (b p)", o=1))\
                        .then_inc(small_in, 16)
                    sp.dma_start(wff[:, :, :], w_in[:, :, 15 * P:15 * P + HEADS]).then_inc(small_in, 16)
                if j == 2:
                    other_loads()
                    sp.wait_ge(small_in, 48)
                for n in range(some * (j - 4), some * (j - 3)) if j >= 4 else ():
                    load_logf(sp, n)

            caches = [(a["cache_fox_k"], a["cache_fox_v"]), (a["cache_moba_k"], a["cache_moba_v"])]

            def page_numbers(bp):
                return [[sp.value_load(pages[0:1, bass.ds(bp * (2 * PAGES) + (par * PAGES + page), 1)],
                                       min_val=0, max_val=POOL - 1) for page in range(PAGES)] for par in range(2)]

            def page_of(cache, number):
                return cache[0, bass.ds(number, 1)].rearrange("o s h d -> (o s) (h d)")

            def load_k(bp, kind, numbers):
                u = bp * 2 + kind
                for par in range(2):
                    if u:
                        sp.wait_ge(t_ready, u * 15 - 12 + 6 * par if u > 1 else 6 * par + 6)
                    for page in range(PAGES):
                        sp.dma_start(k_pages[par][:, page, :],
                                     page_of(caches[kind][0], numbers[par][page])).then_inc(k_in[par], 16)

            def load_v(bp, kind, numbers):
                u = bp * 2 + kind
                for g in range(4):
                    after(sp, v_read, u * 4 + (g - 3))
                    for page in (2 * g, 2 * g + 1):
                        for par in range(2):
                            sp.dma_start(v_pages[:, par, page, :],
                                         page_of(caches[kind][1], numbers[par][page])).then_inc(v_in[g], 16)

            def store_new():
                sp.wait_ge(toka_moved, 6)
                sp.wait_ge(tokv_moved, 6)
                for src, kind, po, so in ((v_tok, 0, "fv_p", "fv_s"), (v_tok, 1, "mv_p", "mv_s"),
                                             (k_tok, 0, "fk_p", "fk_s"), (k_tok, 1, "mk_p", "mk_s")):
                    sp.dma_start(o[po].rearrange("l g (t p) h d -> p (l g t) (h d)", p=P),
                                  src[:, kind, 0:2, :]).then_inc(kv_stored, 16)
                    sp.dma_start(o[so].rearrange("l b t h d -> (l b t) (h d)"), src[0:TSA, kind, 2, :])\
                        .then_inc(kv_stored, 16)
                sp.wait_ge(logft_moved, 1)
                for tt in range(2):
                    sp.dma_start(o["lf_p"][0, 0, tt * P:tt * P + P, :], lf_out[:, tt, :]).then_inc(stored, 16)
                sp.dma_start(o["lf_s"].rearrange("l b t h -> (l b t) h"), lf_out[0:TSA, 2, :]).then_inc(stored, 16)

            def store_conv():
                sp.wait_ge(convlast_made, 1)
                for g in range(4):
                    for at, n, dst in ((0, 16, o["conv_s"]), (16, 2, o["conv_p"])):
                        sp.dma_start(dst.rearrange("l b r (t g j) -> g (l b r) t j", g=4, j=32)[g],
                                      conv_last_t[32 * g + at:32 * g + at + n, :, :]).then_inc(stored, 16)

            for d in ADA2[:5]:
                load_ada(d)
            store_new()
            for d in ADA2[5:8]:
                load_ada(d)
            store_conv()
            for d in ADA2[8:]:
                load_ada(d)
            numbers = page_numbers(0)
            sp.wait_ge(ht_ready, BLK)
            sp.wait_ge(kv_stored, 16 * 8)
            load_v(0, 0, numbers)
            sp.wait_ge(w_used, AT_O)
            load_k(0, 0, numbers)
            sp.wait_ge(ada_made, N_ADA1 + N_ADA2)
            sp.dma_start(ln_g[:, :], a["ln1_g"].to_broadcast([P, D])).then_inc(g_b_in, 16)
            sp.dma_start(ln_b[:, :], a["ln1_b"].to_broadcast([P, D])).then_inc(g_b_in, 16)
            load_k(0, 1, numbers)
            for bp in range(1, BP):
                before, numbers = numbers, page_numbers(bp)
                load_k(bp, 0, numbers)
                load_v(bp - 1, 1, before)
                load_k(bp, 1, numbers)
                load_v(bp, 0, numbers)
            def load_rows(w):
                def load(c):
                    slot_free(c)
                    for kk in range(2):
                        sp.dma_start(raw[c.raw][:, kk * D:kk * D + D],
                                     w[:, bass.ds(c.j * 2 + kk, 1), :].rearrange("p o c -> p (o c)"))\
                            .then_inc(raw_in[c.raw], 16)
                return load

            sp.wait_ge(gb_made, 1)
            for k in range(N_O):
                if k == 2:
                    sp.wait_ge(t_ready, 15 * (2 * BP - 1) + 9)
                load_rows(w_o)(Chunk(AT_O, 0, k))
            load_v(BP - 1, 1, numbers)
            sp.wait_ge(v_read, 8 * BP)
            sp.dma_start(ln_gb1[:, 0, :], a["ln1_g"].to_broadcast([P, D])).then_inc(ln_in, 16)
            sp.dma_start(ln_gb1[:, 1, :], a["ln1_b"].to_broadcast([P, D])).then_inc(ln_in, 16)

            def load_up(c):
                slot_free(c)
                for m in range(2):
                    sp.dma_start(raw_k(c)[:, :, m * P:m * P + P],
                                 w_up[:, :, bass.ds(c.j * P + m * DFF, P)]).then_inc(raw_in[c.raw], 16)

            ring(sp, AT_UP, N_UP, load_up)
            sp.wait_ge(hl_made, BLK + 6)
            sp.dma_start(ln_gb2[:, 0, :], a["ln2_g"].to_broadcast([P, D])).then_inc(ln_in, 16)
            sp.dma_start(ln_gb2[:, 1, :], a["ln2_b"].to_broadcast([P, D])).then_inc(ln_in, 16)
            ring(sp, AT_DOWN, N_DOWN, load_rows(w_down))
            sp.wait_ge(fflast_made, 1)
            for g in range(4):
                for at, n, dst in ((0, 16, o["ffn_s"]), (16, 2, o["ffn_p"])):
                    sp.dma_start(dst.rearrange("l b r (t g j) -> g (l b r) t j", g=4, j=32)[g],
                                 ff_last_t[32 * g + at:32 * g + at + n, :, :]).then_inc(stored, 16)
            y_p = o["y_p"].rearrange("g (t p) d -> p (g t) d", p=P)
            sp.wait_ge(scaled, 4)
            sp.dma_start(y_p[:, 0, :], xt[:, 0, :]).then_inc(stored, 16)
            sp.wait_ge(final_made, 1)
            sp.dma_start(y_p[:, 1, :], xt[:, 1, :]).then_inc(stored, 16)
            sp.wait_ge(final_made, 2)
            sp.dma_start(o["y_s"].rearrange("b t d -> (b t) d"), xt[0:TSA, 2, :]).then_inc(stored, 16)
            sp.wait_ge(stored, 16 * (3 + 8 + 8 + 3))
            sp.wait_ge(kv_stored, 16 * 8)

        @block.tensor
        def _(pe):
            mm = pe.matmul

            def product(out, lhs, rhs, start, stop):
                mm(out, lhs[0], rhs[0], start=start, stop=False)
                mm(out, lhs[0], rhs[1], start=False, stop=False)
                return mm(out, lhs[1], rhs[0], start=False, stop=stop)

            pe.wait_ge(const_in, 16)
            pe.wait_ge(silu_made, 1)
            for k in range(KD):
                t = pe.transpose(ps[:, 6, 9 * k:9 * k + 9], c_silu[:, k * P:k * P + P], ident[0:9, 0:9])
            t.then_inc(ct_ready, 1)
            pe.wait_ge(ch_lo, 1)

            def ada(d):
                c = d.chunk
                pe.wait_ge(lo_made, c.n + 1)
                after(pe, ada_made, d.a + 1 - d.back)
                for half, w in enumerate(hi_lo(c)):
                    for k in range(KD):
                        t = mm(ps[0:18, d.bank, 0:CH], ch[:, k, :], w[:, k, :],
                               start=half == 0 and k == 0, stop=half == 1 and k == KD - 1)
                t.then_inc(w_used, 1)

            def spread(d):
                pe.wait_ge(ada_made, d.a + 1)
                after(pe, mods_made, d.a + 1 - d.back)
                for m in range(2):
                    at = C_SELTOK + m * P
                    t = mm(ps[:, d.spread_bank, m * CH:m * CH + CH], const[0:18, at:at + P], ada_row[d.a % 2][:, :],
                           start=True, stop=True)
                t.then_inc(ex_ready, 1)

            def block_to_features(b):
                pe.wait_ge(rows_made, b + 1)
                after(pe, hl_made, b - 1)
                for kk in range(2):
                    k = 2 * b + kk
                    for tt in range(3):
                        t = pe.transpose(ps[:, 4 + k % 4, tt * P:tt * P + NT[tt]],
                                         rows[0:NT[tt], tt, k * P:k * P + P], ident[0:NT[tt], 0:NT[tt]])
                t.then_inc(ht_ready, 1)

            for d in ADA1:
                ada(d)
                if d.a:
                    spread(ADA1[d.a - 1])
                if d.a % 2 and d.a >= 5:
                    block_to_features((d.a - 5) // 2)
            spread(ADA1[-1])
            block_to_features(BLK - 2)
            block_to_features(BLK - 1)

            def to_features():
                for tt in range(3):
                    if tt:
                        pe.wait_ge(rows_made, BLK + tt)
                    else:
                        pe.wait_ge(row0_made, 1)
                    for half in range(2):
                        for k in range(4):
                            kk = 4 * half + k
                            t = pe.transpose(ps[:, 2 * tt + half, k * P:k * P + NT[tt]],
                                             ln_rows[0:NT[tt], tt, kk * P:kk * P + P], ident[0:NT[tt], 0:NT[tt]])
                        t.then_inc(ht_ready, 1)

            h = (h_h, h_l)

            def product_tiles(c, bank, count_before):
                hi, lo = hi_lo(c)
                for m in range(2):
                    after(pe, tile_moved, c.j * 2 + (count_before + m - 7))
                    for k in range(KD):
                        t = product(ps[:, bank + m, 0:TOK], [w[:, k, m * P:m * P + P] for w in (hi, lo)],
                                    [x[:, k, :] for x in h], k == 0, k == KD - 1)
                    t.then_inc(w_used if m else tile_ready, 1)

            pe.wait_ge(hl_made, BLK)

            def in_step(c):
                pe.wait_ge(lo_made, c.n + 1)
                product_tiles(c, 2 * c.raw, 0)
            ring(pe, AT_IN, N_IN, in_step)
            pe.wait_ge(tile_moved, N_PROJ - 2)
            pe.wait_ge(lf_in, 16 * SEQS * PAGES)
            for hh in range(HEADS):
                t = pe.transpose(ps[:, 1, 64 * hh:64 * hh + 64], lf_rows[:, hh:PAGE * HEADS:HEADS], ident[0:64, 0:64])
            t.then_inc(lft_ready, 1)

            def tokens(n):
                at, tt = (FK, MK, FV, MV)[n // 3], n % 3
                after(pe, (toka_moved, tokv_moved)[n % 2], (n - 2) // 2)
                for p in range(PAIRS):
                    t = pe.transpose(ps[0:NT[tt], 4 + n % 4, p * P:p * P + P],
                                     proj[:, at + p, tt * P:tt * P + NT[tt]], ident)
                t.then_inc(tok_ready, 1)

            pe.wait_ge(tile_moved, N_PROJ)
            for n in range(4):
                tokens(n)
            pe.wait_ge(wff_lo, 1)
            for k in range(KD):
                t = product(ps[0:HEADS, 0, 0:TOK], [wff_h[:, k, :], wff_l[:, k, :]], [x[:, k, :] for x in h],
                            k == 0, k == KD - 1)
            t.then_inc(ff_ready, 1)

            for n in range(4, 12):
                tokens(n)
            pe.wait_ge(tables_in, 16)
            pe.wait_ge(lfsum_made, 1)
            for bp in range(BP):
                out = ps[:, 3, bp * P:bp * P + P]
                flat = [lf_sum[:, n, 2 * bp:2 * bp + 2, :].rearrange("p b c -> p (b c)") for n in range(2)]
                mm(out, flat[0], const[:, C_TRI:C_TRI + P], start=True, stop=False)
                t = mm(out, flat[1], const[:, C_ONES:C_ONES + P], start=False, stop=True)
            t.then_inc(suffix_ready, 1)
            pe.wait_ge(logf_made, 1)
            for tt in range(3):
                t = pe.transpose(ps[0:NT[tt], 2, 8 * tt:8 * tt + HEADS], forget[:, 1, tt * P:tt * P + NT[tt]],
                                 ident[0:HEADS, 0:HEADS])
            t.then_inc(logft_ready, 1)

            pe.wait_ge(cum_made, 1)
            pe.wait_ge(toka_moved, 6)
            pe.wait_ge(tokv_moved, 6)

            def prompt_scores(n):
                kind, hh = n // HEADS, n % HEADS
                q, k = ((FQ, FK), (MQ, MK))[kind]
                r = slice(HD * (hh % 2), HD * (hh % 2) + HD)
                for qt, at in ((0, 0), (1, P)):
                    keys = P * (qt + 1)
                    out = ps[:, n % 2, at:at + keys]
                    t = mm(out, proj[r, q + hh // 2, qt * P:qt * P + P], proj[r, k + hh // 2, 0:keys],
                           start=True, stop=kind == 1)
                    if kind == 0:
                        t = mm(out, const[0:HEADS, C_IDENT + hh:C_IDENT + hh + 1].to_broadcast([HEADS, P]),
                               ncum[:, 0:keys], start=False, stop=True)
                t.then_inc(ps_ready, 1)

            def with_ada(chunks):
                for i in chunks:
                    ada(ADA2[i])
                    if i:
                        spread(ADA2[i - 1])

            prompt_scores(0)
            prompt_scores(1)
            for n in range(2 * HEADS):
                kind, hh = n // HEADS, n % HEADS
                with_ada(WITH_HEAD[n][:1])
                if n == 0:
                    pe.wait_ge(suffix_made, 1)
                    pe.wait_ge(logft_moved, 1)
                pe.wait_ge(pnorm_made, n + 1)
                after(pe, ppt_moved, n - 1)
                base = 384 * (n % 2)
                for b, at in enumerate((0, P, 2 * P)):
                    t = pe.transpose(ps[:, 2 + n % 2, b * P:b * P + P], probs[:, base + at:base + at + P], ident)
                t.then_inc(ppt_ready, 1)
                if n + 2 < 2 * HEADS:
                    prompt_scores(n + 2)
                with_ada(WITH_HEAD[n][1:])
                pe.wait_ge(ppt_moved, n + 1)
                if hh % 2 == 0:
                    after(pe, py_moved, n // 2 - 1)
                bank, r = 4 + 3 * ((n // 2) % 2), HD * (hh % 2)
                pt = probs_t[:, 3 * (n % 2):3 * (n % 2) + 3, :]
                mm(ps[r:r + HD, bank, 0:TP], v_tok[:, kind, 0, HD * hh:HD * hh + HD],
                   pt[:, 0:2, :].rearrange("p a b -> p (a b)"), start=True, stop=True)
                t = mm(ps[r:r + HD, bank, P:TP], v_tok[:, kind, 1, HD * hh:HD * hh + HD], pt[:, 2, :],
                       start=False, stop=True, skip_group_check=True)
                if hh % 2:
                    t.then_inc(py_ready, 1)

            def move_free(stage, position):
                if position >= 3 and stage is not None:
                    e = EVACS[position - 3]
                    pe.wait_ge(moved_a if e == "A" else moved_v, evacs(stage, position - 3, e))
                elif stage is not None:
                    for e, s in (("A", moved_a), ("V", moved_v)):
                        pe.wait_ge(s, stage * PER[e] + BEFORE[e])

            def first_free(position):
                if position >= 3:
                    e = EVACS[position - 3]
                    pe.wait_ge(moved_a if e == "A" else moved_v, EVACS[:position - 2].count(e))

            def transpose_k(stage, u):
                position = 0
                for par in range(2):
                    pe.wait_ge(k_in[par], u * (16 * PAGES) + 16 * PAGES)
                    for p in range(PAIRS):
                        for half in range(2):
                            if stage is None:
                                first_free(position)
                            else:
                                move_free(stage, position)
                            for g in range(4):
                                t = pe.transpose(ps[:, 3 + position % 3, g * P:g * P + P],
                                                 k_pages[par][:, 4 * half + g, p * P:p * P + P], ident)
                            t.then_inc(t_ready, 1)
                            position += 1

            def scores(bp, kind, u):
                pe.wait_ge(q_built, u + 1)
                if kind == 0:
                    pe.wait_ge(bias_built, bp + 1)
                pe.wait_ge(moved_a, u * PER["A"] + BEFORE["A"])
                pe.wait_ge(moved_v, u * PER["V"] + BEFORE["V"])
                knew = (FK, MK)[kind]
                q = qblk[kind][:, :, :, :].rearrange("p a b c -> p (a b c)")
                for c in range(3):
                    for p in range(PAIRS):
                        for par in range(2):
                            out = ps[64 * par:64 * par + 64, c, 0:512 if c < 2 else TSA]
                            keys = k_t[:, par, p, c * 512:c * 512 + 512] if c < 2 else proj[:, knew + p, TP:TOK]
                            t = mm(out, q[:, 192 * par + 48 * p:192 * par + 48 * p + 64], keys,
                                   start=p == 0, stop=p == PAIRS - 1 and kind == 1)
                    if kind == 0:
                        for par in range(2):
                            out = ps[64 * par:64 * par + 64, c, 0:512 if c < 2 else TSA]
                            t = mm(out, selb[par], bias_r[:, c * 512:c * 512 + (512 if c < 2 else TSA)],
                                   start=False, stop=True)
                t.then_inc(s_ready, 1)

            def transpose_p(stage, u, last):
                pe.wait_ge(exp_made, u + 1)
                for position in (12, 13, 14):
                    bank = 3 + position % 3
                    if position < 14:
                        move_free(stage, position - 12 if last else position)
                        for g in range(4):
                            at = (4 * (position - 12) + g) * P
                            if position == 13 and g == 3:
                                move_free(stage, 2 if last else 14)
                            t = pe.transpose(ps[:, bank, g * P:g * P + P], probs[:, at:at + P], ident)
                    else:
                        t = pe.transpose(ps[0:TSA, bank, 0:P], probs[:, PAST:PAST + TSA], ident)
                    t.then_inc(t_ready, 1)

            def values(stage, kind, u, last):
                if last:
                    pe.wait_ge(moved_a, stage * PER["A"] + BEFORE["A"] + 1)
                    pe.wait_ge(moved_v, stage * PER["V"] + BEFORE["V"] + 2)
                else:
                    pe.wait_ge(moved_a, evacs(stage, 14, "A"))
                    pe.wait_ge(moved_v, evacs(stage, 14, "V"))
                if not (isinstance(u, int) and u == 0):
                    pe.wait_ge(yrow_made, u)
                for page in range(PAGES):
                    if page % 2 == 0:
                        pe.wait_ge(v_in[page // 2], u * 64 + 64)
                    for par in range(2):
                        t = mm(ps[64 * par:64 * par + 64, 6, 0:AW], probs_t[:, page, 64 * par:64 * par + 64],
                               v_pages[:, par, page, :], start=page == 0, stop=False)
                    if page % 2:
                        t.then_inc(v_read, 1)
                for par in range(2):
                    t = mm(ps[64 * par:64 * par + 64, 6, 0:AW], probs_t[0:TSA, PAGES, 64 * par:64 * par + 64],
                           v_tok[0:TSA, kind, 2, :], start=False, stop=True)
                t.then_inc(pv_ready, 1)

            def transpose_y(u):
                pe.wait_ge(yrow_made, u + 1)
                after(pe, yt_moved, u)
                for p in range(PAIRS):
                    t = pe.transpose(ps[:, 7, ROWS * p:ROWS * p + ROWS], y_row[0:ROWS, p * P:p * P + P],
                                     ident[0:ROWS, 0:ROWS])
                t.then_inc(yt_ready, 1)

            selb = [const[:, C_SELB + 64 * par:C_SELB + 64 * par + 64] for par in range(2)]
            spread(ADA2[-1])
            pe.wait_ge(py_moved, HEADS)
            pe.wait_ge(mods_made, N_ADA1 + N_ADA2)
            transpose_k(None, 0)

            def units(bp, first, last):
                for kind in range(2):
                    u = bp * 2 + kind
                    scores(bp, kind, u)
                    if not (first and kind == 0):
                        transpose_y(u - 1)
                    end = last and kind == 1
                    if not end:
                        transpose_k(u, u + 1)
                    transpose_p(u, u, end)
                    values(u, kind, u, end)

            units(0, True, False)
            with pe.Fori(1, BP - 1) as bp:
                units(bp, False, False)
            units(BP - 1, False, True)
            transpose_y(2 * BP - 1)

            def project_step(c, x, k_of, start, stop):
                pe.wait_ge(lo_made, c.n + 1)
                if x[0] is act_h:
                    pe.wait_ge(actl_made, k_of + 2)
                for kk in range(2):
                    for m in range(KD):
                        at = kk * D + m * P
                        t = product(ps[:, m, 0:TOK], [w[c.slot][:, at:at + P] for w in (w_h, w_l)],
                                    [y[:, bass.ds(k_of + kk, 1), :].rearrange("p o t -> p (o t)") for y in x],
                                    start and kk == 0, stop and kk == 1)
                t.then_inc(w_used, 1)

            def back_to_tokens(n):
                pe.wait_ge(outa_moved, 4 * n + 4)
                pe.wait_ge(outv_moved, 4 * n + 4)
                for tt in range(3):
                    for k in range(KD):
                        t = pe.transpose(ps[0:NT[tt], 2 * tt + k // 4, (k % 4) * P:(k % 4) * P + P],
                                         y_t[:, k, tt * P:tt * P + NT[tt]], ident)
                    t.then_inc(back_ready, 1)

            pe.wait_ge(mixl_made, 3)
            pe.wait_ge(yt_moved, 2 * BP)
            for k in range(N_O):
                project_step(Chunk(AT_O, 0, k), (h_h, h_l), 2 * k, k == 0, k == N_O - 1)
            back_to_tokens(0)
            to_features()

            pe.wait_ge(hl_made, BLK + 6)

            def up_step(c):
                pe.wait_ge(lo_made, c.n + 1)
                product_tiles(c, 2 * c.raw, N_PROJ)
            ring(pe, AT_UP, N_UP, up_step)
            pe.wait_ge(tile_moved, N_PROJ + 2 * N_UP)
            x = (act_h, act_l)
            project_step(Chunk(AT_DOWN, 0, 0), x, 0, True, False)
            with pe.Fori(0, N_DOWN // 2 - 1) as i:
                for k in (1, 2):
                    c = Chunk(AT_DOWN, 0, k)
                    c.n = i * 2 + (AT_DOWN + k)
                    project_step(c, x, i * 4 + 2 * k, False, False)
            for k in (N_DOWN - 2, N_DOWN - 1):
                project_step(Chunk(AT_DOWN, 0, k), x, 2 * k, False, k == N_DOWN - 1)
            back_to_tokens(1)

        @block.scalar
        def _(act):
            cp = ACT.Copy
            do = act.activation
            link = Chain(act, act_link).link

            def round_hi(c, n):
                act.wait_ge(raw_in[c.raw], c.loads * 32)
                after(act, w_used, c.n - 1)
                do(w_h[c.slot][:, 0:n], raw[c.raw][:, 0:n], cp).then_inc(hi_made, 1)

            act.wait_ge(c_in, 32)
            do(c_silu[:, :], c_rows[:, :], ACT.Silu).then_inc(silu_made, 1)
            act.wait_ge(ct_copied, 1)
            ct3 = c_t[:, :].rearrange("p (k b) -> p k b", k=KD)
            do(ch[:, :, 0:9], ct3, cp).then_inc(ch_hi, 1)

            def ada_mods(d):
                act.wait_ge(ex_ready, d.a + 1)
                do(mods[:, d.part, :, d.block * CH:d.block * CH + CH],
                   ps[:, d.spread_bank, :].rearrange("p (a c) -> p a c", a=2), cp,
                   bias=0.0 if d.part in (SH_A, SH_F) else 1.0).then_inc(mods_made, 1)

            def block_hi(b):
                act.wait_ge(ht_ready, b + 1)
                do(h_h[:, 2 * b:2 * b + 2, :], ps[:, 4 + 2 * b % 4:6 + 2 * b % 4, 0:TOK], cp).then_inc(hh_made, 1)

            for d in ADA1:
                round_hi(d.chunk, KD * CH)
                if d.a >= 3:
                    ada_mods(ADA1[d.a - 3])
                if d.a == 7:
                    block_hi(0)
            ada_mods(ADA1[-3])
            ada_mods(ADA1[-2])
            block_hi(1)
            ada_mods(ADA1[-1])
            block_hi(BLK - 2)
            round_hi(Chunk(AT_IN, 0, 0), KD * CH)
            block_hi(BLK - 1)

            def features_hi():
                for tt in range(3):
                    for half in range(2):
                        act.wait_ge(ht_ready, BLK + 2 * tt + half + 1)
                        do(h_h[:, 4 * half:4 * half + 4, tt * P:tt * P + NT[tt]],
                           ps[:, 2 * tt + half, :].rearrange("p (k t) -> p k t", k=4)[:, :, 0:NT[tt]],
                           cp).then_inc(hh_made, 1)

            act.wait_ge(small_in, 48)
            do(wff_h[:, :, :], wff[:, :, :], cp).then_inc(wff_hi, 1)

            def move_tiles(c, bank):
                for m in range(2):
                    act.wait_ge(w_used if m else tile_ready, c.n + 1 if m else c.j + 1)
                    do(proj[:, bass.ds(c.j * 2 + m, 1), :].rearrange("p o t -> p (o t)"),
                       ps[:, bank + m, 0:TOK], cp).then_inc(tile_moved, 1)

            some = SEQS * PAGES // 2 // (N_IN - 4)
            for j in range(1, N_IN):
                c = Chunk(AT_IN, j // 4, j % 4)
                round_hi(c, KD * CH)
                for n in range(some * (j - 4), some * (j - 3)) if j >= 4 else ():
                    load_logf(act, SEQS * PAGES // 2 + n)
                move_tiles(c.before(), 2 * c.before().raw)
            last = Chunk(AT_IN, N_IN // 4 - 1, 3)
            move_tiles(last, 2 * last.raw)
            round_hi(ADA2[0].chunk, KD * CH)

            def take_tokens(n):
                act.wait_ge(tok_ready, n + 1)
                dst, kind, tt = token_tiles[n]
                do(dst[0:NT[tt], kind, tt, :], ps[0:NT[tt], 4 + n % 4, 0:AW], cp).then_inc(toka_moved, 1)

            take_tokens(0)
            take_tokens(2)
            take_tokens(4)
            act.wait_ge(absz_made, 1)
            do(forget[:, 2, :], forget[:, 1, :], ACT.Exp, scale=-1.0).then_inc(act_step, 1)
            act.wait_ge(act_step, 1)
            do(forget[:, 3, :], forget[:, 2, :], ACT.Ln, bias=1.0).then_inc(softplus_made, 1)
            for n in range(6, 12, 2):
                take_tokens(n)

            def prompt_exp(n):
                act.wait_ge(pnb_made, n + 1)
                after(act, ppt_ready, n - 1)
                for qt, at, w in ((0, 0, P), (1, P, TP)):
                    t = do(probs[:, 384 * (n % 2) + at:384 * (n % 2) + at + w], ps[:, n % 2, at:at + w], ACT.Exp,
                           bias=p_nb[:, n, qt:qt + 1], scale=SCALE, accum_out=p_sum[:, n, qt:qt + 1])
                t.then_inc(pexp_made, 1)

            def next_hi(chunks):
                for i in chunks:
                    if i + 1 < N_ADA2:
                        round_hi(ADA2[i + 1].chunk, KD * CH)

            prompt_exp(0)
            for n in range(2 * HEADS):
                next_hi(WITH_HEAD[n][:1])
                if n + 1 < 2 * HEADS:
                    prompt_exp(n + 1)
                act.wait_ge(ppt_ready, n + 1)
                do(probs_t[:, 3 * (n % 2):3 * (n % 2) + 3, :],
                   ps[:, 2 + n % 2, 0:384].rearrange("p (b q) -> p b q", b=3), cp).then_inc(ppt_moved, 1)
                next_hi(WITH_HEAD[n][1:])
                for i in WITH_HEAD[n]:
                    if i:
                        ada_mods(ADA2[i - 1])
                if n % 2:
                    act.wait_ge(py_ready, n // 2 + 1)
                    q = (FQ, MQ)[n // HEADS] + (n % HEADS) // 2
                    do(proj[:, q, 0:TP], ps[:, 4 + 3 * ((n // 2) % 2), 0:TP], cp).then_inc(py_moved, 1)

            def move(position, stage_ready):
                act.wait_ge(t_ready, stage_ready)
                bank = 3 + position % 3
                if position < 12:
                    par, p, half = position // 6, position % 6 // 2, position % 2
                    do(k_t[:, par, p, 512 * half:512 * half + 512], ps[:, bank, :], cp).then_inc(moved_a, 1)
                else:
                    g = 4 * (position - 12)
                    do(probs_t[:, g:g + 4, :], ps[:, bank, :].rearrange("p (g r) -> p g r", g=4), cp)\
                        .then_inc(moved_a, 1)

            ada_mods(ADA2[-1])
            for position in range(12):
                if EVACS[position] == "A":
                    move(position, position + 1)

            def unit_exp(kind, u):
                act.wait_ge(stats_made, u + 1)
                do(probs[:, :], probs[:, :] if kind else psf[:, 0:PAST + TSA], ACT.Exp, bias=u_nb[:, 0:1], scale=SCALE,
                   accum_out=u_sum[:, 0:1]).then_inc(exp_made, 1)

            def unit(kind, u, last):
                base = u * 15 + (12 + 1)
                if not last:
                    for position in range(6):
                        move(position, base + position)
                unit_exp(kind, u)
                if not last:
                    move(8, base + 8)
                    move(10, base + 10)
                move(13, base + (1 if last else 13))
                if last:
                    for k in range(2):
                        round_hi(Chunk(AT_O, 0, k), 2 * D)
                act.wait_ge(pv_ready, u + 1)
                act.wait_ge(inv_made, u + 1)
                do(y_row[:, :], ps[:, 6, 0:AW], cp, scale=u_inv[:, 0:1]).then_inc(yrow_made, 1)

            unit(0, 0, False)
            unit(1, 1, False)
            with act.Fori(1, BP - 1) as bp:
                unit(0, bp * 2, False)
                unit(1, bp * 2 + 1, False)
            unit(0, 2 * BP - 2, False)
            unit(1, 2 * BP - 1, True)

            act.wait_ge(yt_moved, 2 * BP)
            for at, frm, n in ((0, CB, 2), (2, FQ, 3), (5, MQ, 3)):
                do(h_h[:, at:at + n, :], proj[:, frm:frm + n, :], cp).then_inc(mixh_made, 1)
            for k in range(2, N_O):
                round_hi(Chunk(AT_O, 0, k), 2 * D)

            def move_out(n):
                act.wait_ge(w_used, (AT_UP, AT_DOWN + N_DOWN)[n])
                for m in range(0, KD, 2):
                    do(y_t[:, m, :], ps[:, m, 0:TOK], cp).then_inc(outa_moved, 1)

            move_out(0)

            def norm(n):
                for tt in range(3):
                    act.wait_ge(res_made, 3 * n + tt + 1)
                    r = slice(0, NT[tt])
                    row, x, s = ln_rows[r, tt, :], xt[r, tt, :], ln_s[r, tt, :]
                    link(do(s[:, 1:2], s[:, 0:1], cp, scale=-1.0 / D))
                    link(do(ln_waste[r, :], row, ACT.Square, bias=s[:, 1:2], accum_out=s[:, 2:3]))
                    do(s[:, 3:4], s[:, 2:3], ACT.Sqrt, scale=1.0 / D, bias=eps[r, 0:1]).then_inc(std_made, 1)
                    if n == 0 or tt == 0:
                        act.wait_ge(stat_made, 3 * n + tt + 1)
                        do(x, row, ACT.Identity, scale=s[:, 4:5], bias=s[:, 5:6]).then_inc(normed, 1)

            for k in range(2):
                round_hi(Chunk(AT_UP, 0, k), KD * CH)
            act.wait_ge(eps_set, 1)
            do(ln_s[:, 0, 3:4], eps[:, :], ACT.Sqrt)
            norm(0)
            features_hi()

            def conv_in(c):
                e = ext[c.slot]
                after(act, conv_made, c.j - 1)
                after(act, last_kept, c.j - 1)
                for m in range(2):
                    act.wait_ge(w_used if m else tile_ready, c.n + 1 if m else c.j + (N_IN + 1))
                    bank = 2 * c.raw + m
                    do(e[:, m, 2:2 + TP], ps[:, bank, 0:TP], cp).then_inc(ext_moved, 1)
                    do(e[:, m, 258:338].rearrange("p (b t) -> p b t", b=SEQS)[:, :, 2:10],
                       ps[:, bank, TP:TOK].rearrange("p (b t) -> p b t", b=SEQS), cp).then_inc(tile_moved, 1)

            def first_tap(c):
                e, acc = ext[c.slot], acc2[c.slot]
                act.wait_ge(past_in, c.j + 1)
                act.wait_ge(tile_moved, c.j * 2 + (N_PROJ + 2))
                act.wait_ge(ext_moved, c.j * 2 + 2)
                after(act, actf_made, c.j - 1)
                for m in range(2):
                    tile = st_t[:, bass.ds(c.j + m * FT, 1), :].rearrange("p o r -> p (o r)")
                    t = do(acc[:, m, :], e[:, m, 0:336], ACT.Identity, scale=tile[:, 16:17], bias=tile[:, 19:20])
                t.then_inc(tap_made, 1)

            def silu_gate(c):
                act.wait_ge(conv_made, c.j + 1)
                acc = acc2[c.slot]
                do(acc[:, 0, :], acc[:, 0, :], ACT.Silu).then_inc(gate_made, 1)

            def act_hi(c):
                act.wait_ge(actf_made, c.j + 1)
                do(act_h[:, bass.ds(c.j, 1), :].rearrange("p o t -> p (o t)"), act_f[:, :], cp).then_inc(acth_made, 1)

            def ffn_act(c):
                first = isinstance(c.j, int) and c.j == 0
                if not first:
                    silu_gate(c.before())
                conv_in(c)
                first_tap(c)
                if not first:
                    act_hi(c.before())

            def up_step(c):
                round_hi(c, KD * CH)
                ffn_act(c.before().before())
            ring(act, AT_UP, N_UP, up_step, done=2)
            last = Chunk(AT_UP, N_UP // 4, N_UP % 4 - 1)
            for k, c in enumerate((last.before(), last)):
                round_hi(Chunk(AT_DOWN, 0, k), 2 * D)
                ffn_act(c)
            silu_gate(last)
            act_hi(last)
            ring(act, AT_DOWN, N_DOWN, lambda c: round_hi(c, 2 * D), done=2)
            move_out(1)
            do(ln_s[:, 0, 3:4], eps[:, :], ACT.Sqrt)
            norm(1)

        @block.vector
        def _(dve):
            chain = Chain(dve, dve_step)
            link = chain.link
            stt = dve.scalar_tensor_tensor

            def make_lo(c, n):
                dve.wait_ge(hi_made, c.n + 1)
                after(dve, w_used, c.n - 1)
                dve.tensor_sub(w_l[c.slot][:, 0:n], raw[c.raw][:, 0:n], w_h[c.slot][:, 0:n].bitcast(F32))\
                    .then_inc(lo_made, 1)

            dve.wait_ge(ct_ready, 1)
            dve.tensor_copy(c_t[:, :], ps[:, 6, 0:KD * 9]).then_inc(ct_copied, 1)
            ct3 = c_t[:, :].rearrange("p (k b) -> p k b", k=KD)
            dve.wait_ge(ct_copied, 1)
            dve.wait_ge(ch_hi, 1)
            dve.tensor_sub(ch[:, :, 9:18], ct3, ch[:, :, 0:9].bitcast(F32)).then_inc(ch_lo, 1)

            def ada_rows(d):
                dve.wait_ge(w_used, d.chunk.n + 1)
                dve.wait_ge(bias_in[d.a % 4], 16 * (d.a // 4 + 1))
                after(dve, ex_ready, d.a - 1)
                dve.tensor_add(ada_row[d.a % 2][:, :], ps[0:18, d.bank, 0:CH], b_ada[d.a % 4][:, :])\
                    .then_inc(ada_made, 1)

            def block_lo(b):
                dve.wait_ge(hh_made, b + 1)
                dve.tensor_sub(h_l[:, 2 * b:2 * b + 2, :], ps[:, 4 + 2 * b % 4:6 + 2 * b % 4, 0:TOK],
                               h_h[:, 2 * b:2 * b + 2, :].bitcast(F32)).then_inc(hl_made, 1)

            for d in ADA1:
                make_lo(d.chunk, KD * CH)
                if d.a:
                    ada_rows(ADA1[d.a - 1])
                if d.a == 7:
                    block_lo(0)
            ada_rows(ADA1[-1])
            block_lo(1)
            at = slice(D - CH, D)
            dve.wait_ge(mods_made, N_ADA1)
            for tt in range(3):
                t = dve.tensor_mul(rows[0:NT[tt], tt, at], xt[0:NT[tt], tt, at], mods[0:NT[tt], SC_A, PR[tt], at])
            link(t)
            dve.wait_ge(rows_made, BLK - 1)
            for tt in range(3):
                t = dve.tensor_add(rows[0:NT[tt], tt, at], rows[0:NT[tt], tt, at], mods[0:NT[tt], SH_A, PR[tt], at])
            t.then_inc(rows_made, 1)
            block_lo(BLK - 2)
            make_lo(Chunk(AT_IN, 0, 0), KD * CH)
            block_lo(BLK - 1)

            def features_lo():
                for tt in range(3):
                    for half in range(2):
                        dve.wait_ge(hh_made, BLK + 2 * tt + half + 1)
                        s = (slice(None), slice(4 * half, 4 * half + 4), slice(tt * P, tt * P + NT[tt]))
                        dve.tensor_sub(h_l[s], ps[:, 2 * tt + half, :].rearrange("p (k t) -> p k t", k=4)
                                       [:, :, 0:NT[tt]], h_h[s].bitcast(F32)).then_inc(hl_made, 1)

            dve.wait_ge(wff_hi, 1)
            dve.tensor_sub(wff_l[:, :, :], wff[:, :, :], wff_h[:, :, :].bitcast(F32)).then_inc(wff_lo, 1)
            u_s = u_ext[:, :, 258:338].rearrange("p c (b t) -> p c b t", b=SEQS)

            def short_conv(c):
                dve.tensor_copy(u_s[:, c, :, 0:2], st_t[:, 44 + c, 0:16].rearrange("p (b r) -> p b r", r=2))
                dve.tensor_mul(u_s[:, c, :, 2:10], proj[:, CC + c, TP:TOK].rearrange("p (b t) -> p b t", b=SEQS),
                               proj[:, CX + c, TP:TOK].rearrange("p (b t) -> p b t", b=SEQS))
                link(dve.tensor_mul(u_ext[:, c, 2:258], proj[:, CC + c, 0:TP], proj[:, CX + c, 0:TP]))
                link(dve.tensor_scalar(u_acc[:, c, :], u_ext[:, c, 0:336], st_t[:, 44 + c, 16:17], None, ALU.mult))
                for j in (1, 2):
                    link(stt(u_acc[:, c, :], u_ext[:, c, j:j + 336], st_t[:, 44 + c, 16 + j:17 + j], u_acc[:, c, :],
                             ALU.mult, ALU.add))
                dve.tensor_mul(proj[:, CB + c, 0:TP], proj[:, CB + c, 0:TP], u_acc[:, c, 0:TP])
                new = proj[:, CB + c, TP:TOK].rearrange("p (b t) -> p b t", b=SEQS)
                got = u_acc[:, c, 256:336].rearrange("p (b t) -> p b t", b=SEQS)[:, :, 2:10]
                dve.tensor_mul(new, new, got)
                dve.tensor_copy(conv_last[:, c, 0:16].rearrange("p (b r) -> p b r", r=2), u_s[:, c, :, 8:10])
                link(dve.tensor_copy(conv_last[:, c, 16:18], u_ext[:, c, 256:258]))

            for j in range(1, N_IN):
                make_lo(Chunk(AT_IN, j // 4, j % 4), KD * CH)
                if j == N_IN - 5:
                    dve.wait_ge(state_in, 16 * 4 * 5)
                    dve.transpose(st_t[:, :, :], state_raw[:, :, :]).then_inc(dve_misc, 1)
                    dve.wait_ge(dve_misc, 1)
                    link(dve.memset(u_ext[:, :, 0:2], 0.0))
                if j == N_IN - 4:
                    dve.wait_ge(tile_moved, CX + 2)
                    short_conv(0)
                if j == N_IN - 3:
                    short_conv(1)
                    dve.transpose(conv_last_t[:, :, :], conv_last[:, :, :]).then_inc(convlast_made, 1)

            def take_tokens(n):
                dve.wait_ge(tok_ready, n + 1)
                dst, kind, tt = token_tiles[n]
                dve.tensor_copy(dst[0:NT[tt], kind, tt, :], ps[0:NT[tt], 4 + n % 4, 0:AW]).then_inc(tokv_moved, 1)

            take_tokens(1)
            take_tokens(3)
            make_lo(ADA2[0].chunk, KD * CH)
            dve.wait_ge(tables_in, 16)

            dve.wait_ge(lfsum_zeroed, 1)
            dve.wait_ge(lft_ready, 1)
            lf = [lf_sum[:, n, :, 0:PAGES * HEADS].rearrange("p b (g h) -> p b g h", h=HEADS) for n in range(2)]
            for hh in range(HEADS):
                t = dve.tensor_copy(lf[0][:, :, :, hh],
                                    ps[:, 1, 64 * hh:64 * hh + 64].rearrange("p (b g) -> p b g", g=PAGES))
            link(t)
            dve.wait_ge(ff_ready, 1)
            link(dve.tensor_scalar(forget[:, 0, :], ps[0:HEADS, 0, 0:TOK], b_f[:, 0:1], None, ALU.add))
            stt(forget[:, 1, :], forget[:, 0, :], -1.0, forget[:, 0, :], ALU.mult, ALU.max).then_inc(absz_made, 1)
            for g in range(PAGES - 2, -1, -1):
                t = dve.tensor_add(lf[1][:, :, g, :], lf[1][:, :, g + 1, :], lf[0][:, :, g + 1, :])
                if g:
                    link(t)
            t.then_inc(lfsum_made, 1)
            take_tokens(5)
            take_tokens(7)
            dve.wait_ge(softplus_made, 1)
            stt(forget[:, 1, :], forget[:, 0, :], 0.0, forget[:, 3, :], ALU.min, ALU.subtract).then_inc(logf_made, 1)
            dve.wait_ge(logf_made, 1)
            link(dve.tensor_tensor_scan(forget[:, 2, :], const[0:HEADS, C_SCAN:C_SCAN + TOK], forget[:, 1, :], 0.0,
                                        ALU.mult, ALU.add))
            dve.tensor_scalar(ncum[:, :], forget[:, 2, :], -1.0 / SCALE, None, ALU.mult).then_inc(cum_made, 1)
            for n in (9, 11):
                take_tokens(n)
            dve.wait_ge(suffix_ready, 1)
            dve.tensor_copy(c_suffix[:, :, :], ps[:, 3, :].rearrange("p (b s) -> p b s", b=BP))\
                .then_inc(suffix_made, 1)
            dve.wait_ge(logft_ready, 1)
            for tt in range(3):
                t = dve.tensor_copy(lf_out[0:NT[tt], tt, :], ps[0:NT[tt], 2, 8 * tt:8 * tt + HEADS])
            t.then_inc(logft_moved, 1)
            dve.wait_ge(cum_made, 1)
            dve.wait_ge(newbias_zeroed, 1)
            for par in range(2):
                t = dve.tensor_copy(bias_r[64 * par:64 * par + HEADS, PAST:PAST + TSA], ncum[:, TP:TOK])
                t.then_inc(newbias_made, 1)

            def prompt_stats(n):
                kind, hh = n // HEADS, n % HEADS
                dve.wait_ge(ps_ready, n + 1)
                s = ps[:, n % 2, :]
                if kind == 0:
                    v = s[:, 0:384].rearrange("p (b k) -> p b k", b=3)[:, 0:3:2, :]
                    mask = const[:, C_DIAG:C_DIAG + P].unsqueeze(1).to_broadcast([P, 2, P])
                    link(dve.tensor_add(v, v, mask))
                else:
                    sl = float(slopes()[hh] / SCALE)
                    stt(s[:, 0:P], const[:, C_ALIBI + P:C_ALIBI + 2 * P], sl, s[:, 0:P], ALU.mult, ALU.add)
                    link(stt(s[:, P:3 * P], const[:, C_ALIBI:C_ALIBI + 2 * P], sl, s[:, P:3 * P], ALU.mult, ALU.add))
                dve.tensor_reduce(p_max[:, n, 0:1], s[:, 0:P], AX.X, ALU.max)
                link(dve.tensor_reduce(p_max[:, n, 1:2], s[:, P:3 * P], AX.X, ALU.max))
                dve.tensor_scalar(p_nb[:, n, :], p_max[:, n, :], -SCALE, None, ALU.mult).then_inc(pnb_made, 1)

            prompt_stats(0)
            for n in range(2 * HEADS):
                if n + 1 < 2 * HEADS:
                    prompt_stats(n + 1)
                dve.wait_ge(pexp_made, n + 1)
                link(dve.reciprocal(p_inv[:, n, :], p_sum[:, n, :]))
                base = 384 * (n % 2)
                dve.tensor_scalar(probs[:, base:base + P], probs[:, base:base + P], p_inv[:, n, 0:1], None, ALU.mult)
                dve.tensor_scalar(probs[:, base + P:base + 384], probs[:, base + P:base + 384], p_inv[:, n, 1:2], None,
                                  ALU.mult).then_inc(pnorm_made, 1)
                for i in WITH_HEAD[n]:
                    if i + 1 < N_ADA2:
                        make_lo(ADA2[i + 1].chunk, KD * CH)
                    ada_rows(ADA2[i])

            def move(position, stage_ready):
                dve.wait_ge(t_ready, stage_ready)
                bank = 3 + position % 3
                if position < 12:
                    par, p, half = position // 6, position % 6 // 2, position % 2
                    dve.tensor_copy(k_t[:, par, p, 512 * half:512 * half + 512], ps[:, bank, :]).then_inc(moved_v, 1)
                elif position == 12:
                    dve.tensor_copy(probs_t[:, 0:4, :], ps[:, bank, :].rearrange("p (g r) -> p g r", g=4))\
                        .then_inc(moved_v, 1)
                else:
                    dve.tensor_copy(probs_t[0:TSA, PAGES, :], ps[0:TSA, bank, 0:P]).then_inc(moved_v, 1)

            for position in range(12):
                if EVACS[position] == "V":
                    move(position, position + 1)

            def unit_stats(bp, kind, u):
                dve.wait_ge(s_ready, u + 1)
                new = psf[:, PAST:PAST + TSA]
                at = (C_FOXNEW, C_MOBANEW)[kind]
                mask = const[:, bass.ds(bp * TSA + at, TSA)]
                if kind == 0:
                    link(dve.tensor_add(new, new, mask))
                    link(dve.tensor_reduce(u_max[:, 0:1], psf[:, 0:PAST + TSA], AX.X, ALU.max))
                    dve.tensor_scalar(u_nb[:, 0:1], u_max[:, 0:1], -SCALE, None, ALU.mult).then_inc(stats_made, 1)
                    return
                link(dve.tensor_reduce(gates[:, 0:NBLK], psf[:, 0:PAST].rearrange("p (b k) -> p b k", b=NBLK), AX.X,
                                       ALU.add))
                link(dve.tensor_reduce(gates[:, 4:5], gates[:, 0:NBLK], AX.X, ALU.min))
                link(stt(pick[:, 0:NBLK], gates[:, 0:NBLK], gates[:, 4:5], const[:, C_RANK:C_RANK + NBLK],
                         ALU.is_equal, ALU.mult))
                link(dve.tensor_reduce(pick[:, 4:5], pick[:, 0:NBLK], AX.X, ALU.max))
                link(dve.tensor_scalar(pen[:, 0:NBLK], pick[:, 0:NBLK], pick[:, 4:5], NEG, ALU.is_equal, ALU.mult))
                dve.tensor_add(probs[:, PAST:PAST + TSA], new, mask)
                for b in range(NBLK):
                    at = slice(MBLK * b, MBLK * (b + 1))
                    t = stt(probs[:, at], psf[:, at], pen[:, b:b + 1],
                            const[:, C_MOBAPAST + MBLK * b:C_MOBAPAST + MBLK * (b + 1)], ALU.add, ALU.add)
                link(t)
                link(dve.tensor_reduce(u_max[:, 0:1], probs[:, :], AX.X, ALU.max))
                dve.tensor_scalar(u_nb[:, 0:1], u_max[:, 0:1], -SCALE, None, ALU.mult).then_inc(stats_made, 1)

            def take_y(bp, kind):
                q = (FQ, MQ)[kind]
                for half in range(2):
                    r = slice(HD * half, HD * half + HD)
                    src = ps[r, 7, 0:384].rearrange("p (a b c) -> p a b c", a=3, b=2)[:, :, :, TS * half:TS * half + TS]
                    for p in range(PAIRS):
                        t = dve.tensor_copy(proj[r, q + p, bass.ds(bp * (2 * TS) + TP, 2 * TS)]
                                            .rearrange("p (b t) -> p b t", b=2), src[:, p])
                t.then_inc(yt_moved, 1)

            def unit(bp, kind, u, first, last):
                base = u * 15 + (12 + 1)
                unit_stats(bp, kind, u)
                if not first:
                    dve.wait_ge(yt_ready, u)
                    take_y(bp if kind else bp - 1, 1 - kind)
                if not last:
                    for position in (6, 7, 9, 11):
                        move(position, base + position)
                dve.wait_ge(exp_made, u + 1)
                dve.reciprocal(u_inv[:, 0:1], u_sum[:, 0:1]).then_inc(inv_made, 1)
                move(12, base + (0 if last else 12))
                move(14, base + (2 if last else 14))
                if last:
                    for k in range(2):
                        make_lo(Chunk(AT_O, 0, k), 2 * D)

            LINKS = 2 + 7
            chain.start += chain.k
            chain.k = 0
            chain.enter(0, LINKS)
            unit(0, 0, 0, True, False)
            unit(0, 1, 1, False, False)
            with dve.Fori(1, BP - 1) as bp:
                chain.enter(bp, LINKS)
                unit(bp, 0, bp * 2, False, False)
                unit(bp, 1, bp * 2 + 1, False, False)
            chain.enter(BP - 1, LINKS)
            unit(BP - 1, 0, 2 * BP - 2, False, False)
            unit(BP - 1, 1, 2 * BP - 1, False, True)
            chain.close(BP)
            dve.wait_ge(yt_ready, 2 * BP)
            take_y(BP - 1, 1)

            for n, (at, frm, cnt) in enumerate(((0, CB, 2), (2, FQ, 3), (5, MQ, 3))):
                dve.wait_ge(mixh_made, n + 1)
                dve.wait_ge(yt_moved, 2 * BP)
                dve.tensor_sub(h_l[:, at:at + cnt, :], proj[:, frm:frm + cnt, :],
                               h_h[:, at:at + cnt, :].bitcast(F32)).then_inc(mixl_made, 1)
            for k in range(2, N_O):
                make_lo(Chunk(AT_O, 0, k), 2 * D)

            def move_out(n):
                dve.wait_ge(w_used, (AT_UP, AT_DOWN + N_DOWN)[n])
                for m in range(1, KD, 2):
                    dve.tensor_copy(y_t[:, m, :], ps[:, m, 0:TOK]).then_inc(outv_moved, 1)

            move_out(0)

            def residual(n, tt, gate):
                r = slice(0, NT[tt])
                dve.wait_ge(back_ready, 3 * n + tt + 1)
                row = ln_rows[r, tt, :]
                link(dve.tensor_mul(row, mods[r, gate, PR[tt], :], psf[r, 1024 * tt:1024 * tt + D]))
                stt(row, xt[r, tt, :], ALPHA, row, ALU.mult, ALU.add, accum_out=ln_s[r, tt, 0:1]).then_inc(res_made, 1)

            def inverse_std(n, tt):
                s = ln_s[0:NT[tt], tt, :]
                dve.wait_ge(std_made, 3 * n + tt + 1)
                link(dve.reciprocal(s[:, 4:5], s[:, 3:4]))
                dve.tensor_mul(s[:, 5:6], s[:, 1:2], s[:, 4:5]).then_inc(stat_made, 1)

            def ffn_rows(tt):
                r = slice(0, NT[tt])
                dve.wait_ge(normed, tt + 1)
                link(dve.tensor_mul(ln_rows[r, tt, :], xt[r, tt, :], mods[r, SC_F, PR[tt], :]))
                dve.tensor_add(ln_rows[r, tt, :], ln_rows[r, tt, :], mods[r, SH_F, PR[tt], :]).then_inc(rows_made, 1)

            dve.wait_ge(gb_made, 1)
            residual(0, 0, GT_A)
            residual(0, 1, GT_A)
            inverse_std(0, 0)
            residual(0, 2, GT_A)
            inverse_std(0, 1)
            ffn_rows(1)
            inverse_std(0, 2)
            ffn_rows(2)
            features_lo()
            dve.wait_ge(lo_made, AT_UP + 1)
            make_lo(Chunk(AT_UP, 0, 1), KD * CH)

            for e in ext:
                t = dve.memset(e[:, :, 0:2], 0.0)
            link(t)
            chain.start += chain.k
            chain.k = 0

            def past_rows(c):
                for m in range(2):
                    src = st_t[:, bass.ds(c.j + m * FT, 1), 0:16].rearrange("p o (b r) -> p (o b) r", r=2)
                    t = dve.tensor_copy(ext[c.slot][:, m, 258:338].rearrange("p (b t) -> p b t", b=SEQS)[:, :, 0:2],
                                        src)
                t.then_inc(past_in, 1)

            def conv(c):
                e, acc = ext[c.slot], acc2[c.slot]
                dve.wait_ge(tap_made, c.j + 1)
                for m in range(2):
                    tile = st_t[:, bass.ds(c.j + m * FT, 1), :].rearrange("p o r -> p (o r)")
                    for j in (1, 2):
                        t = stt(acc[:, m, :], e[:, m, j:j + 336], tile[:, 16 + j:17 + j], acc[:, m, :],
                                ALU.mult, ALU.add)
                        if m == 0 or j == 1:
                            link(t)
                t.then_inc(conv_made, 1)

            def gate_value(c):
                acc = acc2[c.slot]
                dve.wait_ge(conv_made, c.j + 1)
                dve.wait_ge(gate_made, c.j + 1)
                after(dve, actl_made, c.j)
                link(dve.tensor_mul(act_f[:, 0:TP], acc[:, 0, 0:TP], acc[:, 1, 0:TP]))
                s = [acc[:, m, 256:336].rearrange("p (b t) -> p b t", b=SEQS)[:, :, 2:10] for m in range(2)]
                dve.tensor_mul(act_f[:, TP:TOK].rearrange("p (b t) -> p b t", b=SEQS), s[0], s[1])\
                    .then_inc(actf_made, 1)

            def act_lo(c):
                dve.wait_ge(actf_made, c.j + 1)
                dve.wait_ge(acth_made, c.j + 1)
                dve.tensor_sub(act_l[:, bass.ds(c.j, 1), :].rearrange("p o t -> p (o t)"), act_f[:, :],
                               act_h[:, bass.ds(c.j, 1), :].rearrange("p o t -> p (o t)").bitcast(F32))\
                    .then_inc(actl_made, 1)

            def ffn_act(c):
                first = isinstance(c.j, int) and c.j == 0
                if first:
                    dve.wait_ge(scaled, 3)
                else:
                    gate_value(c.before())
                conv(c)
                if not first:
                    act_lo(c.before())

            def up_step(c):
                if c.k == 0:
                    chain.start = links + 2 * 3 + 1 - 16
                    chain.enter(c.turn, 16)
                b = c.before().before()
                past_rows(b)
                make_lo(c, KD * CH)
                ffn_act(b)
            links = chain.start
            ring(dve, AT_UP, N_UP, up_step, done=2)
            last = Chunk(AT_UP, N_UP // 4, N_UP % 4 - 1)
            for k, c in enumerate((last.before(), last)):
                past_rows(c)
                make_lo(Chunk(AT_DOWN, 0, k), 2 * D)
                ffn_act(c)
            gate_value(last)
            act_lo(last)
            chain.start, chain.turn, chain.per, chain.k = chain.start + 16 * (N_UP // 4) + chain.k, 0, 0, 0
            dve.wait_ge(last_kept, N_UP)
            dve.transpose(ff_last_t[:, :, :], ff_last[:, :, :]).then_inc(fflast_made, 1)
            ring(dve, AT_DOWN, N_DOWN, lambda c: make_lo(c, 2 * D), done=2)
            move_out(1)
            residual(1, 0, GT_F)
            residual(1, 1, GT_F)
            inverse_std(1, 0)
            residual(1, 2, GT_F)
            for tt in (1, 2):
                inverse_std(1, tt)
                r = slice(0, NT[tt])
                dve.wait_ge(ln_in, 64)
                link(stt(ln_rows[r, tt, :], ln_rows[r, tt, :], ln_s[r, tt, 1:2], ln_gb2[r, 0, :], ALU.add, ALU.mult))
                stt(xt[r, tt, :], ln_rows[r, tt, :], ln_s[r, tt, 4:5], ln_gb2[r, 1, :], ALU.mult, ALU.add)\
                    .then_inc(final_made, 1)

        @block.gpsimd
        def _(pool):
            for b in b_ada:
                t = pool.memset(b[:, :], 0.0)
            t.then_inc(bias_zeroed, 1)
            pool.memset(state_raw[:, :, :], 0.0).then_inc(state_zeroed, 1)
            pool.memset(conv_last[:, :, :], 0.0).then_inc(pool_step, 1)
            pool.memset(eps[:, :], EPS).then_inc(eps_set, 1)
            for b in range(BLK - 1):
                at = slice(b * CH, b * CH + CH)
                pool.wait_ge(x_in, 32)
                pool.wait_ge(mods_made, 2 * b + 2)
                for tt in range(3):
                    n = NT[tt]
                    t = pool.tensor_mul(rows[0:n, tt, at], xt[0:n, tt, at], mods[0:n, SC_A, PR[tt], at])
                t.then_inc(x_scaled, 1)
                pool.wait_ge(x_scaled, b + 1)
                for tt in range(3):
                    n = NT[tt]
                    t = pool.tensor_add(rows[0:n, tt, at], rows[0:n, tt, at], mods[0:n, SH_A, PR[tt], at])
                t.then_inc(rows_made, 1)
            pool.wait_ge(tables_in, 16)
            pool.wait_ge(rows_made, BLK)
            pool.memset(lf_sum[:, :, :, :], 0.0).then_inc(lfsum_zeroed, 1)
            pool.wait_ge(lft_ready, 1)
            pool.memset(bias_r[:, PAST:PAST + TSA], 0.0).then_inc(newbias_zeroed, 1)
            pool.wait_ge(cum_made, 1)
            pool.wait_ge(logft_ready, 1)
            for q in qblk:
                pool.memset(q[:, :, :, :], 0.0).then_inc(pool_step, 1)
            pool.wait_ge(pool_step, 3)

            def build_q(bp, kind, u):
                after(pool, s_ready, u - 1)
                at = (FQ, MQ)[kind]
                for half in range(2):
                    r = slice(HD * half, HD * half + HD)
                    for p in range(PAIRS):
                        t = pool.tensor_copy(qblk[kind][r, :, p, TS * half:TS * half + TS],
                                             proj[r, at + p, bass.ds(bp * (2 * TS) + TP, 2 * TS)]
                                             .rearrange("p (b t) -> p b t", b=2))
                t.then_inc(q_built, 1)

            def build_bias(bp):
                after(pool, s_ready, bp * 2 - 1)
                pool.tensor_tensor(bias_r[:, 0:PAST].rearrange("p (g s) -> p g s", g=PAGES),
                                   c_suffix[:, bass.ds(bp, 1), :].to_broadcast([P, PAGES, P]),
                                   const[:, C_PAGEM:C_PAGEM + PAGES].unsqueeze(2).to_broadcast([P, PAGES, P]),
                                   ALU.mult).then_inc(bias_built, 1)

            pool.wait_ge(tile_moved, N_PROJ)
            pool.wait_ge(suffix_made, 1)
            pool.wait_ge(newbias_made, 2)

            def units(bp):
                after(pool, q_built, bp * 2)
                build_bias(bp)
                pool.wait_ge(bias_built, bp + 1)
                build_q(bp, 0, bp * 2)
                build_q(bp, 1, bp * 2 + 1)
            units(0)
            pool.wait_ge(g_b_in, 32)
            pool.wait_ge(mods_made, N_ADA1 + N_ADA2)
            pool.wait_ge(q_built, 2)
            both = lambda row: row[:, :].unsqueeze(1).to_broadcast([P, 2, D])
            pool.tensor_mul(ln_scaled[:, :, :], mods[:, SC_F, :, :], both(ln_b)).then_inc(gb_step, 1)
            pool.wait_ge(gb_step, 1)
            pool.tensor_add(mods[:, SH_F, :, :], mods[:, SH_F, :, :], ln_scaled[:, :, :])
            pool.tensor_mul(mods[:, SC_F, :, :], mods[:, SC_F, :, :], both(ln_g)).then_inc(gb_made, 1)
            pool.wait_ge(gb_made, 1)
            with pool.Fori(1, BP) as bp:
                units(bp)

            def scale_row(n, gb, tt):
                r = slice(0, NT[tt])
                pool.wait_ge(normed, 3 * n + tt + 1)
                pool.tensor_mul(xt[r, tt, :], xt[r, tt, :], gb[r, 0, :]).then_inc(gain_made, 1)
                pool.wait_ge(gain_made, 3 * n + tt + 1)
                pool.tensor_add(xt[r, tt, :], xt[r, tt, :], gb[r, 1, :]).then_inc(scaled, 1)

            c = Chunk(AT_UP, 0, 0)
            pool.wait_ge(lo_made, c.n)
            pool.wait_ge(hi_made, c.n + 1)
            pool.wait_ge(w_used, c.n - 1)
            pool.tensor_sub(w_l[c.slot][:, :], raw[c.raw][:, :], w_h[c.slot][:, :].bitcast(F32)).then_inc(lo_made, 1)
            pool.wait_ge(normed, 1)
            pool.tensor_mul(ln_rows[:, 0, :], xt[:, 0, :], mods[:, SC_F, 0, :]).then_inc(pool_step, 1)
            pool.wait_ge(pool_step, 4)
            pool.tensor_add(ln_rows[:, 0, :], ln_rows[:, 0, :], mods[:, SH_F, 0, :]).then_inc(row0_made, 1)
            pool.wait_ge(row0_made, 1)
            pool.wait_ge(ln_in, 32)
            for tt in range(3):
                if tt:
                    pool.wait_ge(rows_made, BLK + tt)
                scale_row(0, ln_gb1, tt)
            pool.memset(ff_last[:, :, :], 0.0).then_inc(fflast_zeroed, 1)
            pool.wait_ge(fflast_zeroed, 1)

            def keep_last(c):
                pool.wait_ge(tap_made, c.j + 1)
                e = ext[c.slot]
                for m in range(2):
                    dst = ff_last[:, bass.ds(c.j + m * FT, 1), :].rearrange("p o r -> p (o r)")
                    pool.tensor_copy(dst[:, 0:16].rearrange("p (b r) -> p b r", r=2),
                                     e[:, m, 258:338].rearrange("p (b t) -> p b t", b=SEQS)[:, :, 8:10])
                    t = pool.tensor_copy(dst[:, 16:18], e[:, m, 256:258])
                t.then_inc(last_kept, 1)
            ring(pool, AT_UP, N_UP, keep_last)
            pool.wait_ge(ln_in, 64)
            scale_row(1, ln_gb2, 0)


NAMES = ["x_prompt", "x_sample", "cache_fox_k", "cache_fox_v", "cache_fox_logf", "cache_moba_k", "cache_moba_v",
         "state_conv", "state_ffn", "page_table", "c_prompt", "c_sample", "w_ada", "b_ada", "w_in", "b_f", "conv_w",
         "w_o", "ln1_g", "ln1_b", "w_up", "ffn_conv_w", "ffn_conv_b", "w_down", "ln2_g", "ln2_b"]


def outputs():
    out = [("y_p", (1, TP, D)), ("y_s", (SEQS, TS, D))]
    for s, g, t in (("p", 1, TP), ("s", SEQS, TS)):
        out += [(f"fk_{s}", (1, g, t, HEADS, HD)), (f"fv_{s}", (1, g, t, HEADS, HD)), (f"lf_{s}", (1, g, t, HEADS)),
                (f"mk_{s}", (1, g, t, HEADS, HD)), (f"mv_{s}", (1, g, t, HEADS, HD)), (f"conv_{s}", (1, g, 2, CW)),
                (f"ffn_{s}", (1, g, 2, 2 * DFF))]
    return out


def kernel(**inputs):
    import concourse.bacc as bacc
    from concourse.bass_utils import run_bass_kernel_spmd

    nc = bacc.Bacc("TRN2", target_bir_lowering=False, num_devices=1, dynamic_dma_scratch_size=1024)
    arrays = {n: np.ascontiguousarray(inputs[n]) for n in NAMES}
    arrays["const"] = constants()
    a = {n: nc.dram_tensor(f"in_{n}", x.shape, mybir.dt.from_np(x.dtype), kind="ExternalInput").ap()
         for n, x in arrays.items()}
    o = {n: nc.dram_tensor(f"out_{n}", s, F32, kind="ExternalOutput").ap() for n, s in outputs()}
    build(nc, a, o)
    r = run_bass_kernel_spmd(nc, [{f"in_{n}": x for n, x in arrays.items()}], core_ids=[0])
    return tuple(r.results[0][f"out_{n}"] for n, _ in outputs())
```
